# Optimizing a Trainium2 kernel written in Bass

```python
import jax, jax.numpy as jnp
from jax import lax
import numpy as np

D_MODEL = 1024
BATCH = 1
SEQ = 2048
DEPTH = 1
DEC_BATCH = 8
DEC_SEQ = 4
PAST_LEN = 16384
PAGE_SIZE = 128

MIX_W = D_MODEL
MLSTM_W = MIX_W // 2
NH_M = 4
DV = MLSTM_W // NH_M
DK = DV // 2
CONV_CH = MIX_W - MLSTM_W
CONV_W = 3
D_FF = ((8 * D_MODEL + 3 * 256 - 1) // (3 * 256)) * 256
PLE_DIM = 256
CHUNK = 64
GATE_CAP = 15.0
EPS = 1e-6
PROJ_W = 2 * NH_M * DK + MLSTM_W + 2 * NH_M + MLSTM_W + 3 * CONV_CH

kernel_name = "hymba_mlstm_shortconv_decode_step"

def rmsnorm(x, g):
    xf = x.astype(jnp.float32)
    y = xf * lax.rsqrt(jnp.mean(xf * xf, axis=-1, keepdims=True) + EPS)
    return (y * g.astype(jnp.float32)).astype(x.dtype)

def mlstm_chunkwise(q, k, v, ig, lf, C0, n0, m0, chunk):
    Bn, H, S, _ = q.shape
    nc = S // chunk

    def to_chunks(a):
        a = a.reshape(a.shape[:2] + (nc, chunk) + a.shape[3:])
        return jnp.moveaxis(a, 2, 0)

    xs = tuple(to_chunks(a) for a in (q, k, v, ig, lf))
    causal = jnp.tril(jnp.ones((chunk, chunk), dtype=bool))

    def step(carry, inp):
        C, n, m = carry
        qc, kc, vc, ic, fc = inp
        b = jnp.cumsum(fc, axis=-1)
        g = b + m[..., None]
        Dm = b[..., :, None] - b[..., None, :] + ic[..., None, :]
        Dm = jnp.where(causal, Dm, -jnp.inf)
        mt = jnp.maximum(g, jnp.max(Dm, axis=-1))
        w_inter = jnp.exp(g - mt)
        s = jnp.einsum('bhtd,bhsd->bhts', qc, kc) * jnp.exp(Dm - mt[..., None])
        num = (w_inter[..., None] * jnp.einsum('bhtd,bhde->bhte', qc, C)
               + jnp.einsum('bhts,bhse->bhte', s, vc))
        den = w_inter * jnp.einsum('bhtd,bhd->bht', qc, n) + jnp.sum(s, axis=-1)
        h = num / jnp.maximum(jnp.abs(den), jnp.exp(-mt))[..., None]
        bL = b[..., -1]
        dL = bL[..., None] - b + ic
        m_new = jnp.maximum(bL + m, jnp.max(dL, axis=-1))
        a_st = jnp.exp(bL + m - m_new)
        wk = jnp.exp(dL - m_new[..., None])
        C_new = a_st[..., None, None] * C + jnp.einsum('bhs,bhsd,bhse->bhde', wk, kc, vc)
        n_new = a_st[..., None] * n + jnp.einsum('bhs,bhsd->bhd', wk, kc)
        return (C_new, n_new, m_new), h

    carry0 = (C0.astype(jnp.float32), n0.astype(jnp.float32), m0.astype(jnp.float32))
    (C, n, m), hs = lax.scan(step, carry0, xs)
    h = jnp.moveaxis(hs, 0, 2).reshape(Bn, H, S, v.shape[-1])
    return h, C, n, m

def hybrid_layer(x, pe, C0, n0, m0, conv0, chunk, g_mix, w_in, b_ig, b_fg, g_mh, conv_w, w_out,
                 g_ffn, w_gate, w_up, w_down, w_ple, g_ple, w_pg):
    Bn, S, _ = x.shape
    a = rmsnorm(x, g_mix)
    u = a @ w_in
    sizes = [NH_M * DK, NH_M * DK, MLSTM_W, NH_M, NH_M, MLSTM_W, CONV_CH, CONV_CH, CONV_CH]
    idx = [int(c) for c in np.cumsum(sizes)[:-1]]
    q, k, v, ig, fg, og, bg, cg, hc = jnp.split(u, idx, axis=-1)

    def heads(t, d):
        return t.reshape(Bn, S, NH_M, d).transpose(0, 2, 1, 3).astype(jnp.float32)

    qh = heads(q, DK) * (DK ** -0.5)
    kh = heads(k, DK)
    vh = heads(v, DV)
    igh = (GATE_CAP * jnp.tanh((ig + b_ig).astype(jnp.float32) / GATE_CAP)).transpose(0, 2, 1)
    lfh = jax.nn.log_sigmoid((fg + b_fg).astype(jnp.float32)).transpose(0, 2, 1)
    h, C, n, m = mlstm_chunkwise(qh, kh, vh, igh, lfh, C0, n0, m0, chunk)
    h = h.transpose(0, 2, 1, 3)
    h = h * lax.rsqrt(jnp.mean(h * h, axis=-1, keepdims=True) + EPS)
    h = h.reshape(Bn, S, MLSTM_W) * g_mh.astype(jnp.float32)
    h_m = (jax.nn.sigmoid(og.astype(jnp.float32)) * h).astype(x.dtype)

    z = cg * hc
    zp = jnp.concatenate([conv0.astype(z.dtype), z], axis=1)
    yconv = conv_w[0] * zp[:, 0:S]
    for j in range(1, CONV_W):
        yconv = yconv + conv_w[j] * zp[:, j:j + S]
    y_c = (bg * yconv).astype(x.dtype)
    new_conv = zp[:, S:]

    x = x + jnp.concatenate([h_m, y_c], axis=-1) @ w_out
    f = rmsnorm(x, g_ffn)
    x = x + (jax.nn.silu(f @ w_gate) * (f @ w_up)) @ w_down
    e = rmsnorm(pe @ w_ple, g_ple)
    x = x + jax.nn.sigmoid(x @ w_pg) * e
    return x, C, n, m, new_conv

def setup_inputs(seed: int = 0) -> dict:
    key = jax.random.key(seed)
    ks = jax.random.split(key, 24)
    nrm = jax.random.normal
    f32 = jnp.float32
    d = {}
    d["x_prompt"] = nrm(ks[0], (BATCH, SEQ, D_MODEL), f32)
    d["x_sample"] = nrm(ks[1], (DEC_BATCH, DEC_SEQ, D_MODEL), f32)
    d["p_prompt"] = nrm(ks[2], (DEPTH, BATCH, SEQ, PLE_DIM), f32)
    d["p_sample"] = nrm(ks[3], (DEPTH, DEC_BATCH, DEC_SEQ, PLE_DIM), f32)
    d["state_C"] = 0.5 * nrm(ks[4], (DEPTH, DEC_BATCH, NH_M, DK, DV), f32)
    d["state_n"] = 0.5 * nrm(ks[5], (DEPTH, DEC_BATCH, NH_M, DK), f32)
    d["state_m"] = 1.0 + 0.5 * nrm(ks[6], (DEPTH, DEC_BATCH, NH_M), f32)
    d["state_conv"] = nrm(ks[7], (DEPTH, DEC_BATCH, CONV_W - 1, CONV_CH), f32)
    d["g_mix"] = 1.0 + 0.02 * nrm(ks[8], (DEPTH, D_MODEL), f32)
    d["w_in"] = nrm(ks[9], (DEPTH, D_MODEL, PROJ_W), f32) * D_MODEL ** -0.5
    d["b_ig"] = 0.1 * nrm(ks[10], (DEPTH, NH_M), f32)
    d["b_fg"] = 3.0 + 0.1 * nrm(ks[11], (DEPTH, NH_M), f32)
    d["g_mh"] = 1.0 + 0.02 * nrm(ks[12], (DEPTH, MLSTM_W), f32)
    d["conv_w"] = nrm(ks[13], (DEPTH, CONV_W, CONV_CH), f32) * CONV_W ** -0.5
    d["w_out"] = nrm(ks[14], (DEPTH, MIX_W, D_MODEL), f32) * MIX_W ** -0.5
    d["g_ffn"] = 1.0 + 0.02 * nrm(ks[15], (DEPTH, D_MODEL), f32)
    d["w_gate"] = nrm(ks[16], (DEPTH, D_MODEL, D_FF), f32) * D_MODEL ** -0.5
    d["w_up"] = nrm(ks[17], (DEPTH, D_MODEL, D_FF), f32) * D_MODEL ** -0.5
    d["w_down"] = nrm(ks[18], (DEPTH, D_FF, D_MODEL), f32) * D_FF ** -0.5
    d["w_ple"] = nrm(ks[19], (DEPTH, PLE_DIM, D_MODEL), f32) * PLE_DIM ** -0.5
    d["g_ple"] = 1.0 + 0.02 * nrm(ks[20], (DEPTH, D_MODEL), f32)
    d["w_pg"] = nrm(ks[21], (DEPTH, D_MODEL, D_MODEL), f32) * D_MODEL ** -0.5
    d["g_final"] = 1.0 + 0.02 * nrm(ks[22], (D_MODEL,), f32)
    return d

def reference(x_prompt, x_sample, p_prompt, p_sample, state_C, state_n, state_m, state_conv,
              g_mix, w_in, b_ig, b_fg, g_mh, conv_w, w_out, g_ffn, w_gate, w_up, w_down,
              w_ple, g_ple, w_pg, g_final):
    xp, xs = x_prompt, x_sample
    Bp = xp.shape[0]
    Sp = xp.shape[1]
    chunk_p = min(CHUNK, Sp)
    chunk_s = xs.shape[1]
    Cp_l, np_l, mp_l, cvp_l = [], [], [], []
    Cs_l, ns_l, ms_l, cvs_l = [], [], [], []
    for i in range(DEPTH):
        w = (g_mix[i], w_in[i], b_ig[i], b_fg[i], g_mh[i], conv_w[i], w_out[i], g_ffn[i],
             w_gate[i], w_up[i], w_down[i], w_ple[i], g_ple[i], w_pg[i])
        C0 = jnp.zeros((Bp, NH_M, DK, DV), jnp.float32)
        n0 = jnp.zeros((Bp, NH_M, DK), jnp.float32)
        m0 = jnp.zeros((Bp, NH_M), jnp.float32)
        cv0 = jnp.zeros((Bp, CONV_W - 1, CONV_CH), xp.dtype)
        xp, Cp, n_p, mp, cvp = hybrid_layer(xp, p_prompt[i], C0, n0, m0, cv0, chunk_p, *w)
        xs, Cs, n_s, ms, cvs = hybrid_layer(xs, p_sample[i], state_C[i], state_n[i], state_m[i],
                                            state_conv[i], chunk_s, *w)
        Cp_l.append(Cp); np_l.append(n_p); mp_l.append(mp); cvp_l.append(cvp)
        Cs_l.append(Cs); ns_l.append(n_s); ms_l.append(ms); cvs_l.append(cvs)
    y_prompt = rmsnorm(xp, g_final)
    y_sample = rmsnorm(xs, g_final)
    C_prompt = jnp.stack(Cp_l); n_prompt = jnp.stack(np_l); m_prompt = jnp.stack(mp_l); conv_prompt = jnp.stack(cvp_l)
    C_sample = jnp.stack(Cs_l); n_sample = jnp.stack(ns_l); m_sample = jnp.stack(ms_l); conv_sample = jnp.stack(cvs_l)
    return (y_prompt, y_sample, C_prompt, n_prompt, m_prompt, conv_prompt, C_sample, n_sample, m_sample, conv_sample)


_drawn_inputs = setup_inputs


def setup_inputs(seed=0):
    import zlib

    import numpy as np

    out = dict(_drawn_inputs(seed))
    spreads = {}
    factors = {'g_mh': 8.0, 'g_ffn': 5.001, 'g_ple': 7.965, 'g_final': 2.823}
    for name, (base, spread) in spreads.items():
        noise = np.random.default_rng([zlib.crc32(name.encode()), seed]).standard_normal(out[name].shape)
        drawn = base * np.exp(spread * noise) if base else spread * noise
        out[name] = __import__('jax').numpy.asarray(drawn.astype(out[name].dtype))
    for name, factor in factors.items():
        out[name] = (out[name] * factor).astype(out[name].dtype)
    return out
```

```python
from contextlib import ExitStack

import concourse.bass as bass
from concourse import mybir

ALU = mybir.AluOpType
ACT = mybir.ActivationFunctionType
F32 = mybir.dt.float32
F32R = mybir.dt.float32r
BF16 = mybir.dt.bfloat16
ds = bass.ds

P = 128
D = 1024
KC = D // P
NH, DK, DV = 4, 64, 128
PAIRS = NH // 2
DFF = 2816
FF = DFF // P
PLE = 256
GATE_CAP = 15.0
EPS = 1e-6
NB_S, NT_S = 8, 4
TS = NB_S * NT_S
TP = 1024
TM = TP + TS
NCH = TP // P
QSCALE = DK ** -0.5
NEG = -1e30
GROUP = 4
SLAB = 1024
SLABS = 8 + 1 + 16 + 8 + 2 + (5 * 12 + 6) + 8
COL_G, COL_O = 2 * NH * DK + NH * DV, 2 * NH * DK + NH * DV + 2 * NH
COL_B = COL_O + NH * DV
COL_C = COL_B + 512
COL_H = COL_C + 512
N_CONSTS = 2 + 5 + 3 + 1 + 8


class Super:

    def __init__(self, n):
        self.n = n
        self.sample = n == 1
        self.T = TM if self.sample else TP
        self.nb = 3 if self.sample else 2
        size = self.T // self.nb
        self.blocks = [(b * size, size) for b in range(self.nb)]
        self.tiles = NCH + self.sample
        self.slab0 = n * SLABS


class Banks:

    def __init__(self):
        self.n = [0] * 8

    def take(self, b):
        self.n[b] += 1
        return self.n[b]

    def skip(self, uses, times=1):
        for b, m in uses.items():
            self.n[b] += m * times


class Fills:

    def __init__(self, banks, i, uses):
        self.base, self.i, self.uses, self.k = list(banks.n), i, uses, {b: 0 for b in uses}

    def take(self, b):
        self.k[b] += 1
        return self.base[b] + self.k[b] + self.i * self.uses[b]


class Chain:

    def __init__(self, eng, sem):
        self.eng, self.sem, self.n, self.i, self.per, self.start = eng, sem, 0, 0, 0, 0

    def loop(self, i, per):
        self.i, self.per, self.start = i, per, self.n

    def done(self, times):
        assert self.n - self.start == self.per, (self.n - self.start, self.per)
        self.n, self.i, self.per = self.start + self.per * times, 0, 0

    def link(self, ins):
        self.n += 1
        ins.then_inc(self.sem, 1)
        self.eng.wait_ge(self.sem, self.n + self.i * self.per)


def build(nc, x_prompt, x_sample, p_prompt, p_sample, state_C, state_n, state_m, state_conv, g_mix, w_in,
          b_ig, b_fg, g_mh, conv_w, w_out, g_ffn, w_gate, w_up, w_down, w_ple, g_ple, w_pg, g_final,
          y_prompt, y_sample, C_prompt, n_prompt, m_prompt, conv_prompt, C_sample, n_sample, m_sample,
          conv_sample):
    supers = [Super(0), Super(1)]
    spilled_x = nc.dram_tensor("spilled_x", (P, KC, TM), F32, kind="Internal").ap()

    SLOT = TM * 4
    origin = (nc.sbuf_base + 31) // 32 * 32

    def at(name, shape, dt, offset):
        return nc.alloc_sbuf_tensor_at(name, shape, dt, offset=offset)

    X = at("X", [P, KC, TM], F32, origin)
    AH = at("AH", [P, KC, TM], F32R, origin + 8 * SLOT)
    AL = at("AL", [P, KC, TM], F32R, origin + 16 * SLOT)
    U = at("U", [P, KC, TM], F32, origin + 24 * SLOT)
    R0 = origin + 32 * SLOT
    hid = at("hid", [P, 2, GROUP, TM], F32R, R0)
    rows = at("rows", [P, 8, TM], F32, R0)
    xin = [at(f"xin{p}", [P, D], F32, R0 + p * 4096) for p in range(2)]
    sqt = [at(f"sqt{p}", [P, TM], F32, R0 + (2 + p) * SLOT) for p in range(2)]
    yst = [at(f"yst{p}", [P, D], F32, R0 + p * 4096) for p in range(2)]
    G, LF, B, M, R1, W, CS, EM = (rows[:, n, :] for n in range(8))
    qw = rows[:, 0:2, :]
    zbuf = at("zbuf", [P, TM + 2], F32, R0 + 2 * SLOT)
    Cs = at("Cs", [P, PAIRS, NB_S, DV + 1], F32, R0 + 2 * SLOT)
    kwb = at("kwb", [TS, NH, NB_S, DK], F32, R0)
    stage0 = R0 + 5 * SLOT
    kst = at("kst", [P, PAIRS, P], F32, stage0)
    qz = at("qz", [P, NH, P], F32, stage0 + 1024)
    qwz = at("qwz", [P, NH, P], F32, stage0 + 3072)
    vst = at("vst", [P, NH, P], F32, stage0 + 5120)
    rz = at("rz", [P, P], F32, stage0 + 7168)
    cv = at("cv", [P, TM], F32, R0 + 7 * SLOT)
    qb = at("qb", [P, NH, NB_S, TS], F32, R0 + 7 * SLOT)
    pst = at("pst", [P, NCH, PLE], F32, R0 + 6 * SLOT)
    pst_s = at("pst_s", [P, PLE], F32, R0 + 2 * SLOT)

    slab_at = R0 + 8 * SLOT
    wraw = [at(f"wraw{p}", [P, SLAB], F32, slab_at + p * 4096) for p in range(2)]
    whi = [at(f"whi{p}", [P, SLAB], F32R, slab_at + (2 + p) * 4096) for p in range(2)]
    wlo = [at(f"wlo{p}", [P, SLAB], F32R, slab_at + (4 + p) * 4096) for p in range(2)]

    cursor = [slab_at + 6 * 4096]

    def keep(name, shape, dt=F32):
        size = 1
        for n in shape[1:]:
            size *= n
        size *= 2 if dt == BF16 else 4
        t = at(name, shape, dt, cursor[0])
        cursor[0] += (size + 31) // 32 * 32
        return t

    ident = keep("ident", [P, P])
    identb = keep("identb", [P, P], BF16)
    causal = keep("causal", [P, P], BF16)
    causal_s = keep("causal_s", [P, NB_S, NT_S], BF16)
    batch_s = keep("batch_s", [P, NB_S])
    state = keep("state", [P, PAIRS, DV + 1])
    ones = keep("ones", [P, 1])
    epst = keep("epst", [P, 1])
    neg_half = keep("neg_half", [P, NH])
    gmix, gffn, gple, gfin = (keep(n, [P, KC]) for n in ("gmix", "gffn", "gple", "gfin"))
    gmh = keep("gmh", [P, NH])
    cw = keep("cw", [P, 3, 4])
    bias8 = keep("bias8", [2 * NH, 1])
    hist = keep("hist", [P, 4, 2])
    convs = keep("convs", [P, 4, NB_S, 2])
    zs = keep("zs", [P, NB_S, 2 + NT_S])
    carry = keep("carry", [NH, 1])
    mprev = keep("mprev", [NH, NCH + NB_S])
    m_out = keep("m_out", [NH, NB_S])
    ms0 = keep("ms0", [NH, NB_S])
    sI = keep("sI", [NH, NB_S, NT_S])
    sF = keep("sF", [NH, NB_S, NT_S])
    decay = keep("decay", [P, PAIRS, NCH + NB_S])
    cols = keep("cols", [P, 3, NCH + 1, NH])
    colst = [keep(f"colst{p}", [P, 14]) for p in range(2)]
    sm = keep("sm", [P, 6, NH])
    ss4, dm, d2, tt, rr, _ = (sm[:, n, :] for n in range(6))
    mix0 = cursor[0]
    expE = keep("expE", [P, NH, P])
    Pm = keep("Pm", [P, NH, P])
    V = keep("V", [P, NH, DV + 1])
    kw = keep("kw", [P, NH, DK])
    hn = keep("hn", [P, NH, P])
    batch_t = keep("batch_t", [P, NB_S, TS])
    pair_rows = keep("pair_rows", [NH, PAIRS, P])
    cursor[0] = mix0
    ss = keep("ss", [P, TM])
    sl = keep("sl", [P, TM])
    tmp = [keep(f"tmp{p}", [P, 512]) for p in range(3)]
    assert cursor[0] <= nc.sbuf_usable_end, (cursor[0], nc.sbuf_usable_end)

    def by_k(w):
        return w.rearrange("(k p) n -> p k n", p=P)

    w_in_v, w_out_v, w_gate_v, w_up_v, w_down_v, w_ple_v, w_pg_v = (
        by_k(w[0]) for w in (w_in, w_out, w_gate, w_up, w_down, w_ple, w_pg))

    with ExitStack() as ctx:
        bank = [ctx.enter_context(nc.psum_tensor(f"bank{b}", [P, 512], F32)) for b in range(8)]

        def sem(name):
            return ctx.enter_context(nc.semaphore(name))

        consts_in = sem("consts_in")
        consts_made = sem("consts_made")
        landed = [sem("landed_even"), sem("landed_odd")]
        hi_done, lo_done = sem("hi_done"), sem("lo_done")
        slab_begun = sem("slab_begun")
        full = [sem(f"full{b}") for b in range(8)]
        free = [sem(f"free{b}") for b in range(8)]
        dve_own, pool_own = sem("dve_own"), sem("pool_own")
        names = ["x_landed0", "x_landed1", "x_sq", "x_sum", "x_spilled", "normed", "high", "low",
                 "softcap", "lf_abs", "lf_soft", "rows_made", "rows_exp", "stage_clear", "staged", "conv_done",
                 "sq_done", "root_in", "root_done", "sig_o", "merged", "mix_hi", "mix_lo", "reload", "p_landed",
                 "p_hi", "res_sq", "res_sum", "normed2", "high2", "low2", "e_sq", "e_sum", "e_done",
                 "h_hi", "h_lo", "x3_hi", "x3_lo", "x4", "x4_sq", "x4_sum", "y_t", "y_out0", "y_out1"]
        S = [{n: sem(f"{n}_{q}") for n in names} for q in range(2)]
        states_in, batch_queries, batch_keys = sem("states_in"), sem("batch_queries"), sem("batch_keys")
        small_out = sem("small_out")
        ctx.enter_context(nc.allow_non_contiguous_dma(reason="gains, biases and small states"))
        block = ctx.enter_context(nc.Block())

        def was_filled(eng, banks, *bks):
            for b in bks:
                eng.wait_ge(full[b], banks.n[b])

        def was_read(eng, banks, *bks):
            for b in bks:
                eng.wait_ge(free[b], banks.n[b] + 1)

        class ChunkFills:

            def __init__(self, banks, c):
                n = banks
                self.exponent, self.score = n[2] + c + 1, n[3] + c + 1
                self.keys, self.out01 = n[4] + 2 * c + 1, n[4] + 2 * c + 2
                self.out23, self.state = n[5] + c + 1, n[6] + c + 1
                self.values, self.h_t = n[7] + 2 * c + 1, n[7] + 2 * c + 2

        CHUNK_USES = {2: 1, 3: 1, 4: 2, 5: 1, 6: 1, 7: 2}

        def prep_fills(banks, q):
            lf = [banks.take(2 + b) for b in range(q.nb)]
            columns = banks.take(5)
            pairs = [(6 + k % 2, banks.take(6 + k % 2)) for k in range(PAIRS * q.nb)]
            return lf, columns, pairs, banks.take(4)

        N_SMALL = 4 + 4 + 8 + 2 * PAIRS

        def small_outputs(sp):
            def out(dst, src):
                sp.dma_start(dst, src).then_inc(small_out, 16)

            out(C_prompt[0, 0].rearrange("(j hh) d e -> (hh d) j e", hh=2), state[:, :, 0:DV])
            out(n_prompt[0, 0].rearrange("(j hh) d -> (hh d) j", hh=2), state[:, :, DV])
            out(m_prompt[0, 0].rearrange("(h a) -> h a", a=1), carry[:, :])
            out(m_sample[0].rearrange("b h -> h b"), m_out[:, :])
            for c in range(4):
                out(conv_prompt[0, 0, :, c * P:(c + 1) * P].rearrange("w p -> p w"), hist[:, c, :])
                for w in range(2):
                    out(conv_sample[0, :, w, c * P:(c + 1) * P].rearrange("b p -> p b"), convs[:, c, :, w])
            for j in range(PAIRS):
                out(C_sample[0, :, 2 * j:2 * j + 2].rearrange("b hh d e -> (hh d) b e"), Cs[:, j, :, 0:DV])
                out(n_sample[0, :, 2 * j:2 * j + 2].rearrange("b hh d -> (hh d) b"), Cs[:, j, :, DV])

        @block.sync
        def _(sp):
            banks = Banks()
            def constants():
                sp.dma_start(bias8[0:NH, :], b_ig.rearrange("a h -> h a")).then_inc(consts_in, 16)
                sp.dma_start(bias8[NH:2 * NH, :], b_fg.rearrange("a h -> h a")).then_inc(consts_in, 16)
                for t, g in ((gmix, g_mix[0]), (gffn, g_ffn[0]), (gple, g_ple[0]), (gfin, g_final), (gmh, g_mh[0])):
                    sp.dma_start(t[:, :], g.rearrange("(c p) -> p c", p=P)).then_inc(consts_in, 16)
                for w in range(3):
                    sp.dma_start(cw[:, w, :], conv_w[0, w].rearrange("(c p) -> p c", p=P)).then_inc(consts_in, 16)
                sp.dma_start(ms0[:, :], state_m[0].rearrange("b h -> h b")).then_inc(consts_in, 16)
                for c in range(4):
                    for w in range(2):
                        sp.dma_start(convs[:, c, :, w], state_conv[0, :, w, c * P:(c + 1) * P].rearrange("b p -> p b"))\
                            .then_inc(consts_in, 16)

            def slab(s, p, src):
                sp.wait_ge(hi_done, s + 1)
                sp.wait_ge(lo_done, s + 1)
                sp.dma_start(wraw[p][:, :].rearrange("p (k n) -> p k n", k=src.shape[1]), src).then_inc(landed[p], 16)

            def first_slabs(q):
                for s in (q.slab0, q.slab0 + 1):
                    c0 = (s - q.slab0) * P
                    slab(s, s % 2, w_in_v[:, :, c0:c0 + P])

            for q in supers:
                v, s0 = S[q.n], q.slab0
                par = s0 % 2
                if q.n:
                    sp.wait_ge(S[0]["y_out0"], 16 * NCH // 2)
                    sp.wait_ge(S[0]["y_out1"], 16 * NCH // 2)
                tile0 = banks.n[3]
                for p in range(2):
                    sp.dma_start(xin[p][:, :], x_prompt[0, q.n * TP + p * P:q.n * TP + (p + 1) * P, :])\
                        .then_inc(v[f"x_landed{p}"], 16)
                if q.n == 0:
                    constants()
                    first_slabs(q)
                with sp.Fori(1, NCH // 2) as i:
                    for p in range(2):
                        sp.wait_ge(full[3], tile0 + 2 * i + p - 1)
                        sp.dma_start(xin[p][:, :], x_prompt[0, ds(i * 2 * P + (q.n * TP + p * P), P), :])\
                            .then_inc(v[f"x_landed{p}"], 16)
                if q.sample:
                    sp.wait_ge(full[3], tile0 + NCH - 1)
                    sp.dma_start(xin[0][0:TS, :], x_sample.rearrange("b s d -> (b s) d")).then_inc(v["x_landed0"], 16)
                banks.skip({2: 1, 3: 1}, q.tiles)
                was_read(sp, banks, 2, 3)
                sp.dma_start(spilled_x[:, :, 0:q.T], X[:, :, 0:q.T]).then_inc(v["x_spilled"], 16)
                banks.skip({6: q.nb})
                with sp.Fori(1, 4) as i:
                    for p in range(2):
                        slab(s0 + p + 2 * i, (par + p) % 2, w_in_v[:, :, ds(i * 2 * P + p * P, P)])
                slab(s0 + 8, par, w_in_v[:, :, COL_G:COL_G + P])
                banks.skip({0: 4 * q.nb, 1: 4 * q.nb})
                banks.skip({0: (q.nb + 1) // 2, 1: q.nb // 2})
                prep_fills(banks, q)
                chunk0 = list(banks.n)
                with sp.Fori(0, 4) as i:
                    for n, col in enumerate((COL_O, COL_C, COL_H, COL_B)):
                        slab(s0 + 9 + n + 4 * i, (par + 9 + n) % 2, w_in_v[:, :, ds(i * P + col, P)])
                banks.skip({0: 8 * q.nb, 1: 8 * q.nb})
                banks.skip(CHUNK_USES, NCH)
                s = s0 + 25
                for p in range(2):
                    slab(s + p, (s + p) % 2, w_out_v[:, :, p * P:(p + 1) * P])
                if q.sample:
                    sp.wait_ge(v["conv_done"], 5)
                    for j in range(PAIRS):
                        sp.dma_start(Cs[:, j, :, 0:DV],
                                     state_C[0, :, 2 * j:2 * j + 2].rearrange("b hh d e -> (hh d) b e")).then_inc(states_in, 16)
                        sp.dma_start(Cs[:, j, :, DV],
                                     state_n[0, :, 2 * j:2 * j + 2].rearrange("b hh d -> (hh d) b")).then_inc(states_in, 16)
                    banks.skip(CHUNK_USES)
                    banks.skip({2: 2, 3: 2, 6: 1})
                was_read(sp, banks, 0, 1, 2, 3, 6, 7)
                sp.wait_ge(v["staged"], q.tiles)
                sp.wait_ge(v["x_spilled"], 16)
                sp.dma_start(X[:, 0:4, 0:q.T], spilled_x[:, 0:4, 0:q.T]).then_inc(v["reload"], 16)
                if q.sample:
                    small_outputs(sp)
                    sp.wait_ge(small_out, 16 * N_SMALL)
                sp.dma_start(pst[:, :, :], p_prompt[0, 0, q.n * TP:(q.n + 1) * TP, :].rearrange("(t p) n -> p t n", p=P))\
                    .then_inc(v["p_landed"], 16)
                if q.sample:
                    sp.dma_start(pst_s[0:TS, :], p_sample[0].rearrange("b s n -> (b s) n")).then_inc(v["p_landed"], 16)
                sp.wait_ge(v["merged"], 4)
                sp.dma_start(X[:, 4:8, 0:q.T], spilled_x[:, 4:8, 0:q.T]).then_inc(v["reload"], 16)
                with sp.Fori(1, 4) as i:
                    for p in range(2):
                        slab(s + p + 2 * i, (s + p) % 2, w_out_v[:, :, ds(i * 2 * P + p * P, P)])
                s += 8
                for p in range(2):
                    slab(s + p, (s + p) % 2, w_ple_v[:, :, p * 512:(p + 1) * 512])
                s += 2
                with sp.Fori(0, 4) as g:
                    for c in range(GROUP):
                        for p, w in enumerate((w_gate_v, w_up_v)):
                            slab(s + 2 * c + p + 12 * g, (s + p) % 2, w[:, :, ds(g * GROUP * P + c * P, P)])
                    for n in range(4):
                        slab(s + 8 + n + 12 * g, (s + n) % 2, w_down_v[:, ds(g * GROUP, GROUP), n * 256:(n + 1) * 256])
                s += 48
                for g, size in ((4, 4), (5, 2)):
                    for c in range(size):
                        ff = g * GROUP + c
                        for w in (w_gate_v, w_up_v):
                            slab(s, s % 2, w[:, :, ff * P:(ff + 1) * P])
                            s += 1
                    nw = SLAB // size
                    for n in range(D // nw):
                        slab(s, s % 2, w_down_v[:, g * GROUP:g * GROUP + size, n * nw:(n + 1) * nw])
                        s += 1
                with sp.Fori(0, 4) as i:
                    for p in range(2):
                        slab(s + p + 2 * i, (s + p) % 2, w_pg_v[:, :, ds(i * 2 * P + p * P, P)])
                for g in range(4):
                    banks.take(2 + g)
                if q.sample:
                    banks.take(6)
                banks.skip({0: 4 * q.nb, 1: 4 * q.nb, 6: q.nb})
                banks.skip({0: 4 * q.nb, 1: 4 * q.nb})
                for b in range(q.nb):
                    banks.skip({b: FF, 3 + b: FF})
                banks.skip({6: 6 * 4 * q.nb + 2 * q.nb, 7: 6 * 4 * q.nb, 0: 4 * q.nb, 1: 4 * q.nb})
                if q.n == 0:
                    first_slabs(supers[1])
                for t in range(q.tiles):
                    sp.wait_ge(free[2], banks.take(2) + 1)
                    sp.wait_ge(free[3], banks.take(3) + 1)
                    if t < NCH:
                        dst, n = y_prompt[0, q.n * TP + t * P:q.n * TP + (t + 1) * P, :], P
                    else:
                        dst, n = y_sample.rearrange("b s d -> (b s) d"), TS
                    sp.dma_start(dst, yst[t % 2][0:n, :]).then_inc(v[f"y_out{t % 2}"], 16)
            sp.wait_ge(S[1]["y_out0"], 16 * (NCH // 2 + 1))
            sp.wait_ge(S[1]["y_out1"], 16 * NCH // 2)

        @block.tensor
        def _(pe):
            banks = Banks()

            pe.sem_inc(slab_begun, 1)
            pe.wait_ge(consts_made, 1)

            def product(q, no, bk, p, kc, n, b, src=(AH, AL), begins=False, ready=None):
                b0, bl = q.blocks[b]
                pe.wait_ge(free[bk], no)
                hi = whi[p][:, :].rearrange("p (k n) -> p k n", k=kc)
                lo = wlo[p][:, :].rearrange("p (k n) -> p k n", k=kc)
                o, cols_ = bank[bk][:, 0:bl], slice(n * P, (n + 1) * P)
                for k in range(kc):
                    mh, ml = src[0][:, k, b0:b0 + bl], src[1][:, k, b0:b0 + bl]
                    if ready:
                        ready(b, k)
                    first = nc.tensor.matmul(o, hi[:, k, cols_], mh, start=k == 0, stop=False)
                    if begins and k == 0:
                        first.then_inc(slab_begun, 1)
                    nc.tensor.matmul(o, hi[:, k, cols_], ml, start=False, stop=False)
                    last = nc.tensor.matmul(o, lo[:, k, cols_], mh, start=False, stop=k == kc - 1)
                last.then_inc(full[bk], 1)

            def slab_ready(s):
                pe.wait_ge(lo_done, s + 3)

            def sum_over_features(q, bk=6):
                for b0, bl in q.blocks:
                    pe.wait_ge(free[bk], banks.take(bk))
                    nc.tensor.matmul(bank[bk][:, 0:bl], ones[:, 0:1].to_broadcast([P, P]), ss[:, b0:b0 + bl],
                                     start=True, stop=True).then_inc(full[bk], 1)

            def chunk_scores(v, n0, c, n=P):
                f = ChunkFills(n0, c)
                mask = causal[:, :] if n == P else causal_s[:, :, :].rearrange("p b t -> p (b t)")
                pe.wait_ge(v["staged"], c + 1)
                pe.wait_ge(free[2], f.exponent)
                for h in range(NH):
                    e = bank[2][0:n, h * n:(h + 1) * n]
                    nc.tensor.matmul(e, identb[:, 0:n], mask, start=True, stop=False)
                    last = nc.tensor.matmul(e, ident[:, h:h + 1].to_broadcast([P, n]), rz[:, 0:n], start=False, stop=True)
                last.then_inc(full[2], 1)
                pe.wait_ge(free[3], f.score)
                for h in range(NH):
                    last = nc.tensor.matmul(bank[3][0:n, h * n:(h + 1) * n], kst[:, h // 2, 0:n], qz[:, h, 0:n],
                                            start=True, stop=True)
                last.then_inc(full[3], 1)
                pe.wait_ge(free[4], f.keys)
                for j in range(PAIRS):
                    last = nc.tensor.transpose(bank[4][0:n, j * P:(j + 1) * P], kst[:, j, 0:n], ident[:, :])
                last.then_inc(full[4], 1)
                pe.wait_ge(free[7], f.values)
                for h in range(NH):
                    last = nc.tensor.transpose(bank[7][0:n, h * P:(h + 1) * P], vst[:, h, 0:n], ident[:, :])
                last.then_inc(full[7], 1)

            def chunk_outputs(v, n0, c):
                f = ChunkFills(n0, c)
                pe.wait_ge(free[3], f.score + 1)
                pe.wait_ge(free[7], f.values + 1)
                pe.wait_ge(free[6], f.state)
                for bk, no, hs in ((4, f.out01, (0, 1)), (5, f.out23, (2, 3))):
                    pe.wait_ge(free[bk], no)
                    for h in hs:
                        o = bank[bk][:, (h % 2) * (DV + 1):(h % 2 + 1) * (DV + 1)]
                        nc.tensor.matmul(o, Pm[:, h, :], V[:, h, :], start=True, stop=False)
                        last = nc.tensor.matmul(o, qwz[:, h, :], state[:, h // 2, :], start=False, stop=True)
                    last.then_inc(full[bk], 1)
                for h in range(NH):
                    r, j = DK * (h % 2), h // 2
                    last = nc.tensor.matmul(bank[6][r:r + DK, j * (DV + 1):(j + 1) * (DV + 1)], kw[:, h, :], V[:, h, :],
                                            start=True, stop=True)
                last.then_inc(full[6], 1)

            def chunk_transposes(v, n0, c, n=P):
                f = ChunkFills(n0, c)
                pe.wait_ge(free[4], f.out01 + 1)
                pe.wait_ge(free[5], f.out23 + 1)
                pe.wait_ge(free[7], f.h_t)
                for h in range(NH):
                    last = nc.tensor.transpose(bank[7][:, h * n:(h + 1) * n], hn[0:n, h, :], ident[0:n, 0:n])
                last.then_inc(full[7], 1)

            def linear(q, s, uses, ready):
                with pe.Fori(0, 4) as i:
                    f = Fills(banks, i, uses)
                    k = 0
                    for p in range(2):
                        slab_ready(s + p + 2 * i)
                        for b in range(q.nb):
                            product(q, f.take(k % 2), k % 2, (s + p) % 2, KC, 0, b, begins=b == 0,
                                    ready=ready if p == 0 else None)
                            k += 1
                banks.skip(uses, 4)

            for q in supers:
                v, s0, nb = S[q.n], q.slab0, q.nb
                par = s0 % 2
                uses = {0: nb, 1: nb}

                def x_tile(f, p, n, landed_value):
                    pe.wait_ge(v[f"x_landed{p}"], landed_value)
                    for bk in (2, 3):
                        pe.wait_ge(free[bk], f.take(bk))
                        for c in range(4):
                            cc = (bk - 2) * 4 + c
                            last = nc.tensor.transpose(bank[bk][:, c * n:(c + 1) * n], xin[p][0:n, cc * P:(cc + 1) * P],
                                                       ident[0:n, 0:n])
                        last.then_inc(full[bk], 1)

                with pe.Fori(0, NCH // 2) as i:
                    f = Fills(banks, i, {2: 2, 3: 2})
                    for p in range(2):
                        x_tile(f, p, P, 16 * i + 16)
                banks.skip({2: 2, 3: 2}, NCH // 2)
                if q.sample:
                    x_tile(banks, 0, TS, 16 * (NCH // 2 + 1))
                pe.wait_ge(v["x_sum"], KC - 1)
                sum_over_features(q)

                linear(q, s0, uses, lambda b, k: pe.wait_ge(v["low"], KC * b + k + 1))
                slab_ready(s0 + 8)
                for b in range(nb):
                    product(q, banks.take(b % 2), b % 2, par, KC, 0, b, begins=b == 0)
                was_read(pe, banks, 0, 1)
                lf, columns, pairs, over_chunk = prep_fills(banks, q)
                for b, (b0, bl) in enumerate(q.blocks):
                    pe.wait_ge(free[2 + b], lf[b])
                    nc.tensor.matmul(bank[2 + b][0:NH, 0:bl], ident[0:2 * NH, NH:2 * NH], G[0:2 * NH, b0:b0 + bl],
                                     start=True, stop=True).then_inc(full[2 + b], 1)
                pe.wait_ge(v["rows_exp"], 3)
                pe.wait_ge(free[5], columns)
                for r, row in enumerate((CS, LF, EM)):
                    for t in range(q.tiles):
                        n = P if t < NCH else TS
                        col = (r * (NCH + 1) + t) * NH
                        last = nc.tensor.transpose(bank[5][0:n, col:col + NH], row[0:NH, t * P:t * P + n], ident[0:NH, 0:NH])
                last.then_inc(full[5], 1)
                k = 0
                for j in range(PAIRS):
                    for b0, bl in q.blocks:
                        bk, no = pairs[k]
                        pe.wait_ge(free[bk], no)
                        nc.tensor.matmul(bank[bk][:, 0:bl], pair_rows[:, j, :], W[0:NH, b0:b0 + bl], start=True, stop=True)\
                            .then_inc(full[bk], 1)
                        k += 1
                pe.wait_ge(free[4], over_chunk)
                for j in range(PAIRS):
                    c0 = j * (NCH + NB_S)
                    last = nc.tensor.matmul(bank[4][:, c0:c0 + NCH], pair_rows[:, j, :], W[0:NH, P - 1:TP:P],
                                            start=True, stop=True)
                    if q.sample:
                        last = nc.tensor.matmul(bank[4][:, c0 + NCH:c0 + NCH + NB_S], pair_rows[:, j, :],
                                                W[0:NH, TP + NT_S - 1:TM:NT_S], start=True, stop=True)
                last.then_inc(full[4], 1)

                n0 = list(banks.n)
                loop_uses = {0: 2 * nb, 1: 2 * nb}
                with pe.Fori(0, 4) as i:
                    f = Fills(banks, i, loop_uses)
                    k = nb % 2
                    for n in range(4):
                        c = 2 * i + n // 2
                        if n % 2 == 0:
                            chunk_scores(v, n0, c)
                        else:
                            chunk_outputs(v, n0, c)
                        slab_ready(s0 + 9 + n + 4 * i)
                        for b in range(nb):
                            product(q, f.take(k % 2), k % 2, (par + 9 + n) % 2, KC, 0, b, begins=b == 0)
                            k += 1
                        if n % 2:
                            chunk_transposes(v, n0, c)
                banks.skip(loop_uses, 4)
                banks.skip(CHUNK_USES, NCH)

                if q.sample:
                    f = ChunkFills(n0, NCH)
                    chunk_scores(v, n0, NCH, TS)
                    pe.wait_ge(free[3], f.score + 1)
                    pe.wait_ge(free[7], f.values + 1)
                    pe.wait_ge(batch_queries, NH)
                    pe.wait_ge(states_in, 16 * 2 * PAIRS)
                    for bk, no, hs in ((4, f.out01, (0, 1)), (5, f.out23, (2, 3))):
                        pe.wait_ge(free[bk], no)
                        for h in hs:
                            o = bank[bk][0:TS, (h % 2) * (DV + 1):(h % 2 + 1) * (DV + 1)]
                            nc.tensor.matmul(o, Pm[:, h, 0:TS], V[:, h, :], start=True, stop=False)
                            for b in range(NB_S):
                                last = nc.tensor.matmul(o, qb[:, h, b, :], Cs[:, h // 2, b, :], start=False,
                                                        stop=b == NB_S - 1)
                        last.then_inc(full[bk], 1)
                    pe.wait_ge(batch_keys, NH)
                    banks.skip(CHUNK_USES)
                    banks.n[6] -= 1
                    for j in range(PAIRS):
                        for g, b0 in enumerate((0, 3, 6)):
                            bk = (2, 3, 6)[g]
                            pe.wait_ge(free[bk], banks.take(bk))
                            for hh in range(2):
                                for b in range(b0, min(b0 + 3, NB_S)):
                                    o = bank[bk][hh * DK:(hh + 1) * DK, (b - b0) * (DV + 1):(b - b0 + 1) * (DV + 1)]
                                    last = nc.tensor.matmul(o, kwb[:, 2 * j + hh, b, :], V[0:TS, 2 * j + hh, :],
                                                            start=True, stop=True)
                            last.then_inc(full[bk], 1)
                    chunk_transposes(v, n0, NCH, TS)

                pe.wait_ge(v["p_landed"], 16 * (1 + q.sample))
                for g in range(NCH // 2):
                    bk = 2 + g
                    pe.wait_ge(free[bk], banks.take(bk))
                    for t in range(2):
                        for c in range(2):
                            o = bank[bk][:, (2 * t + c) * P:(2 * t + c + 1) * P]
                            last = nc.tensor.transpose(o, pst[:, 2 * g + t, c * P:(c + 1) * P], ident[:, :])
                    last.then_inc(full[bk], 1)
                if q.sample:
                    pe.wait_ge(free[6], banks.take(6))
                    for c in range(2):
                        last = nc.tensor.transpose(bank[6][:, c * TS:(c + 1) * TS], pst_s[0:TS, c * P:(c + 1) * P],
                                                   ident[0:TS, 0:TS])
                    last.then_inc(full[6], 1)

                s = s0 + 25
                linear(q, s, uses, lambda b, k: pe.wait_ge(v["mix_lo"], KC))
                s += 8
                pe.wait_ge(v["res_sum"], KC * nb + 2)
                sum_over_features(q)
                was_read(pe, banks, 2, 3, 4, 5)
                k = 0
                for p in range(2):
                    slab_ready(s)
                    for n in range(4):
                        for b in range(nb):
                            product(q, banks.take(k % 2), k % 2, s % 2, 2, n, b, (hid[:, 0], hid[:, 1]),
                                    begins=n == 0 and b == 0)
                            k += 1
                    s += 1

                def normed_ready(b, k):
                    pe.wait_ge(v["low2"], KC * b + k + 1)

                def up_chunk(f, s, p, first):
                    for w in range(2):
                        slab_ready(s + w)
                        for b in range(nb):
                            product(q, f.take(3 * w + b), 3 * w + b, (p + w) % 2, KC, 0, b, begins=b == 0,
                                    ready=normed_ready if first and w == 0 else None)

                def down(f, s, p, size, before):
                    def hidden_ready(b, k):
                        pe.wait_ge(v["h_lo"], nb * (before + 1) + nb * k + b + 1)

                    nw = SLAB // size // P
                    k = 0
                    for m in range(KC // nw):
                        slab_ready(s + m)
                        for n in range(nw):
                            for b in range(nb):
                                product(q, f.take(6 + k % 2), 6 + k % 2, (p + m) % 2, size, n, b, (hid[:, 0], hid[:, 1]),
                                        begins=n == 0 and b == 0, ready=hidden_ready if m == 0 and n == 0 else None)
                                k += 1

                ffn_uses = {b: 4 for b in range(nb)}
                ffn_uses.update({3 + b: 4 for b in range(nb)})
                ffn_uses.update({6: 4 * nb, 7: 4 * nb})
                with pe.Fori(0, 4) as g:
                    f = Fills(banks, g, ffn_uses)
                    for c in range(GROUP):
                        up_chunk(f, s + 2 * c + 12 * g, s % 2, c == 0)
                    down(f, s + 8 + 12 * g, s % 2, GROUP, GROUP * g)
                banks.skip(ffn_uses, 4)
                s += 48
                for size, before in ((4, 16), (2, 20)):
                    if size == 2:
                        pe.wait_ge(v["e_sum"], KC * nb + 2)
                        sum_over_features(q)
                    for c in range(size):
                        up_chunk(banks, s, s % 2, False)
                        s += 2
                    down(banks, s, s % 2, size, before)
                    s += size

                linear(q, s, uses, lambda b, k: pe.wait_ge(v["x3_lo"], k * nb + b + 1))
                s += 8
                assert s == s0 + SLABS
                pe.wait_ge(v["x4_sum"], KC * nb + 2)
                sum_over_features(q)
                for t in range(q.tiles):
                    n = P if t < NCH else TS
                    last_block = (t * P + n - 1) // q.blocks[0][1]
                    pe.wait_ge(v["y_t"], KC * (last_block + 1))
                    for bk in (2, 3):
                        pe.wait_ge(free[bk], banks.take(bk))
                        for c in range(4):
                            last = nc.tensor.transpose(bank[bk][0:n, c * P:(c + 1) * P],
                                                       U[:, (bk - 2) * 4 + c, t * P:t * P + n], ident[:, :])
                        last.then_inc(full[bk], 1)

        @block.scalar
        def _(act):
            banks = Banks()
            act.sem_inc(hi_done, 2)
            act.wait_ge(consts_made, 1)
            act.wait_ge(consts_in, 16 * N_CONSTS)

            def next_high(s, i=0, step=0):
                p = s % 2
                act.wait_ge(landed[p], 16 * (s // 2 + 1) + 8 * step * i)
                act.wait_ge(slab_begun, s + 1 + step * i)
                nc.scalar.activation(whi[p][:, :], wraw[p][:, :], ACT.Copy).then_inc(hi_done, 1)

            def roots(q, bk=6):
                for b0, bl in q.blocks:
                    act.wait_ge(full[bk], banks.take(bk))
                    nc.scalar.activation(ss[:, b0:b0 + bl], bank[bk][:, 0:bl], ACT.Sqrt, bias=epst[:, 0:1],
                                         scale=1.0 / D).then_inc(free[bk], 1)

            def high_of_normed(v, q, m, normed, high):
                c, (b0, bl) = m % KC, q.blocks[m // KC]
                act.wait_ge(v[normed], m + 1)
                nc.scalar.activation(AH[:, c, b0:b0 + bl], tmp[m % 3][:, 0:bl], ACT.Copy).then_inc(v[high], 1)

            def chunk_exps(v, n0, c, p, n=P):
                f = ChunkFills(n0, c)
                act.wait_ge(v["staged"], c + 1)
                act.wait_ge(free[5], f.out23)
                act.wait_ge(full[2], f.exponent)
                for h in range(NH):
                    last = nc.scalar.activation(expE[0:n, h, 0:n], bank[2][0:n, h * n:(h + 1) * n], ACT.Exp,
                                                bias=colst[p][0:n, h:h + 1])
                last.then_inc(free[2], 1)
                act.wait_ge(full[7], f.values)
                nc.scalar.activation(V[0:n, :, 0:DV], bank[7][0:n, :].rearrange("p (h e) -> p h e", h=NH), ACT.Copy)\
                    .then_inc(free[7], 1)

            def chunk_squares(v, n0, c, n=P):
                f = ChunkFills(n0, c)
                act.wait_ge(free[3], f.score + 1)
                for bk, no, hs in ((4, f.out01, (0, 1)), (5, f.out23, (2, 3))):
                    act.wait_ge(full[bk], no)
                    for h in hs:
                        o = (h % 2) * (DV + 1)
                        last = nc.scalar.activation(expE[0:n, h, :], bank[bk][0:n, o:o + DV], ACT.Square,
                                                    scale=DV ** -0.5, accum_out=ss4[0:n, h:h + 1])
                last.then_inc(v["sq_done"], 1)

            def chunk_out(n0, c, tok, n=P):
                act.wait_ge(full[7], ChunkFills(n0, c).h_t)
                nc.scalar.activation(X[:, 4:8, tok], bank[7][:, 0:NH * n].rearrange("p (h t) -> p h t", h=NH), ACT.Copy)\
                    .then_inc(free[7], 1)

            next_high(0)
            for q in supers:
                v, s0, nb = S[q.n], q.slab0, q.nb
                uses = {0: nb, 1: nb}
                with act.Fori(0, NCH // 2) as i:
                    f = Fills(banks, i, {2: 2})
                    for p in range(2):
                        act.wait_ge(full[2], f.take(2))
                        nc.scalar.activation(X[:, 0:4, ds(i * 2 * P + p * P, P)],
                                             bank[2][:, :].rearrange("p (c t) -> p c t", c=4), ACT.Copy).then_inc(free[2], 1)
                banks.skip({2: 2, 3: 2}, NCH // 2)
                if q.sample:
                    act.wait_ge(full[2], banks.take(2))
                    banks.take(3)
                    nc.scalar.activation(X[:, 0:4, TP:TM], bank[2][:, 0:4 * TS].rearrange("p (c t) -> p c t", c=4), ACT.Copy)\
                        .then_inc(free[2], 1)
                was_read(act, banks, 2, 3)
                for c in range(KC):
                    if c >= 3:
                        act.wait_ge(v["x_sum"], c - 2)
                    dst = sqt[c % 2] if c else ss
                    nc.scalar.activation(dst[:, 0:q.T], X[:, c, 0:q.T], ACT.Square).then_inc(v["x_sq"], 1)
                roots(q)
                for m in range(KC * nb):
                    high_of_normed(v, q, m, "normed", "high")

                act.wait_ge(v["x_spilled"], 16)
                with act.Fori(0, 4) as i:
                    f = Fills(banks, i, uses)
                    k = 0
                    for p in range(2):
                        next_high(s0 + p + 1, i, 2)
                        for b0, bl in q.blocks:
                            act.wait_ge(full[k % 2], f.take(k % 2))
                            nc.scalar.activation(X[:, 2 * i + p, b0:b0 + bl], bank[k % 2][:, 0:bl], ACT.Copy)\
                                .then_inc(free[k % 2], 1)
                            k += 1
                banks.skip(uses, 4)
                next_high(s0 + 9)
                for b in range(nb):
                    banks.take(b % 2)
                lf, columns, pairs, over_chunk = prep_fills(banks, q)
                for b, (b0, bl) in enumerate(q.blocks):
                    act.wait_ge(full[2 + b], lf[b])
                    nc.scalar.activation(EM[0:NH, b0:b0 + bl], bank[2 + b][0:NH, 0:bl], ACT.Abs).then_inc(v["lf_abs"], 1)
                nc.scalar.activation(G[0:NH, 0:q.T], G[0:NH, 0:q.T], ACT.Tanh, scale=1.0 / GATE_CAP).then_inc(v["softcap"], 1)
                act.wait_ge(v["lf_abs"], nb)
                nc.scalar.activation(EM[0:NH, 0:q.T], EM[0:NH, 0:q.T], ACT.Exp, scale=-1.0).then_inc(v["lf_abs"], 1)
                act.wait_ge(v["lf_abs"], nb + 1)
                nc.scalar.activation(EM[0:NH, 0:q.T], EM[0:NH, 0:q.T], ACT.Ln, bias=1.0).then_inc(v["lf_soft"], 1)
                act.wait_ge(v["rows_made"], 1)
                for row, src, scale in ((EM, M, -1.0), (W, W, 1.0), (LF, LF, 1.0)):
                    nc.scalar.activation(row[0:NH, 0:q.T], src[0:NH, 0:q.T], ACT.Exp, scale=scale).then_inc(v["rows_exp"], 1)

                n0 = list(banks.n)
                loop_uses = {0: 2 * nb, 1: 2 * nb}
                with act.Fori(0, 4) as i:
                    f = Fills(banks, i, loop_uses)
                    k = nb % 2
                    for n in range(4):
                        c = 2 * i + n // 2
                        next_high(s0 + 10 + n, i, 4)
                        if n % 2 == 0:
                            chunk_exps(v, n0, c, n // 2)
                        else:
                            chunk_squares(v, n0, c)
                        for b0, bl in q.blocks:
                            no = f.take(k % 2)
                            if n < 2:
                                act.wait_ge(full[k % 2], no)
                                if n == 1:
                                    act.wait_ge(v["conv_done"], i + 1)
                                dst = zbuf[:, 2 + b0:2 + b0 + bl] if n else U[:, i, b0:b0 + bl]
                                nc.scalar.activation(dst, bank[k % 2][:, 0:bl], ACT.Copy).then_inc(free[k % 2], 1)
                            k += 1
                        if n % 2:
                            chunk_out(n0, c, ds(c * P, P))
                banks.skip(loop_uses, 4)
                banks.skip(CHUNK_USES, NCH)
                if q.sample:
                    chunk_exps(v, n0, NCH, 0, TS)
                    chunk_squares(v, n0, NCH, TS)
                    chunk_out(n0, NCH, slice(TP, TM), TS)
                    banks.skip(CHUNK_USES)
                    banks.skip({2: 2, 3: 2, 6: 1})

                was_filled(act, banks, 0, 1)
                was_read(act, banks, 0, 1)
                for m in (4, 5, 6, 7):
                    nc.scalar.activation(AH[:, m, 0:q.T], U[:, m, 0:q.T], ACT.Copy).then_inc(v["mix_hi"], 1)
                for m in range(4):
                    nc.scalar.activation(U[:, m, 0:q.T], U[:, m, 0:q.T], ACT.Sigmoid).then_inc(v["sig_o"], 1)
                for m in range(4):
                    act.wait_ge(v["merged"], m + 1)
                    nc.scalar.activation(AH[:, m, 0:q.T], U[:, m, 0:q.T], ACT.Copy).then_inc(v["mix_hi"], 1)
                for g in range(NCH // 2):
                    act.wait_ge(full[2 + g], banks.take(2 + g))
                    src = bank[2 + g][:, :].rearrange("p (t c n) -> p c t n", t=2, c=2)
                    dst = hid[:, 0, 0:2, 2 * g * P:(2 * g + 2) * P].rearrange("p c (t n) -> p c t n", t=2)
                    nc.scalar.activation(dst, src, ACT.Copy).then_inc(v["p_hi"], 1)
                if q.sample:
                    act.wait_ge(full[6], banks.take(6))
                    nc.scalar.activation(hid[:, 0, 0:2, TP:TM], bank[6][:, 0:2 * TS].rearrange("p (c n) -> p c n", c=2),
                                         ACT.Copy).then_inc(v["p_hi"], 1)

                s = s0 + 25
                with act.Fori(0, 4) as i:
                    f = Fills(banks, i, uses)
                    k = 0
                    for p in range(2):
                        next_high(s + p + 1, i, 2)
                        for b0, bl in q.blocks:
                            act.wait_ge(free[k % 2], f.take(k % 2) + 1)
                            act.wait_ge(v["res_sum"], k + 1 + 2 * nb * i)
                            nc.scalar.activation(tmp[k % 2][:, 0:bl], X[:, 2 * i + p, b0:b0 + bl], ACT.Square)\
                                .then_inc(v["res_sq"], 1)
                            k += 1
                banks.skip(uses, 4)
                s += 8
                roots(q)
                for m in range(KC * nb):
                    n, (b0, bl) = m // nb, q.blocks[m % nb]
                    if m % (4 * nb) == 0:
                        next_high(s + 1)
                        s += 1
                    act.wait_ge(full[m % 2], banks.take(m % 2))
                    nc.scalar.activation(U[:, n, b0:b0 + bl], bank[m % 2][:, 0:bl], ACT.Copy).then_inc(free[m % 2], 1)
                    high_of_normed(v, q, m, "normed2", "high2")

                def up_chunk(f, s, i, hc, count):
                    next_high(s + 1, i, 12)
                    for b, (b0, bl) in enumerate(q.blocks):
                        act.wait_ge(full[b], f.take(b))
                        act.wait_ge(v["h_lo"], count + b + 1)
                        nc.scalar.activation(sl[:, b0:b0 + bl], bank[b][:, 0:bl], ACT.Silu).then_inc(free[b], 1)
                    next_high(s + 2, i, 12)
                    for b, (b0, bl) in enumerate(q.blocks):
                        act.wait_ge(free[3 + b], f.take(3 + b) + 1)
                        nc.scalar.activation(hid[:, 0, hc, b0:b0 + bl], sl[:, b0:b0 + bl], ACT.Copy).then_inc(v["h_hi"], 1)

                ffn_uses = {b: 4 for b in range(nb)}
                ffn_uses.update({3 + b: 4 for b in range(nb)})
                ffn_uses.update({6: 4 * nb, 7: 4 * nb})
                with act.Fori(0, 4) as g:
                    f = Fills(banks, g, ffn_uses)
                    for c in range(GROUP):
                        up_chunk(f, s + 2 * c, g, c, nb * (c + GROUP * g))
                    k = 0
                    for n in range(4):
                        next_high(s + 9 + n, g, 12)
                        if n >= 2:
                            for b0, bl in q.blocks:
                                act.wait_ge(v["e_sum"], k + 1 + 2 * nb * g)
                                nc.scalar.activation(tmp[k % 2][:, 0:bl], U[:, 2 * g + n - 2, b0:b0 + bl], ACT.Square)\
                                    .then_inc(v["e_sq"], 1)
                                k += 1
                banks.skip(ffn_uses, 4)
                s += 48
                count = 16 * nb
                for size in (4, 2):
                    if size == 2:
                        roots(q)
                    for c in range(size):
                        up_chunk(banks, s, 0, c, count)
                        count += nb
                        s += 2
                    k = 0
                    for m in range(size):
                        next_high(s + 1)
                        for n in range(KC // size * nb):
                            no = banks.take(6 + k % 2)
                            if size == 2:
                                c, (b0, bl) = k // nb, q.blocks[k % nb]
                                act.wait_ge(free[6 + k % 2], no + 1)
                                nc.scalar.activation(AH[:, c, b0:b0 + bl], X[:, c, b0:b0 + bl], ACT.Copy).then_inc(v["x3_hi"], 1)
                            k += 1
                        s += 1

                def gate_slab(f, s, i, step, p, last):
                    if not last:
                        next_high(s + p + 1, i, step)
                    for b, (b0, bl) in enumerate(q.blocks):
                        k = p * nb + b
                        act.wait_ge(full[k % 2], f.take(k % 2))
                        act.wait_ge(v["x4"], k + 1 + nb * step * i)
                        nc.scalar.activation(sl[:, b0:b0 + bl], bank[k % 2][:, 0:bl], ACT.Sigmoid).then_inc(free[k % 2], 1)
                    for b, (b0, bl) in enumerate(q.blocks):
                        k = p * nb + b
                        act.wait_ge(v["x4"], k + 1 + nb + nb * step * i)
                        act.wait_ge(v["x4_sum"], k + 1 + nb * step * i)
                        nc.scalar.activation(tmp[k % 2][:, 0:bl], X[:, 2 * i + p, b0:b0 + bl], ACT.Square)\
                            .then_inc(v["x4_sq"], 1)

                with act.Fori(0, 3) as i:
                    f = Fills(banks, i, uses)
                    for p in range(2):
                        gate_slab(f, s, i, 2, p, False)
                banks.skip(uses, 3)
                f = Fills(banks, 0, uses)
                for p in range(2):
                    last_slab = q.sample and p == 1
                    if not last_slab:
                        next_high(s + 6 + p + 1)
                    for b, (b0, bl) in enumerate(q.blocks):
                        k = p * nb + b
                        act.wait_ge(full[k % 2], f.take(k % 2))
                        act.wait_ge(v["x4"], k + 1 + 6 * nb)
                        nc.scalar.activation(sl[:, b0:b0 + bl], bank[k % 2][:, 0:bl], ACT.Sigmoid).then_inc(free[k % 2], 1)
                    for b, (b0, bl) in enumerate(q.blocks):
                        k = p * nb + b
                        act.wait_ge(v["x4"], k + 1 + 7 * nb)
                        act.wait_ge(v["x4_sum"], k + 1 + 6 * nb)
                        nc.scalar.activation(tmp[k % 2][:, 0:bl], X[:, 6 + p, b0:b0 + bl], ACT.Square)\
                            .then_inc(v["x4_sq"], 1)
                banks.skip(uses, 1)
                roots(q)
                for t in range(q.tiles):
                    n = P if t < NCH else TS
                    act.wait_ge(full[2], banks.take(2))
                    banks.take(3)
                    if t >= 2:
                        act.wait_ge(v[f"y_out{t % 2}"], 16 * (t // 2))
                    nc.scalar.activation(yst[t % 2][0:n, 0:512], bank[2][0:n, :], ACT.Copy).then_inc(free[2], 1)

        @block.vector
        def _(dve):
            banks = Banks()
            for b in range(8):
                dve.sem_inc(free[b], 1)
            for q in supers:
                dve.sem_inc(S[q.n]["h_lo"], q.nb)
                dve.sem_inc(S[q.n]["x4"], q.nb)
                dve.sem_inc(S[q.n]["conv_done"], 1)
            dve.wait_ge(consts_made, 1)
            dve.wait_ge(consts_in, 16 * N_CONSTS)
            own = Chain(dve, dve_own)

            def copy_at(out, in_):
                return nc.vector.tensor_scalar(out, in_, 1.0, None, ALU.mult)

            def normalise(v, q, g, normed, high, low):
                total = KC * q.nb

                def low_part(m):
                    c, (b0, bl) = m % KC, q.blocks[m // KC]
                    dve.wait_ge(v[high], m + 1)
                    nc.vector.tensor_tensor(AL[:, c, b0:b0 + bl], tmp[m % 3][:, 0:bl], AH[:, c, b0:b0 + bl],
                                            ALU.subtract).then_inc(v[low], 1)

                for m in range(total):
                    c, b, (b0, bl) = m % KC, m // KC, q.blocks[m // KC]
                    if c == 0:
                        dve.wait_ge(free[6], banks.take(6) + 1)
                        own.link(nc.vector.reciprocal(ss[:, b0:b0 + bl], ss[:, b0:b0 + bl]))
                    if m >= 3:
                        dve.wait_ge(v[low], m - 2)
                    nc.vector.scalar_tensor_tensor(tmp[m % 3][:, 0:bl], X[:, c, b0:b0 + bl], g[:, c:c + 1],
                                                   ss[:, b0:b0 + bl], ALU.mult, ALU.mult).then_inc(v[normed], 1)
                    if m:
                        low_part(m - 1)
                low_part(total - 1)

            def chunk_weights(v, n0, c, p, n=P):
                f = ChunkFills(n0, c)
                dve.wait_ge(free[2], f.exponent + 1)
                dve.wait_ge(full[3], f.score)
                nc.vector.scalar_tensor_tensor(Pm[0:n, :, 0:n], bank[3][0:n, 0:NH * n].rearrange("p (h t) -> p h t", h=NH),
                                               QSCALE, expE[0:n, :, 0:n], ALU.mult, ALU.mult)\
                    .then_inc(free[3], 1)
                dve.wait_ge(full[4], f.keys)
                nc.vector.tensor_tensor(kw[0:n, :, :], bank[4][0:n, 0:NH * DK].rearrange("p (h d) -> p h d", h=NH),
                                        colst[p][0:n, 4:8].unsqueeze(2).to_broadcast([n, NH, DK]), ALU.mult)\
                    .then_inc(free[4], 1)

            def chunk_heads(v, n0, c, p, n=P):
                f = ChunkFills(n0, c)
                dve.wait_ge(v["sq_done"], c + 1)
                for bk, no, h in ((4, f.out01, 0), (5, f.out23, 2)):
                    dve.wait_ge(full[bk], no)
                    den = bank[bk][0:n, 0:2 * (DV + 1)].rearrange("p (h e) -> p h e", h=2)[:, :, DV]
                    own.link(nc.vector.scalar_tensor_tensor(dm[0:n, h:h + 2], den, -1.0, colst[p][0:n, 8 + h:10 + h],
                                                            ALU.mult, ALU.max))
                    own.link(nc.vector.tensor_tensor(dm[0:n, h:h + 2], den, dm[0:n, h:h + 2], ALU.max))
                own.link(nc.vector.scalar_tensor_tensor(d2[0:n, :], dm[0:n, :], EPS, dm[0:n, :], ALU.mult, ALU.mult))
                nc.vector.tensor_tensor(tt[0:n, :], d2[0:n, :], ss4[0:n, :], ALU.add).then_inc(v["root_in"], 1)
                dve.wait_ge(v["root_done"], c + 1)
                for bk, h in ((4, 0), (5, 2)):
                    num = bank[bk][0:n, 0:2 * (DV + 1)].rearrange("p (h e) -> p h e", h=2)[:, :, 0:DV]
                    nc.vector.tensor_tensor(hn[0:n, h:h + 2, :], num, rr[0:n, h:h + 2].unsqueeze(2).to_broadcast([n, 2, DV]),
                                            ALU.mult).then_inc(free[bk], 1)

            for q in supers:
                v, s0, nb = S[q.n], q.slab0, q.nb
                T = q.T
                uses = {0: nb, 1: nb}
                with dve.Fori(0, NCH // 2) as i:
                    f = Fills(banks, i, {3: 2})
                    for p in range(2):
                        dve.wait_ge(full[3], f.take(3))
                        copy_at(X[:, 4:8, ds(i * 2 * P + p * P, P)],
                                bank[3][:, :].rearrange("p (c t) -> p c t", c=4)).then_inc(free[3], 1)
                banks.skip({2: 2, 3: 2}, NCH // 2)
                if q.sample:
                    banks.take(2)
                    dve.wait_ge(full[3], banks.take(3))
                    nc.vector.tensor_copy(X[:, 4:8, TP:TM], bank[3][:, 0:4 * TS].rearrange("p (c t) -> p c t", c=4))\
                        .then_inc(free[3], 1)
                for c in range(1, KC):
                    dve.wait_ge(v["x_sq"], c + 1)
                    if c > 1:
                        dve.wait_ge(v["x_sum"], c - 1)
                    nc.vector.tensor_tensor(ss[:, 0:T], ss[:, 0:T], sqt[c % 2][:, 0:T], ALU.add).then_inc(v["x_sum"], 1)
                normalise(v, q, gmix, "normed", "high", "low")

                banks.skip(uses, 4)
                for b, (b0, bl) in enumerate(q.blocks):
                    dve.wait_ge(full[b % 2], banks.take(b % 2))
                    nc.vector.tensor_scalar(G[0:2 * NH, b0:b0 + bl], bank[b % 2][0:2 * NH, 0:bl], bias8[:, 0:1], None,
                                            ALU.add).then_inc(free[b % 2], 1)
                lf, columns, pairs, over_chunk = prep_fills(banks, q)
                own.link(nc.vector.tensor_copy(pair_rows[:, :, :].rearrange("p j (hh d) -> p (j hh) d", hh=2),
                                               ident[0:NH, 0:NH].unsqueeze(2).to_broadcast([NH, NH, DK])))
                own.link(nc.vector.memset(W[0:NH, 0:T], 1.0))
                own.link(nc.vector.memset(W[0:NH, 0:TP:P], 0.0))
                if q.sample:
                    own.link(nc.vector.memset(W[0:NH, TP:TM:NT_S], 0.0))
                dve.wait_ge(v["lf_soft"], 1)
                for b, (b0, bl) in enumerate(q.blocks):
                    nc.vector.scalar_tensor_tensor(LF[0:NH, b0:b0 + bl], bank[2 + b][0:NH, 0:bl], 0.0, EM[0:NH, b0:b0 + bl],
                                                   ALU.min, ALU.subtract).then_inc(free[2 + b], 1)
                for b in range(nb):
                    dve.wait_ge(free[2 + b], lf[b] + 1)
                dve.wait_ge(v["softcap"], 1)
                own.link(nc.vector.tensor_scalar(G[0:NH, 0:T], G[0:NH, 0:T], GATE_CAP, None, ALU.mult))
                own.link(nc.vector.tensor_tensor_scan(B[0:NH, 0:T], W[0:NH, 0:T], LF[0:NH, 0:T], 0.0, ALU.mult, ALU.add))
                own.link(nc.vector.tensor_tensor_scan(M[0:NH, 0:TP], LF[0:NH, 0:TP], G[0:NH, 0:TP], carry[:, 0:1],
                                                      ALU.add, ALU.max))
                own.link(nc.vector.tensor_copy(mprev[:, 0:1], carry[:, :]))
                own.link(nc.vector.tensor_copy(mprev[:, 1:NCH], M[0:NH, P - 1:TP - P:P]))
                own.link(nc.vector.tensor_copy(carry[:, :], M[0:NH, TP - 1:TP]))
                if q.sample:
                    by_batch = "p (b t) -> p b t"
                    own.link(nc.vector.tensor_copy(sI[:, :, :], G[0:NH, TP:TM].rearrange(by_batch, t=NT_S)))
                    own.link(nc.vector.tensor_copy(sF[:, :, :], LF[0:NH, TP:TM].rearrange(by_batch, t=NT_S)))
                    own.link(nc.vector.tensor_copy(mprev[:, NCH:], ms0[:, :]))
                    own.link(nc.vector.tensor_tensor(m_out[:, :], sF[:, :, 0], ms0[:, :], ALU.add))
                    own.link(nc.vector.tensor_tensor(sI[:, :, 0], sI[:, :, 0], m_out[:, :], ALU.max))
                    own.link(nc.vector.memset(sF[:, :, 0], NEG))
                    own.link(nc.vector.tensor_tensor_scan(M[0:NH, TP:TM], sF[:, :, :].rearrange("p b t -> p (b t)"),
                                                          sI[:, :, :].rearrange("p b t -> p (b t)"), 0.0, ALU.add, ALU.max))
                    own.link(nc.vector.tensor_copy(m_out[:, :], M[0:NH, TP + NT_S - 1:TM:NT_S]))
                own.link(nc.vector.tensor_tensor(R1[0:NH, 0:T], B[0:NH, 0:T], M[0:NH, 0:T], ALU.subtract))
                own.link(nc.vector.tensor_tensor(CS[0:NH, 0:T], G[0:NH, 0:T], B[0:NH, 0:T], ALU.subtract))
                spans = [(0, TP, P, 0)] + ([(TP, TM, NT_S, NCH)] if q.sample else [])
                for a, z, n, m0 in spans:
                    k = (z - a) // n
                    by = dict(n=n)
                    r1 = R1[0:NH, a:z].rearrange("p (c n) -> p c n", **by)
                    own.link(nc.vector.tensor_tensor(W[0:NH, a:z].rearrange("p (c n) -> p c n", **by), r1,
                                                     mprev[:, m0:m0 + k].unsqueeze(2).to_broadcast([NH, k, n]), ALU.add))
                    end = R1[0:NH, a + n - 1:z:n].unsqueeze(2).to_broadcast([NH, k, n])
                    own.link(nc.vector.tensor_tensor(LF[0:NH, a:z].rearrange("p (c n) -> p c n", **by),
                                                     CS[0:NH, a:z].rearrange("p (c n) -> p c n", **by), end, ALU.add))
                dve.sem_inc(v["rows_made"], 1)
                dve.wait_ge(full[5], columns)
                stripe = bank[5][:, 0:3 * (NCH + 1) * NH].rearrange("p (r c h) -> p r c h", r=3, h=NH)
                if q.sample:
                    own.link(nc.vector.tensor_copy(cols[0:TS, :, NCH, :], stripe[0:TS, :, NCH, :]))
                nc.vector.tensor_copy(cols[:, :, 0:NCH, :], stripe[:, :, 0:NCH, :]).then_inc(free[5], 1)
                k = 0
                for j in range(PAIRS):
                    for b0, bl in q.blocks:
                        bk, no = pairs[k]
                        dve.wait_ge(full[bk], no)
                        nc.vector.scalar_tensor_tensor(qw[:, j, b0:b0 + bl], X[:, j, b0:b0 + bl], QSCALE,
                                                       bank[bk][:, 0:bl], ALU.mult, ALU.mult).then_inc(free[bk], 1)
                        k += 1
                dve.wait_ge(full[4], over_chunk)
                width = NCH + NB_S if q.sample else NCH
                nc.vector.tensor_copy(decay[:, :, 0:width],
                                      bank[4][:, 0:PAIRS * (NCH + NB_S)].rearrange("p (j c) -> p j c", j=PAIRS)[:, :, 0:width])\
                    .then_inc(free[4], 1)

                n0 = list(banks.n)
                loop_uses = {0: 2 * nb, 1: 2 * nb}

                def state_update(c, p):
                    dve.wait_ge(full[6], ChunkFills(n0, c).state)
                    for j in range(PAIRS):
                        last = nc.vector.scalar_tensor_tensor(state[:, j, :], state[:, j, :], colst[p][:, 12 + j:13 + j],
                                                              bank[6][:, j * (DV + 1):(j + 1) * (DV + 1)], ALU.mult, ALU.add)
                    last.then_inc(free[6], 1)

                with dve.Fori(0, 4) as i:
                    f = Fills(banks, i, loop_uses)
                    own.loop(i, 2 * 5 + 4 + (2 + 1 + 2 + 1 if q.sample else 0))
                    k = nb % 2
                    turns = []
                    for n in range(4 * nb):
                        turns.append((k % 2, f.take(k % 2)))
                        k += 1
                    chunk_weights(v, n0, 2 * i, 0)
                    state_update(2 * i, 0)
                    chunk_heads(v, n0, 2 * i, 0)
                    chunk_weights(v, n0, 2 * i + 1, 1)
                    for b, (b0, bl) in enumerate(q.blocks):
                        dve.wait_ge(free[turns[nb + b][0]], turns[nb + b][1] + 1)
                        bk, no = turns[2 * nb + b]
                        dve.wait_ge(full[bk], no)
                        z = zbuf[:, 2 + b0:2 + b0 + bl]
                        nc.vector.tensor_tensor(z, z, bank[bk][:, 0:bl], ALU.mult).then_inc(free[bk], 1)
                    for b in range(2):
                        bk, no = turns[2 * nb + nb - 1 - b]
                        dve.wait_ge(free[bk], no + 1)
                    own.link(copy_at(zbuf[:, 0:2], hist[:, i, :]))
                    own.link(copy_at(hist[:, i, :], zbuf[:, TP:TP + 2]))
                    if q.sample:
                        own.link(copy_at(zs[:, :, 0:2], convs[:, i, :, :]))
                        own.link(nc.vector.tensor_copy(zs[:, :, 2:], zbuf[:, 2 + TP:2 + TM].rearrange("p (b t) -> p b t", t=NT_S)))
                    own.link(nc.vector.tensor_scalar(cv[:, 0:T], zbuf[:, 2:2 + T], cw[:, 2, ds(i, 1)], None, ALU.mult))
                    own.link(nc.vector.scalar_tensor_tensor(cv[:, 0:T], zbuf[:, 1:1 + T], cw[:, 1, ds(i, 1)], cv[:, 0:T],
                                                            ALU.mult, ALU.add))
                    nc.vector.scalar_tensor_tensor(cv[:, 0:T], zbuf[:, 0:T], cw[:, 0, ds(i, 1)], cv[:, 0:T],
                                                   ALU.mult, ALU.add).then_inc(v["conv_done"], 1)
                    dve.wait_ge(v["conv_done"], i + 2)
                    if q.sample:
                        own.link(copy_at(convs[:, i, :, :], zs[:, :, NT_S:]))
                        cvs = cv[:, TP:TM].rearrange("p (b t) -> p b t", t=NT_S)
                        own.link(nc.vector.tensor_scalar(cvs, zs[:, :, 2:], cw[:, 2, ds(i, 1)], None, ALU.mult))
                        for w in (1, 0):
                            tail = nc.vector.scalar_tensor_tensor(cvs, zs[:, :, w:w + NT_S], cw[:, w, ds(i, 1)], cvs,
                                                                  ALU.mult, ALU.add)
                            own.link(tail)
                    state_update(2 * i + 1, 1)
                    chunk_heads(v, n0, 2 * i + 1, 1)
                    for b, (b0, bl) in enumerate(q.blocks):
                        bk, no = turns[3 * nb + b]
                        dve.wait_ge(full[bk], no)
                        nc.vector.tensor_tensor(U[:, i + 4, b0:b0 + bl], cv[:, b0:b0 + bl], bank[bk][:, 0:bl], ALU.mult)\
                            .then_inc(free[bk], 1)
                own.done(4)
                banks.skip(loop_uses, 4)
                banks.skip(CHUNK_USES, NCH)

                if q.sample:
                    f = ChunkFills(n0, NCH)
                    dve.wait_ge(free[5], f.out23)
                    own.link(nc.vector.memset(Pm[:, :, 0:TS], 0.0))
                    chunk_weights(v, n0, NCH, 0, TS)
                    dve.wait_ge(free[4], f.keys + 1)
                    dve.wait_ge(v["staged"], NCH + 1)
                    for h in range(NH):
                        nc.vector.tensor_tensor(kwb[:, h, :, :], kw[0:TS, h, :].unsqueeze(1).to_broadcast([TS, NB_S, DK]),
                                                batch_s[0:TS, :].unsqueeze(2).to_broadcast([TS, NB_S, DK]), ALU.mult)\
                            .then_inc(batch_keys, 1)
                    chunk_heads(v, n0, NCH, 0, TS)
                    banks.skip(CHUNK_USES)
                    banks.n[6] -= 1
                    for j in range(PAIRS):
                        own.link(nc.vector.tensor_tensor(
                            Cs[:, j, :, :], Cs[:, j, :, :],
                            decay[:, j, NCH:].unsqueeze(2).to_broadcast([P, NB_S, DV + 1]), ALU.mult))
                        for bk, b0 in ((2, 0), (3, 3), (6, 6)):
                            n = min(3, NB_S - b0)
                            dve.wait_ge(full[bk], banks.take(bk))
                            nc.vector.tensor_tensor(Cs[:, j, b0:b0 + n, :], Cs[:, j, b0:b0 + n, :],
                                                    bank[bk][:, 0:n * (DV + 1)].rearrange("p (b e) -> p b e", b=n), ALU.add)\
                                .then_inc(free[bk], 1)

                def mix_low(m, hi_count):
                    dve.wait_ge(v["mix_hi"], hi_count)
                    nc.vector.tensor_tensor(AL[:, m, 0:T], U[:, m, 0:T], AH[:, m, 0:T], ALU.subtract).then_inc(v["mix_lo"], 1)

                was_read(dve, banks, 7)
                for m in range(4):
                    mix_low(4 + m, m + 1)
                    dve.wait_ge(v["sig_o"], m + 1)
                    nc.vector.scalar_tensor_tensor(U[:, m, 0:T], X[:, 4 + m, 0:T], gmh[:, m:m + 1], U[:, m, 0:T],
                                                   ALU.mult, ALU.mult).then_inc(v["merged"], 1)
                for m in range(4):
                    mix_low(m, 5 + m)
                for g in range(NCH // 2):
                    banks.take(2 + g)
                    dve.wait_ge(v["p_hi"], g + 1)
                    toks = slice(2 * g * P, (2 * g + 2) * P)
                    for c in range(2):
                        src = bank[2 + g][:, :].rearrange("p (t c n) -> p c t n", t=2, c=2)[:, c]
                        last = nc.vector.tensor_tensor(hid[:, 1, c, toks].rearrange("p (t n) -> p t n", t=2), src,
                                                       hid[:, 0, c, toks].rearrange("p (t n) -> p t n", t=2), ALU.subtract)
                        if c == 0:
                            own.link(last)
                    last.then_inc(free[2 + g], 1)
                if q.sample:
                    banks.take(6)
                    dve.wait_ge(v["p_hi"], NCH // 2 + 1)
                    nc.vector.tensor_tensor(hid[:, 1, 0:2, TP:TM], bank[6][:, 0:2 * TS].rearrange("p (c n) -> p c n", c=2),
                                            hid[:, 0, 0:2, TP:TM], ALU.subtract).then_inc(free[6], 1)

                dve.wait_ge(v["reload"], 32)
                with dve.Fori(0, 4) as i:
                    f = Fills(banks, i, uses)
                    k = 0
                    for p in range(2):
                        for b0, bl in q.blocks:
                            dve.wait_ge(full[k % 2], f.take(k % 2))
                            x = X[:, 2 * i + p, b0:b0 + bl]
                            nc.vector.tensor_tensor(x, x, bank[k % 2][:, 0:bl], ALU.add).then_inc(free[k % 2], 1)
                            k += 1
                banks.skip(uses, 4)
                normalise(v, q, gffn, "normed2", "high2", "low2")
                banks.skip(uses, 4)

                def up_chunk(f, hc, count):
                    for b, (b0, bl) in enumerate(q.blocks):
                        dve.wait_ge(free[b], f.take(b) + 1)
                        dve.wait_ge(full[3 + b], f.take(3 + b))
                        nc.vector.tensor_tensor(sl[:, b0:b0 + bl], sl[:, b0:b0 + bl], bank[3 + b][:, 0:bl], ALU.mult)\
                            .then_inc(free[3 + b], 1)
                    for b, (b0, bl) in enumerate(q.blocks):
                        dve.wait_ge(v["h_hi"], count + b + 1)
                        nc.vector.tensor_tensor(hid[:, 1, hc, b0:b0 + bl], sl[:, b0:b0 + bl], hid[:, 0, hc, b0:b0 + bl],
                                                ALU.subtract).then_inc(v["h_lo"], 1)

                def down(f, low_too):
                    for k in range(KC * nb):
                        c, (b0, bl) = k // nb, q.blocks[k % nb]
                        no = f.take(6 + k % 2)
                        dve.wait_ge(full[6 + k % 2], no)
                        x = X[:, c, b0:b0 + bl]
                        nc.vector.tensor_tensor(x, x, bank[6 + k % 2][:, 0:bl], ALU.add).then_inc(free[6 + k % 2], 1)
                        if low_too and k:
                            final_low(k - 1)
                    if low_too:
                        final_low(KC * nb - 1)

                def final_low(k):
                    c, (b0, bl) = k // nb, q.blocks[k % nb]
                    dve.wait_ge(v["x3_hi"], k + 1)
                    nc.vector.tensor_tensor(AL[:, c, b0:b0 + bl], X[:, c, b0:b0 + bl], AH[:, c, b0:b0 + bl],
                                            ALU.subtract).then_inc(v["x3_lo"], 1)

                ffn_uses = {b: 4 for b in range(nb)}
                ffn_uses.update({3 + b: 4 for b in range(nb)})
                ffn_uses.update({6: 4 * nb, 7: 4 * nb})
                with dve.Fori(0, 4) as g:
                    f = Fills(banks, g, ffn_uses)
                    for c in range(GROUP):
                        up_chunk(f, c, nb * (c + GROUP * g))
                    down(f, False)
                banks.skip(ffn_uses, 4)
                count = 16 * nb
                for size in (4, 2):
                    if size == 2:
                        for b0, bl in q.blocks:
                            dve.wait_ge(free[6], banks.take(6) + 1)
                            own.link(nc.vector.reciprocal(ss[:, b0:b0 + bl], ss[:, b0:b0 + bl]))
                    for c in range(size):
                        up_chunk(banks, c, count)
                        count += nb
                        if size == 2:
                            for e in range(4 * c, 4 * c + 4):
                                nc.vector.scalar_tensor_tensor(U[:, e, 0:T], U[:, e, 0:T], gple[:, e:e + 1], ss[:, 0:T],
                                                               ALU.mult, ALU.mult).then_inc(v["e_done"], 1)
                    down(banks, size == 2)

                dve.wait_ge(v["e_done"], KC)
                with dve.Fori(0, 4) as i:
                    f = Fills(banks, i, uses)
                    own.loop(i, 2 * nb)
                    k = 0
                    for p in range(2):
                        for b0, bl in q.blocks:
                            dve.wait_ge(free[k % 2], f.take(k % 2) + 1)
                            g_ = sl[:, b0:b0 + bl]
                            own.link(nc.vector.tensor_tensor(g_, g_, U[:, 2 * i + p, b0:b0 + bl], ALU.mult))
                            x = X[:, 2 * i + p, b0:b0 + bl]
                            nc.vector.tensor_tensor(x, x, g_, ALU.add).then_inc(v["x4"], 1)
                            k += 1
                own.done(4)
                banks.skip(uses, 4)

                dve.wait_ge(v["x4"], KC * nb + nb)
                for b, (b0, bl) in enumerate(q.blocks):
                    dve.wait_ge(free[6], banks.take(6) + 1)
                    own.link(nc.vector.reciprocal(ss[:, b0:b0 + bl], ss[:, b0:b0 + bl]))
                    for c in range(KC):
                        nc.vector.scalar_tensor_tensor(U[:, c, b0:b0 + bl], X[:, c, b0:b0 + bl], gfin[:, c:c + 1],
                                                       ss[:, b0:b0 + bl], ALU.mult, ALU.mult).then_inc(v["y_t"], 1)
                for t in range(q.tiles):
                    n = P if t < NCH else TS
                    banks.take(2)
                    dve.wait_ge(full[3], banks.take(3))
                    if t >= 2:
                        dve.wait_ge(v[f"y_out{t % 2}"], 16 * (t // 2))
                    nc.vector.tensor_copy(yst[t % 2][0:n, 512:], bank[3][0:n, :]).then_inc(free[3], 1)

        @block.gpsimd
        def _(pool):
            banks = Banks()
            pool.sem_inc(lo_done, 2)
            for v in S:
                for name in ("res_sum", "e_sum", "x4_sum"):
                    pool.sem_inc(v[name], 1)
            made = Chain(pool, pool_own)
            for t, value in ((ident, 0.0), (identb, 0.0), (causal, 0.0), (causal_s, 0.0), (ones, 1.0),
                             (batch_s, 1.0), (state, 0.0), (epst, EPS), (neg_half, -0.5), (hist, 0.0), (carry, 0.0)):
                nc.gpsimd.memset(t[tuple([slice(None)] * len(t.shape))], value)
            made.link(nc.gpsimd.memset(sm[:, :, :], 0.0))

            def select(t, pattern, base, cm, op, fill):
                made.link(nc.gpsimd.affine_select(out=t, in_=t, compare_op=op, fill=fill, base=base, pattern=pattern,
                                                  channel_multiplier=cm))

            for t in (ident, identb):
                select(t[:, :], [[-1, P]], 0, 1, ALU.not_equal, 1.0)
            select(causal[:, :], [[1, P]], 0, -1, ALU.is_ge, NEG)
            select(causal_s[:, :, :], [[NT_S, NB_S], [1, NT_S]], 0, -1, ALU.is_ge, NEG)
            select(causal_s[:, :, :], [[-NT_S, NB_S], [0, NT_S]], 0, 1, ALU.is_ge, NEG)
            select(batch_s[:, :], [[-NT_S, NB_S]], 0, 1, ALU.is_ge, 0.0)
            select(batch_s[:, :], [[NT_S, NB_S]], NT_S - 1, -1, ALU.is_ge, 0.0)
            pool.sem_inc(consts_made, 1)

            def next_low(s, i=0, step=0):
                p = s % 2
                pool.wait_ge(hi_done, s + 3 + step * i)
                nc.gpsimd.tensor_tensor(wlo[p][:, :], wraw[p][:, :], whi[p][:, :], ALU.subtract).then_inc(lo_done, 1)

            def clear_sums(v, q, name):
                nc.gpsimd.memset(ss[:, 0:q.T], 0.0).then_inc(v[name], 1)

            def add_square(v, q, name, squares, k, b, turn=0):
                b0, bl = q.blocks[b]
                pool.wait_ge(v[squares], k + 1 + turn)
                pool.wait_ge(v[name], k + 2 + turn)
                nc.gpsimd.tensor_tensor(ss[:, b0:b0 + bl], ss[:, b0:b0 + bl], tmp[k % 2][:, 0:bl], ALU.add)\
                    .then_inc(v[name], 1)

            next_low(0)
            for q in supers:
                v, s0, nb = S[q.n], q.slab0, q.nb
                uses = {0: nb, 1: nb}
                banks.skip({2: 1, 3: 1}, q.tiles)
                banks.skip({6: nb})
                with pool.Fori(0, 4) as i:
                    for p in range(2):
                        next_low(s0 + p + 1, i, 2)
                next_low(s0 + 9)
                banks.skip(uses, 4)
                for b in range(nb):
                    banks.take(b % 2)
                lf, columns, pairs, over_chunk = prep_fills(banks, q)
                n0 = list(banks.n)

                pool.wait_ge(full[4], over_chunk)
                for t in (qz[:, :, :], qwz[:, :, :], rz[:, :]):
                    nc.gpsimd.memset(t, 0.0).then_inc(v["stage_clear"], 1)
                nc.gpsimd.memset(V[:, :, DV:], 1.0).then_inc(v["stage_clear"], 1)
                pool.wait_ge(v["stage_clear"], 4)
                was_read(pool, banks, 4, 5, 6, 7)

                def stage_scores(c, tok, n=P):
                    pool.wait_ge(full[7], ChunkFills(n0, c).values - 2)
                    made.link(nc.gpsimd.tensor_copy(kst[:, :, 0:n], X[:, 2:4, tok]))
                    for half in range(2):
                        r = slice(half * DK, (half + 1) * DK)
                        made.link(nc.gpsimd.tensor_copy(qz[r, half:NH:2, 0:n], X[r, 0:2, tok]))
                    made.link(nc.gpsimd.tensor_copy(vst[:, :, 0:n], X[:, 4:8, tok]))
                    made.link(nc.gpsimd.tensor_copy(rz[0:NH, 0:n], R1[0:NH, tok]))

                def stage_outputs(c, p, tok, n=P):
                    pool.wait_ge(full[6], ChunkFills(n0, c).state - 1)
                    for half in range(2):
                        r = slice(half * DK, (half + 1) * DK)
                        made.link(nc.gpsimd.tensor_copy(qwz[r, half:NH:2, 0:n], qw[r, :, tok]))
                    made.link(nc.gpsimd.tensor_copy(colst[p][0:n, 0:12].rearrange("p (r h) -> p r h", r=3), cols[0:n, :, c, :]))
                    nc.gpsimd.tensor_copy(colst[p][:, 12:14], decay[:, :, c if n == P else 0]).then_inc(v["staged"], 1)

                def root(c, n=P):
                    pool.wait_ge(v["root_in"], c + 1)
                    nc.gpsimd.tensor_tensor(rr[0:n, :], tt[0:n, :], neg_half[0:n, :], ALU.pow).then_inc(v["root_done"], 1)

                def chunk(i, m, stage_next=True):
                    c = 2 * i + m
                    next_low(s0 + 10 + 2 * m, i, 4)
                    if stage_next:
                        stage_scores(c + 1, ds((c + 1) * P, P))
                        stage_outputs(c + 1, 1 - m, ds((c + 1) * P, P))
                    next_low(s0 + 11 + 2 * m, i, 4)
                    root(c)

                stage_scores(0, slice(0, P))
                stage_outputs(0, 0, slice(0, P))
                with pool.Fori(0, 3) as i:
                    made.loop(i, 2 * 8)
                    chunk(i, 0)
                    chunk(i, 1)
                made.done(3)
                chunk(3, 0)
                chunk(3, 1, stage_next=False)
                banks.skip({0: 2 * nb, 1: 2 * nb}, 4)
                banks.skip(CHUNK_USES, NCH)
                if q.sample:
                    stage_scores(NCH, slice(TP, TM), TS)
                    stage_outputs(NCH, 0, slice(TP, TM), TS)
                    made.link(nc.gpsimd.memset(batch_t[:, :, :], 1.0))
                    select(batch_t[:, :, :], [[-NT_S, NB_S], [1, TS]], 0, 0, ALU.is_ge, 0.0)
                    select(batch_t[:, :, :], [[NT_S, NB_S], [-1, TS]], NT_S - 1, 0, ALU.is_ge, 0.0)
                    was_read(pool, banks, 0, 1)
                    pool.wait_ge(v["staged"], NCH + 1)
                    for h in range(NH):
                        nc.gpsimd.tensor_tensor(qb[:, h, :, :], qwz[:, h, 0:TS].unsqueeze(1).to_broadcast([P, NB_S, TS]),
                                                batch_t[:, :, :], ALU.mult).then_inc(batch_queries, 1)
                    root(NCH, TS)
                    banks.skip(CHUNK_USES)
                    banks.skip({2: 2, 3: 2, 6: 1})

                was_filled(pool, banks, 2, 3, 4, 5, 6, 7)
                was_read(pool, banks, 7)
                clear_sums(v, q, "res_sum")
                s = s0 + 25
                with pool.Fori(0, 4) as i:
                    for p in range(2):
                        next_low(s + p + 1, i, 2)
                        for b in range(nb):
                            add_square(v, q, "res_sum", "res_sq", p * nb + b, b, 2 * nb * i)
                s += 8
                for p in range(2):
                    next_low(s + 1)
                    s += 1
                pool.wait_ge(v["low2"], KC * nb)
                clear_sums(v, q, "e_sum")
                with pool.Fori(0, 4) as g:
                    for n in range(12):
                        next_low(s + n + 1, g, 12)
                        if n >= 10:
                            for b in range(nb):
                                add_square(v, q, "e_sum", "e_sq", (n - 10) * nb + b, b, 2 * nb * g)
                s += 48
                for n in range(18):
                    next_low(s + 1)
                    s += 1
                pool.wait_ge(v["e_done"], KC)
                clear_sums(v, q, "x4_sum")
                turns = 4 - q.sample
                with pool.Fori(0, turns) as i:
                    for p in range(2):
                        next_low(s + p + 1, i, 2)
                        for b in range(nb):
                            add_square(v, q, "x4_sum", "x4_sq", p * nb + b, b, 2 * nb * i)
                if q.sample:
                    for p in range(2):
                        if p == 0:
                            next_low(s + 7)
                        for b in range(nb):
                            add_square(v, q, "x4_sum", "x4_sq", 6 * nb + p * nb + b, b)
                for g in range(4):
                    banks.take(2 + g)
                if q.sample:
                    banks.take(6)
                banks.skip({0: 12 * nb, 1: 12 * nb, 6: 3 * nb})
                for b in range(nb):
                    banks.skip({b: FF, 3 + b: FF})
                banks.skip({6: 24 * nb, 7: 24 * nb})
                banks.skip({2: 1, 3: 1}, q.tiles)


INS = ["x_prompt", "x_sample", "p_prompt", "p_sample", "state_C", "state_n", "state_m", "state_conv", "g_mix", "w_in",
       "b_ig", "b_fg", "g_mh", "conv_w", "w_out", "g_ffn", "w_gate", "w_up", "w_down", "w_ple", "g_ple", "w_pg", "g_final"]
OUTS = [("y_prompt", (1, 2 * TP, D)), ("y_sample", (NB_S, NT_S, D)), ("C_prompt", (1, 1, NH, DK, DV)),
        ("n_prompt", (1, 1, NH, DK)), ("m_prompt", (1, 1, NH)), ("conv_prompt", (1, 1, 2, 512)),
        ("C_sample", (1, NB_S, NH, DK, DV)), ("n_sample", (1, NB_S, NH, DK)), ("m_sample", (1, NB_S, NH)),
        ("conv_sample", (1, NB_S, 2, 512))]


def kernel(**inputs):
    import numpy as np
    import concourse.bacc as bacc
    from concourse.bass_utils import run_bass_kernel_spmd

    nc = bacc.Bacc("TRN2", target_bir_lowering=False, num_devices=1)
    arrays, args = {}, []
    for name in INS:
        a = np.ascontiguousarray(inputs[name])
        arrays[name] = a
        args.append(nc.dram_tensor(name, a.shape, F32, kind="ExternalInput").ap())
    for name, shape in OUTS:
        args.append(nc.dram_tensor(name, shape, F32, kind="ExternalOutput").ap())
    build(nc, *args)
    got = run_bass_kernel_spmd(nc, [arrays], core_ids=[0]).results[0]
    return tuple(got[name] for name, _ in OUTS)
```

```python
from contextlib import ExitStack, nullcontext

import concourse.bass as bass
from concourse import mybir

ALU = mybir.AluOpType
ACT = mybir.ActivationFunctionType
F32 = mybir.dt.float32
F32R = mybir.dt.float32r
BF16 = mybir.dt.bfloat16
ds = bass.ds

P = 128
D = 1024
KC = D // P
NH, DK, DV = 4, 64, 128
PAIRS = NH // 2
DFF = 2816
FF = DFF // P
PLE = 256
GATE_CAP = 15.0
EPS = 1e-6
NB_S, NT_S = 8, 4
TS = NB_S * NT_S
TP = 1024
TM = TP + TS
NCH = TP // P
QSCALE = DK ** -0.5
NEG = -1e30
GROUP = 4
SLAB = 1024
SLABS = 8 + 1 + 16 + 8 + 2 + (5 * 12 + 6) + 8
COL_G, COL_O = 2 * NH * DK + NH * DV, 2 * NH * DK + NH * DV + 2 * NH
COL_B = COL_O + NH * DV
COL_C = COL_B + 512
COL_H = COL_C + 512
N_CONSTS = 2 + 4 + 3 + 1 + 8


class Super:

    def __init__(self, n):
        self.n = n
        self.sample = n == 1
        self.T = TM if self.sample else TP
        self.nb = 3 if self.sample else 2
        size = self.T // self.nb
        self.blocks = [(b * size, size) for b in range(self.nb)]
        self.tiles = NCH + self.sample
        self.slab0 = n * SLABS


class Banks:

    def __init__(self):
        self.n = [0] * 8

    def take(self, b):
        self.n[b] += 1
        return self.n[b]

    def skip(self, uses, times=1):
        for b, m in uses.items():
            self.n[b] += m * times


class Fills:

    def __init__(self, banks, i, uses):
        self.base, self.i, self.uses, self.k = list(banks.n), i, uses, {b: 0 for b in uses}

    def take(self, b):
        self.k[b] += 1
        return self.base[b] + self.k[b] + self.i * self.uses[b]


class Chain:

    def __init__(self, eng, sem):
        self.eng, self.sem, self.n, self.i, self.per, self.start = eng, sem, 0, 0, 0, 0

    def loop(self, i, per):
        self.i, self.per, self.start = i, per, self.n

    def done(self, times):
        assert self.n - self.start == self.per, (self.n - self.start, self.per)
        self.n, self.i, self.per = self.start + self.per * times, 0, 0

    def link(self, ins):
        self.n += 1
        ins.then_inc(self.sem, 1)
        self.eng.wait_ge(self.sem, self.n + self.i * self.per)


def build(nc, x_prompt, x_sample, p_prompt, p_sample, state_C, state_n, state_m, state_conv, g_mix, w_in,
          b_ig, b_fg, g_mh, conv_w, w_out, g_ffn, w_gate, w_up, w_down, w_ple, g_ple, w_pg, g_final,
          y_prompt, y_sample, C_prompt, n_prompt, m_prompt, conv_prompt, C_sample, n_sample, m_sample,
          conv_sample):
    supers = [Super(0), Super(1)]
    stored_x = [nc.dram_tensor(f"stored_x{n}", (P, KC, TM), F32, kind="Internal").ap() for n in range(2)]

    SLOT = TM * 4
    origin = (nc.sbuf_base + 31) // 32 * 32

    def at(name, shape, dt, offset):
        return nc.alloc_sbuf_tensor_at(name, shape, dt, offset=offset)

    wide0 = at("wide0", [P, KC, TM], F32, origin)
    AH = at("AH", [P, KC, TM], F32R, origin + 8 * SLOT)
    AL = at("AL", [P, KC, TM], F32R, origin + 16 * SLOT)
    wide1 = at("wide1", [P, KC, TM], F32, origin + 24 * SLOT)
    R0 = origin + 32 * SLOT
    hid = at("hid", [P, 2, GROUP, TM], F32R, R0)
    rows = at("rows", [P, 8, TM], F32, R0)
    next_x = at("next_x", [P, KC, TM], F32, R0)
    xin = [at(f"xin{t}", [P, D], F32, R0 + t * 4096) for t in range(NCH)]
    y_end = [at(f"y_end{p}", [P, D], F32, R0 + p * 4096) for p in range(3)]
    y_squares = at("y_squares", [P, 3, 2, 512], F32, R0 + 3 * 4096)
    for q, x_, u_, home in zip(supers, (wide0, wide1), (wide1, wide0), (wide1, next_x)):
        q.X, q.U, q.home = x_, u_, home
    G, LF, B, M, R1, W, CS, EM = (rows[:, n, :] for n in range(8))
    qw = rows[:, 0:2, :]
    zbuf = at("zbuf", [P, TM + 2], F32, R0 + 2 * SLOT)
    Cs = at("Cs", [P, PAIRS, NB_S, DV + 1], F32, R0 + 2 * SLOT)
    kwb = at("kwb", [TS, NH, NB_S, DK], F32, R0)
    stage0 = R0 + 5 * SLOT
    kst = at("kst", [P, PAIRS, P], F32, stage0)
    qz = at("qz", [P, NH, P], F32, stage0 + 1024)
    qwz = at("qwz", [P, NH, P], F32, stage0 + 3072)
    vst = at("vst", [P, NH, P], F32, stage0 + 5120)
    rz = at("rz", [P, P], F32, stage0 + 7168)
    cv = at("cv", [P, TM], F32, R0 + 7 * SLOT)
    qb = at("qb", [P, NH, NB_S, TS], F32, R0 + 7 * SLOT)
    pst = at("pst", [P, NCH, PLE], F32, R0 + 6 * SLOT)
    pst_s = at("pst_s", [P, PLE], F32, R0 + 2 * SLOT)

    slab_at = R0 + 8 * SLOT
    wraw = [at(f"wraw{p}", [P, SLAB], F32, slab_at + p * 4096) for p in range(2)]
    whi = [at(f"whi{p}", [P, SLAB], F32R, slab_at + (2 + p) * 4096) for p in range(2)]
    wlo = [at(f"wlo{p}", [P, SLAB], F32R, slab_at + (4 + p) * 4096) for p in range(2)]

    cursor = [slab_at + 6 * 4096]

    def keep(name, shape, dt=F32):
        size = 1
        for n in shape[1:]:
            size *= n
        size *= 2 if dt == BF16 else 4
        t = at(name, shape, dt, cursor[0])
        cursor[0] += (size + 31) // 32 * 32
        return t

    ident = keep("ident", [P, P])
    identb = keep("identb", [P, P], BF16)
    causal = keep("causal", [P, P], BF16)
    causal_s = keep("causal_s", [P, NB_S, NT_S], BF16)
    batch_s = keep("batch_s", [P, NB_S])
    state = keep("state", [P, PAIRS, DV + 1])
    ones = keep("ones", [P, 1])
    epst = keep("epst", [P, 1])
    neg_half = keep("neg_half", [P, NCH + 1])
    gmix, gffn, gple, gfin = (keep(n, [P, KC]) for n in ("gmix", "gffn", "gple", "gfin"))
    gmh = keep("gmh", [P, NH])
    cw = keep("cw", [P, 3, 4])
    bias8 = keep("bias8", [2 * NH, 1])
    hist = keep("hist", [P, 4, 2])
    convs = keep("convs", [P, 4, NB_S, 2])
    zs = keep("zs", [P, NB_S, 2 + NT_S])
    carry = keep("carry", [NH, 1])
    mprev = keep("mprev", [NH, NCH + NB_S])
    m_out = keep("m_out", [NH, NB_S])
    ms0 = keep("ms0", [NH, NB_S])
    sI = keep("sI", [NH, NB_S, NT_S])
    sF = keep("sF", [NH, NB_S, NT_S])
    decay = keep("decay", [P, PAIRS, NCH + NB_S])
    cols = keep("cols", [P, 3, NCH + 1, NH])
    colst = [keep(f"colst{p}", [P, 14]) for p in range(2)]
    sm = keep("sm", [P, 5, NH])
    ss4, dm, d2, tt, rr = (sm[:, n, :] for n in range(5))
    sq_tile = keep("sq_tile", [P, 2])
    x_sums = keep("x_sums", [P, NCH + 1])
    x_roots = keep("x_roots", [P, NCH + 1])
    y_sums = keep("y_sums", [P, 3, 2])
    y_roots = keep("y_roots", [P, 3, 2])
    mix0 = cursor[0]
    expE = keep("expE", [P, NH, P])
    Pm = keep("Pm", [P, NH, P])
    V = keep("V", [P, NH, DV + 1])
    kw = keep("kw", [P, NH, DK])
    hn = keep("hn", [P, NH, P])
    batch_t = keep("batch_t", [P, NB_S, TS])
    cursor[0] = mix0
    ss = keep("ss", [P, TM])
    sl = keep("sl", [P, TM])
    tmp = [keep(f"tmp{p}", [P, 512]) for p in range(3)]
    pair_rows = at("pair_rows", [NH, PAIRS, P], F32, cursor[0] - 1024)
    gain_row = at("gain_row", [P, D], F32, mix0)
    xs = [at(f"xs{p}", [P, D], F32, mix0 + p * SLOT) for p in range(2)]
    squares = at("squares", [P, D], F32, mix0 + 2 * SLOT)
    y_stage = at("y_stage", [P, KC, P], F32, mix0 + SLOT)
    y_rows = at("y_rows", [P, D], F32, mix0 + 2 * SLOT)
    assert cursor[0] <= nc.sbuf_usable_end, (cursor[0], nc.sbuf_usable_end)

    def by_k(w):
        return w.rearrange("(k p) n -> p k n", p=P)

    w_in_v, w_out_v, w_gate_v, w_up_v, w_down_v, w_ple_v, w_pg_v = (
        by_k(w[0]) for w in (w_in, w_out, w_gate, w_up, w_down, w_ple, w_pg))

    with ExitStack() as ctx:
        bank = [ctx.enter_context(nc.psum_tensor(f"bank{b}", [P, 512], F32)) for b in range(8)]

        def sem(name):
            return ctx.enter_context(nc.semaphore(name))

        gmix_in = sem("gmix_in")
        consts_in = sem("consts_in")
        consts_made = sem("consts_made")
        landed = [sem("landed_even"), sem("landed_odd")]
        hi_done, lo_done = sem("hi_done"), sem("lo_done")
        slab_begun = sem("slab_begun")
        full = [sem(f"full{b}") for b in range(8)]
        free = [sem(f"free{b}") for b in range(8)]
        dve_own, pool_own = sem("dve_own"), sem("pool_own")
        names = ["x_landed0", "x_landed1", "x_sq", "x_kept", "x_root", "x_stored", "x_back", "normed", "high", "low",
                 "softcap", "lf_abs", "lf_soft", "rows_made", "rows_exp", "stage_clear", "staged", "conv_done",
                 "sq_done", "root_in", "root_done", "sig_o", "merged", "mix_hi", "mix_lo", "reload", "p_landed",
                 "p_hi", "res_sq", "res_sum", "normed2", "high2", "low2", "e_sq", "e_sum", "e_done",
                 "h_hi", "h_lo", "x3_hi", "x3_lo", "x4", "gain_in", "y_staged", "y_sq", "y_root", "y_gained",
                 "y_out0", "y_out1", "y_out2"]
        S = [{n: sem(f"{n}_{q}") for n in names} for q in range(2)]
        x_in = [sem(f"x_in{t}") for t in range(NCH)]
        states_in, batch_queries, batch_keys = sem("states_in"), sem("batch_queries"), sem("batch_keys")
        small_out = sem("small_out")
        ctx.enter_context(nc.allow_non_contiguous_dma(reason="gains, biases and small states"))
        block = ctx.enter_context(nc.Block())

        def was_filled(eng, banks, *bks):
            for b in bks:
                eng.wait_ge(full[b], banks.n[b])

        def was_read(eng, banks, *bks):
            for b in bks:
                eng.wait_ge(free[b], banks.n[b] + 1)

        class ChunkFills:

            def __init__(self, banks, c):
                n = banks
                self.exponent, self.score = n[2] + c + 1, n[3] + c + 1
                self.keys, self.out01 = n[4] + 2 * c + 1, n[4] + 2 * c + 2
                self.out23, self.state = n[5] + c + 1, n[6] + c + 1
                self.values, self.h_t = n[7] + 2 * c + 1, n[7] + 2 * c + 2

        CHUNK_USES = {2: 1, 3: 1, 4: 2, 5: 1, 6: 1, 7: 2}

        TILE_USES = {2: 1, 3: 1}
        PARTS = ((0, 2), (2, 3), (3, 4))

        def turns(eng, first, last):
            return eng.Fori(first, last) if last - first > 1 else nullcontext(first)

        def qkv_uses(q):
            return {0: q.nb, 1: q.nb, 2: 2, 3: 2}

        def lf_fills(banks, q):
            return [banks.take(2 + b) for b in range(q.nb)]

        def prep_fills(banks, q):
            columns = banks.take(5)
            pairs = [(6 + k % 2, banks.take(6 + k % 2)) for k in range(PAIRS * q.nb)]
            return columns, pairs, banks.take(4)

        def qkv_skip(banks, q):
            for b in range(q.nb):
                banks.take(b % 2)
            lf_fills(banks, q)
            prep_fills(banks, q)
            banks.skip(qkv_uses(q), 4)
            if q.n == 0:
                banks.skip(TILE_USES)

        N_SMALL = 4 + 4 + 8 + 2 * PAIRS

        def small_outputs(sp):
            def out(dst, src):
                sp.dma_start(dst, src).then_inc(small_out, 16)

            out(C_prompt[0, 0].rearrange("(j hh) d e -> (hh d) j e", hh=2), state[:, :, 0:DV])
            out(n_prompt[0, 0].rearrange("(j hh) d -> (hh d) j", hh=2), state[:, :, DV])
            out(m_prompt[0, 0].rearrange("(h a) -> h a", a=1), carry[:, :])
            out(m_sample[0].rearrange("b h -> h b"), m_out[:, :])
            for c in range(4):
                out(conv_prompt[0, 0, :, c * P:(c + 1) * P].rearrange("w p -> p w"), hist[:, c, :])
                for w in range(2):
                    out(conv_sample[0, :, w, c * P:(c + 1) * P].rearrange("b p -> p b"), convs[:, c, :, w])
            for j in range(PAIRS):
                out(C_sample[0, :, 2 * j:2 * j + 2].rearrange("b hh d e -> (hh d) b e"), Cs[:, j, :, 0:DV])
                out(n_sample[0, :, 2 * j:2 * j + 2].rearrange("b hh d -> (hh d) b"), Cs[:, j, :, DV])

        @block.sync
        def _(sp):
            banks = Banks()
            def constants():
                sp.dma_start(bias8[0:NH, :], b_ig.rearrange("a h -> h a")).then_inc(consts_in, 16)
                sp.dma_start(bias8[NH:2 * NH, :], b_fg.rearrange("a h -> h a")).then_inc(consts_in, 16)
                for t, g in ((gffn, g_ffn[0]), (gple, g_ple[0]), (gfin, g_final), (gmh, g_mh[0])):
                    sp.dma_start(t[:, :], g.rearrange("(c p) -> p c", p=P)).then_inc(consts_in, 16)
                for w in range(3):
                    sp.dma_start(cw[:, w, :], conv_w[0, w].rearrange("(c p) -> p c", p=P)).then_inc(consts_in, 16)
                sp.dma_start(ms0[:, :], state_m[0].rearrange("b h -> h b")).then_inc(consts_in, 16)
                for c in range(4):
                    for w in range(2):
                        sp.dma_start(convs[:, c, :, w], state_conv[0, :, w, c * P:(c + 1) * P].rearrange("b p -> p b"))\
                            .then_inc(consts_in, 16)

            def slab(s, p, src):
                sp.wait_ge(hi_done, s + 1)
                sp.wait_ge(lo_done, s + 1)
                sp.dma_start(wraw[p][:, :].rearrange("p (k n) -> p k n", k=src.shape[1]), src).then_inc(landed[p], 16)

            def first_slabs(q):
                for s, c0 in ((q.slab0, COL_G), (q.slab0 + 1, 0)):
                    slab(s, s % 2, w_in_v[:, :, c0:c0 + P])

            for t in range(NCH):
                sp.dma_start(xin[t][:, :], x_prompt[0, t * P:(t + 1) * P, :]).then_inc(x_in[t], 16)
                if t == 1:
                    first_slabs(supers[0])
                    sp.dma_start(gmix[:, :], g_mix[0].rearrange("(c p) -> p c", p=P)).then_inc(gmix_in, 16)
            constants()
            for q in supers:
                X, v, s0 = q.X, S[q.n], q.slab0
                par = s0 % 2
                if q.n == 0:
                    banks.skip(TILE_USES, NCH)
                    was_read(sp, banks, 2, 3)
                    sp.dma_start(stored_x[0][:, :, 0:q.T], q.home[:, :, 0:q.T]).then_inc(v["x_stored"], 16)
                    for p in range(2):
                        sp.dma_start(xs[p][:, :], x_prompt[0, TP + p * P:TP + (p + 1) * P, :])\
                            .then_inc(S[1][f"x_landed{p}"], 16)
                    banks.skip({5 + b: 1 for b in range(q.nb)})
                slab(s0 + 2, par, w_in_v[:, :, P:2 * P])
                tile0 = banks.n[3] + 1

                with sp.Fori(0, 3) as i:
                    for p in range(2):
                        if q.n == 0:
                            src = x_prompt[0, ds(i * 2 * P + (TP + (2 + p) * P), P), :]
                            sp.wait_ge(free[3], tile0 + 2 * i + p + 2)
                            sp.dma_start(xs[p][:, :], src)\
                                .then_inc(S[1][f"x_landed{p}"], 16)
                        slab(s0 + 3 + p + 2 * i, (par + 3 + p) % 2, w_in_v[:, :, ds(i * 2 * P + (2 + p) * P, P)])
                        if q.n:
                            dst = y_prompt[0, ds(i * 2 * P + p * P, P), :]
                            sp.wait_ge(S[0]["y_gained"], 2 * i + p + 1)
                            sp.dma_start(dst, y_rows[:, :]).then_inc(S[0]["y_out0"], 16)
                if q.n == 0:
                    sp.wait_ge(free[3], tile0 + NCH)
                    sp.dma_start(xs[0][0:TS, :], x_sample.rearrange("b s d -> (b s) d")).then_inc(S[1]["x_landed0"], 16)
                else:
                    for t in (NCH - 2, NCH - 1):
                        sp.wait_ge(S[0]["y_gained"], t + 1)
                        sp.dma_start(y_prompt[0, t * P:(t + 1) * P, :], y_rows[:, :]).then_inc(S[0]["y_out0"], 16)
                qkv_skip(banks, q)
                chunk0 = list(banks.n)
                with sp.Fori(0, 4) as i:
                    for n, col in enumerate((COL_O, COL_C, COL_H, COL_B)):
                        slab(s0 + 9 + n + 4 * i, (par + 9 + n) % 2, w_in_v[:, :, ds(i * P + col, P)])
                banks.skip({0: 8 * q.nb, 1: 8 * q.nb})
                banks.skip(CHUNK_USES, NCH)
                s = s0 + 25
                for p in range(2):
                    slab(s + p, (s + p) % 2, w_out_v[:, :, p * P:(p + 1) * P])
                if q.sample:
                    sp.wait_ge(v["conv_done"], 5)
                    for j in range(PAIRS):
                        sp.dma_start(Cs[:, j, :, 0:DV],
                                     state_C[0, :, 2 * j:2 * j + 2].rearrange("b hh d e -> (hh d) b e")).then_inc(states_in, 16)
                        sp.dma_start(Cs[:, j, :, DV],
                                     state_n[0, :, 2 * j:2 * j + 2].rearrange("b hh d -> (hh d) b")).then_inc(states_in, 16)
                    banks.skip(CHUNK_USES)
                    banks.skip({2: 2, 3: 2, 6: 1})
                was_read(sp, banks, 0, 1, 2, 3, 6, 7)
                sp.wait_ge(v["staged"], q.tiles)
                sp.wait_ge(v["x_stored"], 16 * (1 if q.n == 0 else q.tiles))
                sp.dma_start(X[:, 0:4, 0:q.T], stored_x[q.n][:, 0:4, 0:q.T]).then_inc(v["reload"], 16)
                if q.sample:
                    small_outputs(sp)
                    sp.wait_ge(small_out, 16 * N_SMALL)
                sp.dma_start(pst[:, :, :], p_prompt[0, 0, q.n * TP:(q.n + 1) * TP, :].rearrange("(t p) n -> p t n", p=P))\
                    .then_inc(v["p_landed"], 16)
                if q.sample:
                    sp.dma_start(pst_s[0:TS, :], p_sample[0].rearrange("b s n -> (b s) n")).then_inc(v["p_landed"], 16)
                sp.wait_ge(v["merged"], 4)
                sp.dma_start(X[:, 4:8, 0:q.T], stored_x[q.n][:, 4:8, 0:q.T]).then_inc(v["reload"], 16)
                with sp.Fori(1, 4) as i:
                    for p in range(2):
                        slab(s + p + 2 * i, (s + p) % 2, w_out_v[:, :, ds(i * 2 * P + p * P, P)])
                s += 8
                for p in range(2):
                    slab(s + p, (s + p) % 2, w_ple_v[:, :, p * 512:(p + 1) * 512])
                s += 2
                with sp.Fori(0, 4) as g:
                    for c in range(GROUP):
                        for p, w in enumerate((w_gate_v, w_up_v)):
                            slab(s + 2 * c + p + 12 * g, (s + p) % 2, w[:, :, ds(g * GROUP * P + c * P, P)])
                    for n in range(4):
                        slab(s + 8 + n + 12 * g, (s + n) % 2, w_down_v[:, ds(g * GROUP, GROUP), n * 256:(n + 1) * 256])
                s += 48
                for g, size in ((4, 4), (5, 2)):
                    for c in range(size):
                        ff = g * GROUP + c
                        for w in (w_gate_v, w_up_v):
                            slab(s, s % 2, w[:, :, ff * P:(ff + 1) * P])
                            s += 1
                    nw = SLAB // size
                    for n in range(D // nw):
                        slab(s, s % 2, w_down_v[:, g * GROUP:g * GROUP + size, n * nw:(n + 1) * nw])
                        s += 1
                for p in range(2):
                    slab(s + p, (s + p) % 2, w_pg_v[:, :, p * P:(p + 1) * P])
                for g in range(4):
                    banks.take(2 + g)
                if q.sample:
                    banks.take(6)
                banks.skip({0: 4 * q.nb, 1: 4 * q.nb, 6: q.nb})
                banks.skip({0: 4 * q.nb, 1: 4 * q.nb})
                for b in range(q.nb):
                    banks.skip({b: FF, 3 + b: FF})
                banks.skip({6: 6 * 4 * q.nb + q.nb, 7: 6 * 4 * q.nb})
                sp.wait_ge(v["e_done"], KC)
                sp.dma_start(gain_row[:, :], g_final.rearrange("(a d) -> a d", a=1).to_broadcast([P, D])).then_inc(v["gain_in"], 16)
                if q.n == 0:
                    was_filled(sp, banks, 6, 7)
                    sp.wait_ge(S[1]["x_stored"], 16 * supers[1].tiles)
                    sp.dma_start(next_x[:, :, :], stored_x[1][:, :, :]).then_inc(S[1]["x_back"], 16)
                with sp.Fori(1, 4) as i:
                    for p in range(2):
                        slab(s + p + 2 * i, (s + p) % 2, w_pg_v[:, :, ds(i * 2 * P + p * P, P)])
                if q.n == 0:
                    banks.skip({5 + b: 1 for b in range(supers[1].nb)})
                banks.skip({0: 4 * q.nb, 1: 4 * q.nb})
                if q.n == 0:
                    first_slabs(supers[1])
            for t in range(q.tiles):
                for bk in (2 + 2 * (t % 3), 3 + 2 * (t % 3)):
                    sp.wait_ge(free[bk], banks.take(bk) + 1)
                if t < NCH:
                    dst, n = y_prompt[0, TP + t * P:TP + (t + 1) * P, :], P
                else:
                    dst, n = y_sample.rearrange("b s d -> (b s) d"), TS
                sp.dma_start(dst, y_end[t % 3][0:n, :]).then_inc(v[f"y_out{t % 3}"], 16)
            for p in range(3):
                sp.wait_ge(v[f"y_out{p}"], 16 * 3)

        @block.tensor
        def _(pe):
            banks = Banks()

            pe.sem_inc(slab_begun, 1)
            pe.wait_ge(consts_made, 1)

            def product(q, no, bk, p, kc, n, b, src=(AH, AL), begins=False, ready=None):
                b0, bl = q.blocks[b]
                pe.wait_ge(free[bk], no)
                hi = whi[p][:, :].rearrange("p (k n) -> p k n", k=kc)
                lo = wlo[p][:, :].rearrange("p (k n) -> p k n", k=kc)
                o, cols_ = bank[bk][:, 0:bl], slice(n * P, (n + 1) * P)
                for k in range(kc):
                    mh, ml = src[0][:, k, b0:b0 + bl], src[1][:, k, b0:b0 + bl]
                    if ready:
                        ready(b, k)
                    first = nc.tensor.matmul(o, hi[:, k, cols_], mh, start=k == 0, stop=False)
                    if begins and k == 0:
                        first.then_inc(slab_begun, 1)
                    nc.tensor.matmul(o, hi[:, k, cols_], ml, start=False, stop=False)
                    last = nc.tensor.matmul(o, lo[:, k, cols_], mh, start=False, stop=k == kc - 1)
                last.then_inc(full[bk], 1)

            def slab_ready(s):
                pe.wait_ge(lo_done, s + 3)

            def sum_over_features(q, bk=6):
                for b0, bl in q.blocks:
                    pe.wait_ge(free[bk], banks.take(bk))
                    nc.tensor.matmul(bank[bk][:, 0:bl], ones[:, 0:1].to_broadcast([P, P]), ss[:, b0:b0 + bl],
                                     start=True, stop=True).then_inc(full[bk], 1)

            def chunk_scores(v, n0, c, n=P):
                f = ChunkFills(n0, c)
                mask = causal[:, :] if n == P else causal_s[:, :, :].rearrange("p b t -> p (b t)")
                pe.wait_ge(v["staged"], c + 1)
                pe.wait_ge(free[2], f.exponent)
                for h in range(NH):
                    e = bank[2][0:n, h * n:(h + 1) * n]
                    nc.tensor.matmul(e, identb[:, 0:n], mask, start=True, stop=False)
                    last = nc.tensor.matmul(e, ident[:, h:h + 1].to_broadcast([P, n]), rz[:, 0:n], start=False, stop=True)
                last.then_inc(full[2], 1)
                pe.wait_ge(free[3], f.score)
                for h in range(NH):
                    last = nc.tensor.matmul(bank[3][0:n, h * n:(h + 1) * n], kst[:, h // 2, 0:n], qz[:, h, 0:n],
                                            start=True, stop=True)
                last.then_inc(full[3], 1)
                pe.wait_ge(free[4], f.keys)
                for j in range(PAIRS):
                    last = nc.tensor.transpose(bank[4][0:n, j * P:(j + 1) * P], kst[:, j, 0:n], ident[:, :])
                last.then_inc(full[4], 1)
                pe.wait_ge(free[7], f.values)
                for h in range(NH):
                    last = nc.tensor.transpose(bank[7][0:n, h * P:(h + 1) * P], vst[:, h, 0:n], ident[:, :])
                last.then_inc(full[7], 1)

            def chunk_outputs(v, n0, c):
                f = ChunkFills(n0, c)
                pe.wait_ge(free[3], f.score + 1)
                pe.wait_ge(free[7], f.values + 1)
                pe.wait_ge(free[6], f.state)
                for bk, no, hs in ((4, f.out01, (0, 1)), (5, f.out23, (2, 3))):
                    pe.wait_ge(free[bk], no)
                    for h in hs:
                        o = bank[bk][:, (h % 2) * (DV + 1):(h % 2 + 1) * (DV + 1)]
                        nc.tensor.matmul(o, Pm[:, h, :], V[:, h, :], start=True, stop=False)
                        last = nc.tensor.matmul(o, qwz[:, h, :], state[:, h // 2, :], start=False, stop=True)
                    last.then_inc(full[bk], 1)
                for h in range(NH):
                    r, j = DK * (h % 2), h // 2
                    last = nc.tensor.matmul(bank[6][r:r + DK, j * (DV + 1):(j + 1) * (DV + 1)], kw[:, h, :], V[:, h, :],
                                            start=True, stop=True)
                last.then_inc(full[6], 1)

            def chunk_transposes(v, n0, c, n=P):
                f = ChunkFills(n0, c)
                pe.wait_ge(free[4], f.out01 + 1)
                pe.wait_ge(free[5], f.out23 + 1)
                pe.wait_ge(free[7], f.h_t)
                for h in range(NH):
                    last = nc.tensor.transpose(bank[7][:, h * n:(h + 1) * n], hn[0:n, h, :], ident[0:n, 0:n])
                last.then_inc(full[7], 1)

            def linear(q, s, uses, ready, middle=None):
                for first, last in ((0, 2), (2, 4)) if middle else ((0, 4),):
                    with pe.Fori(first, last) as i:
                        f = Fills(banks, i, uses)
                        k = 0
                        for p in range(2):
                            slab_ready(s + p + 2 * i)
                            for b in range(q.nb):
                                product(q, f.take(k % 2), k % 2, (s + p) % 2, KC, 0, b, begins=b == 0,
                                        ready=ready if p == 0 and first == 0 else None)
                                k += 1
                    if middle and last == 2:
                        middle()
                banks.skip(uses, 4)

            def to_features(f, src, n=P):
                for bk in (2, 3):
                    pe.wait_ge(free[bk], f.take(bk))
                    for c in range(4):
                        cc = (bk - 2) * 4 + c
                        last = nc.tensor.transpose(bank[bk][:, c * n:(c + 1) * n], src[0:n, cc * P:(cc + 1) * P],
                                                   ident[0:n, 0:n])
                    last.then_inc(full[bk], 1)

            def to_tokens(f, src, t, bk0, n=P):
                for m in range(2):
                    pe.wait_ge(free[bk0 + m], f.take(bk0 + m))
                    for c in range(4):
                        last = nc.tensor.transpose(bank[bk0 + m][0:n, c * P:(c + 1) * P],
                                                   src[:, m * 4 + c, t * P:t * P + n], ident[:, :])
                    last.then_inc(full[bk0 + m], 1)

            def spread_roots(q, b, no):
                b0, bl = q.blocks[b]
                pe.wait_ge(free[5 + b], no)
                for t in range(b0 // P, (b0 + bl - 1) // P + 1):
                    a, z = max(b0, t * P), min(b0 + bl, (t + 1) * P)
                    n = P if t < NCH else TS
                    last = nc.tensor.matmul(bank[5 + b][:, a - b0:z - b0], x_roots[0:n, t:t + 1].to_broadcast([n, P]),
                                            ident[0:n, a - t * P:z - t * P], start=True, stop=True)
                last.then_inc(full[5 + b], 1)

            for q in supers:
                X, U, v, s0, nb = q.X, q.U, S[q.n], q.slab0, q.nb
                par = s0 % 2
                uses = {0: nb, 1: nb}

                if q.n == 0:
                    for t in range(NCH):
                        pe.wait_ge(x_in[t], 16)
                        to_features(banks, xin[t])
                        if t % 4 == 3:
                            pe.wait_ge(v["x_root"], t // 4 + 1)
                            spread_roots(q, t // 4, banks.take(5 + t // 4))

                slab_ready(s0)
                for b in range(nb):
                    product(q, banks.take(b % 2), b % 2, par, KC, 0, b, begins=b == 0,
                            ready=lambda b, k: pe.wait_ge(v["low"], KC * b + k + 1))
                was_read(pe, banks, 0, 1)
                for b, no in enumerate(lf_fills(banks, q)):
                    b0, bl = q.blocks[b]
                    pe.wait_ge(free[2 + b], no)
                    nc.tensor.matmul(bank[2 + b][0:NH, 0:bl], ident[0:2 * NH, NH:2 * NH], G[0:2 * NH, b0:b0 + bl],
                                     start=True, stop=True).then_inc(full[2 + b], 1)

                def gate_rows():
                    columns, pairs, over_chunk = prep_fills(banks, q)
                    pe.wait_ge(v["rows_exp"], 3)
                    pe.wait_ge(free[5], columns)
                    for r, row in enumerate((CS, LF, EM)):
                        for t in range(q.tiles):
                            n = P if t < NCH else TS
                            col = (r * (NCH + 1) + t) * NH
                            last = nc.tensor.transpose(bank[5][0:n, col:col + NH], row[0:NH, t * P:t * P + n],
                                                       ident[0:NH, 0:NH])
                    last.then_inc(full[5], 1)
                    k = 0
                    for j in range(PAIRS):
                        for b0, bl in q.blocks:
                            bk, no = pairs[k]
                            pe.wait_ge(free[bk], no)
                            nc.tensor.matmul(bank[bk][:, 0:bl], pair_rows[:, j, :], W[0:NH, b0:b0 + bl], start=True,
                                             stop=True).then_inc(full[bk], 1)
                            k += 1
                    pe.wait_ge(free[4], over_chunk)
                    for j in range(PAIRS):
                        c0 = j * (NCH + NB_S)
                        last = nc.tensor.matmul(bank[4][:, c0:c0 + NCH], pair_rows[:, j, :], W[0:NH, P - 1:TP:P],
                                                start=True, stop=True)
                        if q.sample:
                            last = nc.tensor.matmul(bank[4][:, c0 + NCH:c0 + NCH + NB_S], pair_rows[:, j, :],
                                                    W[0:NH, TP + NT_S - 1:TM:NT_S], start=True, stop=True)
                    last.then_inc(full[4], 1)

                for part in PARTS:
                    with turns(pe, *part) as i:
                        f = Fills(banks, i, qkv_uses(q))
                        k = 0
                        for p in range(2):
                            if q.n == 0:
                                pe.wait_ge(S[1][f"x_landed{p}"], 16 * i + 16)
                                to_features(f, xs[p])
                            else:
                                pe.wait_ge(S[0]["y_staged"], 2 * i + p + 1)
                                to_tokens(f, y_stage, 0, 2)
                            slab_ready(s0 + 1 + p + 2 * i)
                            for b in range(nb):
                                product(q, f.take(k % 2), k % 2, (par + 1 + p) % 2, KC, 0, b, begins=b == 0)
                                k += 1
                    if part[1] == 3:
                        gate_rows()
                banks.skip(qkv_uses(q), 4)
                if q.n == 0:
                    pe.wait_ge(S[1]["x_landed0"], 16 * (NCH // 2 + 1))
                    to_features(banks, xs[0], TS)

                n0 = list(banks.n)
                loop_uses = {0: 2 * nb, 1: 2 * nb}
                with pe.Fori(0, 4) as i:
                    f = Fills(banks, i, loop_uses)
                    k = nb % 2
                    for n in range(4):
                        c = 2 * i + n // 2
                        if n % 2 == 0:
                            chunk_scores(v, n0, c)
                        else:
                            chunk_outputs(v, n0, c)
                        slab_ready(s0 + 9 + n + 4 * i)
                        for b in range(nb):
                            product(q, f.take(k % 2), k % 2, (par + 9 + n) % 2, KC, 0, b, begins=b == 0)
                            k += 1
                        if n % 2:
                            chunk_transposes(v, n0, c)
                banks.skip(loop_uses, 4)
                banks.skip(CHUNK_USES, NCH)

                if q.sample:
                    f = ChunkFills(n0, NCH)
                    chunk_scores(v, n0, NCH, TS)
                    pe.wait_ge(free[3], f.score + 1)
                    pe.wait_ge(free[7], f.values + 1)
                    pe.wait_ge(batch_queries, NH)
                    pe.wait_ge(states_in, 16 * 2 * PAIRS)
                    for bk, no, hs in ((4, f.out01, (0, 1)), (5, f.out23, (2, 3))):
                        pe.wait_ge(free[bk], no)
                        for h in hs:
                            o = bank[bk][0:TS, (h % 2) * (DV + 1):(h % 2 + 1) * (DV + 1)]
                            nc.tensor.matmul(o, Pm[:, h, 0:TS], V[:, h, :], start=True, stop=False)
                            for b in range(NB_S):
                                last = nc.tensor.matmul(o, qb[:, h, b, :], Cs[:, h // 2, b, :], start=False,
                                                        stop=b == NB_S - 1)
                        last.then_inc(full[bk], 1)
                    pe.wait_ge(batch_keys, NH)
                    banks.skip(CHUNK_USES)
                    banks.n[6] -= 1
                    for j in range(PAIRS):
                        for g, b0 in enumerate((0, 3, 6)):
                            bk = (2, 3, 6)[g]
                            pe.wait_ge(free[bk], banks.take(bk))
                            for hh in range(2):
                                for b in range(b0, min(b0 + 3, NB_S)):
                                    o = bank[bk][hh * DK:(hh + 1) * DK, (b - b0) * (DV + 1):(b - b0 + 1) * (DV + 1)]
                                    last = nc.tensor.matmul(o, kwb[:, 2 * j + hh, b, :], V[0:TS, 2 * j + hh, :],
                                                            start=True, stop=True)
                            last.then_inc(full[bk], 1)
                    chunk_transposes(v, n0, NCH, TS)

                pe.wait_ge(v["p_landed"], 16 * (1 + q.sample))
                for g in range(NCH // 2):
                    bk = 2 + g
                    pe.wait_ge(free[bk], banks.take(bk))
                    for t in range(2):
                        for c in range(2):
                            o = bank[bk][:, (2 * t + c) * P:(2 * t + c + 1) * P]
                            last = nc.tensor.transpose(o, pst[:, 2 * g + t, c * P:(c + 1) * P], ident[:, :])
                    last.then_inc(full[bk], 1)
                if q.sample:
                    pe.wait_ge(free[6], banks.take(6))
                    for c in range(2):
                        last = nc.tensor.transpose(bank[6][:, c * TS:(c + 1) * TS], pst_s[0:TS, c * P:(c + 1) * P],
                                                   ident[0:TS, 0:TS])
                    last.then_inc(full[6], 1)

                s = s0 + 25
                linear(q, s, uses, lambda b, k: pe.wait_ge(v["mix_lo"], KC))
                s += 8
                pe.wait_ge(v["res_sum"], KC * nb + 2)
                sum_over_features(q)
                was_read(pe, banks, 2, 3, 4, 5)
                k = 0
                for p in range(2):
                    slab_ready(s)
                    for n in range(4):
                        for b in range(nb):
                            product(q, banks.take(k % 2), k % 2, s % 2, 2, n, b, (hid[:, 0], hid[:, 1]),
                                    begins=n == 0 and b == 0)
                            k += 1
                    s += 1

                def normed_ready(b, k):
                    pe.wait_ge(v["low2"], KC * b + k + 1)

                def up_chunk(f, s, p, first):
                    for w in range(2):
                        slab_ready(s + w)
                        for b in range(nb):
                            product(q, f.take(3 * w + b), 3 * w + b, (p + w) % 2, KC, 0, b, begins=b == 0,
                                    ready=normed_ready if first and w == 0 else None)

                def down(f, s, p, size, before):
                    def hidden_ready(b, k):
                        pe.wait_ge(v["h_lo"], nb * (before + 1) + nb * k + b + 1)

                    nw = SLAB // size // P
                    k = 0
                    for m in range(KC // nw):
                        slab_ready(s + m)
                        for n in range(nw):
                            for b in range(nb):
                                product(q, f.take(6 + k % 2), 6 + k % 2, (p + m) % 2, size, n, b, (hid[:, 0], hid[:, 1]),
                                        begins=n == 0 and b == 0, ready=hidden_ready if m == 0 and n == 0 else None)
                                k += 1

                ffn_uses = {b: 4 for b in range(nb)}
                ffn_uses.update({3 + b: 4 for b in range(nb)})
                ffn_uses.update({6: 4 * nb, 7: 4 * nb})
                with pe.Fori(0, 4) as g:
                    f = Fills(banks, g, ffn_uses)
                    for c in range(GROUP):
                        up_chunk(f, s + 2 * c + 12 * g, s % 2, c == 0)
                    down(f, s + 8 + 12 * g, s % 2, GROUP, GROUP * g)
                banks.skip(ffn_uses, 4)
                s += 48
                for size, before in ((4, 16), (2, 20)):
                    if size == 2:
                        pe.wait_ge(v["e_sum"], KC * nb + 2)
                        sum_over_features(q)
                    for c in range(size):
                        up_chunk(banks, s, s % 2, False)
                        s += 2
                    down(banks, s, s % 2, size, before)
                    s += size

                def next_roots():
                    pe.wait_ge(S[1]["x_root"], 2)
                    for b in range(supers[1].nb):
                        spread_roots(supers[1], b, banks.take(5 + b))

                linear(q, s, uses, lambda b, k: pe.wait_ge(v["x3_lo"], k * nb + b + 1),
                       middle=next_roots if q.n == 0 else None)
                s += 8
                assert s == s0 + SLABS
            for t in range(q.tiles):
                n = P if t < NCH else TS
                pe.wait_ge(v["x4"], nb + (KC - 1) * nb + (t * P + n - 1) // q.blocks[0][1] + 1)
                to_tokens(banks, X, t, 2 + 2 * (t % 3), n)

        @block.scalar
        def _(act):
            banks = Banks()
            act.sem_inc(hi_done, 2)
            act.wait_ge(consts_made, 1)

            def next_high(s, i=0, step=0):
                p = s % 2
                act.wait_ge(landed[p], 16 * (s // 2 + 1) + 8 * step * i)
                act.wait_ge(slab_begun, s + 1 + step * i)
                nc.scalar.activation(whi[p][:, :], wraw[p][:, :], ACT.Copy).then_inc(hi_done, 1)

            def roots(q, bk=6):
                for b0, bl in q.blocks:
                    act.wait_ge(full[bk], banks.take(bk))
                    nc.scalar.activation(ss[:, b0:b0 + bl], bank[bk][:, 0:bl], ACT.Sqrt, bias=epst[:, 0:1],
                                         scale=1.0 / D).then_inc(free[bk], 1)

            def high_of_normed(v, q, m, normed, high):
                c, (b0, bl) = m % KC, q.blocks[m // KC]
                act.wait_ge(v[normed], m + 1)
                nc.scalar.activation(AH[:, c, b0:b0 + bl], tmp[m % 3][:, 0:bl], ACT.Copy).then_inc(v[high], 1)

            def chunk_exps(v, n0, c, p, n=P):
                f = ChunkFills(n0, c)
                act.wait_ge(v["staged"], c + 1)
                act.wait_ge(free[5], f.out23)
                act.wait_ge(full[2], f.exponent)
                for h in range(NH):
                    last = nc.scalar.activation(expE[0:n, h, 0:n], bank[2][0:n, h * n:(h + 1) * n], ACT.Exp,
                                                bias=colst[p][0:n, h:h + 1])
                last.then_inc(free[2], 1)
                act.wait_ge(full[7], f.values)
                nc.scalar.activation(V[0:n, :, 0:DV], bank[7][0:n, :].rearrange("p (h e) -> p h e", h=NH), ACT.Copy)\
                    .then_inc(free[7], 1)

            def chunk_squares(v, n0, c, n=P):
                f = ChunkFills(n0, c)
                act.wait_ge(free[3], f.score + 1)
                for bk, no, hs in ((4, f.out01, (0, 1)), (5, f.out23, (2, 3))):
                    act.wait_ge(full[bk], no)
                    for h in hs:
                        o = (h % 2) * (DV + 1)
                        last = nc.scalar.activation(expE[0:n, h, :], bank[bk][0:n, o:o + DV], ACT.Square,
                                                    scale=DV ** -0.5, accum_out=ss4[0:n, h:h + 1])
                last.then_inc(v["sq_done"], 1)

            def chunk_out(n0, c, tok, n=P):
                act.wait_ge(full[7], ChunkFills(n0, c).h_t)
                nc.scalar.activation(X[:, 4:8, tok], bank[7][:, 0:NH * n].rearrange("p (h t) -> p h t", h=NH), ACT.Copy)\
                    .then_inc(free[7], 1)

            for q in supers:
                X, U, v, s0, nb = q.X, q.U, S[q.n], q.slab0, q.nb
                uses = {0: nb, 1: nb}
                if q.n == 0:
                    for t in range(NCH):
                        act.wait_ge(x_in[t], 16)
                        nc.scalar.activation(X[:, t, 0:D], xin[t][:, :], ACT.Square, accum_out=x_sums[:, t:t + 1])\
                            .then_inc(v["x_sq"], 1)
                        act.wait_ge(full[2], banks.take(2))
                        banks.take(3)
                        nc.scalar.activation(q.home[:, 0:4, t * P:(t + 1) * P],
                                             bank[2][:, :].rearrange("p (c t) -> p c t", c=4), ACT.Copy).then_inc(free[2], 1)
                        if t == 2:
                            next_high(0)
                        if t >= 4:
                            for m in (2 * (t - 4), 2 * (t - 4) + 1):
                                high_of_normed(v, q, m, "normed", "high")
                    for b in range(nb):
                        banks.take(5 + b)
                    for m in range(KC, KC * nb):
                        high_of_normed(v, q, m, "normed", "high")
                else:
                    act.wait_ge(S[0]["x4"], supers[0].nb * (KC + 1))
                    act.wait_ge(v["low"], KC * nb)
                    nc.scalar.activation(y_stage[:, :, :], U[:, :, 0:P], ACT.Copy).then_inc(S[0]["y_staged"], 1)

                next_high(s0 + 1)
                for b in range(nb):
                    banks.take(b % 2)
                for b, no in enumerate(lf_fills(banks, q)):
                    b0, bl = q.blocks[b]
                    act.wait_ge(full[2 + b], no)
                    nc.scalar.activation(EM[0:NH, b0:b0 + bl], bank[2 + b][0:NH, 0:bl], ACT.Abs).then_inc(v["lf_abs"], 1)
                nc.scalar.activation(G[0:NH, 0:q.T], G[0:NH, 0:q.T], ACT.Tanh, scale=1.0 / GATE_CAP).then_inc(v["softcap"], 1)
                act.wait_ge(v["lf_abs"], nb)
                nc.scalar.activation(EM[0:NH, 0:q.T], EM[0:NH, 0:q.T], ACT.Exp, scale=-1.0).then_inc(v["lf_abs"], 1)
                act.wait_ge(v["lf_abs"], nb + 1)
                nc.scalar.activation(EM[0:NH, 0:q.T], EM[0:NH, 0:q.T], ACT.Ln, bias=1.0).then_inc(v["lf_soft"], 1)

                def next_tile(f, i, p, n=P):
                    t = 2 * i + p
                    w = S[1]
                    act.wait_ge(w[f"x_landed{p}"], 16 * i + 16)
                    act.wait_ge(w["x_kept"], t + 1)
                    nc.scalar.activation(squares[0:n, :], xs[p][0:n, :], ACT.Square, accum_out=sq_tile[0:n, 0:1])\
                        .then_inc(w["x_sq"], 1)
                    tok = ds(t * P, P) if n == P else slice(TP, TM)
                    last = [f.take(2), f.take(3)]
                    for m in range(2):
                        act.wait_ge(full[2 + m], last[m])
                        nc.scalar.activation(wide1[:, 4 * m:4 * m + 4, tok],
                                             bank[2 + m][:, 0:4 * n].rearrange("p (c t) -> p c t", c=4), ACT.Copy)\
                            .then_inc(free[2 + m], 1)
                    for m in range(2):
                        act.wait_ge(free[2 + m], last[m] + 1)
                    act.dma_start(stored_x[1][:, :, tok], wide1[:, :, tok]).then_inc(w["x_stored"], 16)

                def finished_tile(f, i, p, stage_next):
                    w, t = S[0], 2 * i + p
                    last = [f.take(2), f.take(3)]
                    for m in range(2):
                        act.wait_ge(full[2 + m], last[m])
                    for m in range(2):
                        nc.scalar.activation(y_stage[:, 4 * m:4 * m + 4, :], bank[2 + m][:, :].rearrange("p (c t) -> p c t", c=4),
                                             ACT.Square, scale=D ** -0.5, accum_out=y_sums[:, 0, m:m + 1])\
                            .then_inc(w["y_sq"], 1)
                    if stage_next:
                        act.wait_ge(w["y_sq"], 2 * t + 2)
                        nc.scalar.activation(y_stage[:, :, :], U[:, :, ds((t + 1) * P, P)], ACT.Copy).then_inc(w["y_staged"], 1)
                    act.wait_ge(w["y_root"], t + 1)
                    act.wait_ge(w["y_out0"], 16 * t + 16)
                    for m in range(2):
                        nc.scalar.activation(y_rows[:, m * 512:(m + 1) * 512], bank[2 + m][:, :], ACT.Copy,
                                             scale=y_roots[:, 0, 0:1]).then_inc(free[2 + m], 1)

                if q.n == 0:
                    act.wait_ge(v["x_stored"], 16)
                    act.wait_ge(v["low"], KC * nb)
                for part in PARTS:
                    with turns(act, *part) as i:
                        f = Fills(banks, i, qkv_uses(q))
                        k = 0
                        for p in range(2):
                            if q.n == 0:
                                next_tile(f, i, p)
                            else:
                                finished_tile(f, i, p, not (part[0] == 3 and p))
                            next_high(s0 + p + 2, i, 2)
                            for b0, bl in q.blocks:
                                act.wait_ge(full[k % 2], f.take(k % 2))
                                nc.scalar.activation(X[:, 2 * i + p, b0:b0 + bl], bank[k % 2][:, 0:bl], ACT.Copy)\
                                    .then_inc(free[k % 2], 1)
                                k += 1
                    if part[1] == 2:
                        act.wait_ge(v["rows_made"], 1)
                        for row, src, scale in ((EM, M, -1.0), (W, W, 1.0), (LF, LF, 1.0)):
                            nc.scalar.activation(row[0:NH, 0:q.T], src[0:NH, 0:q.T], ACT.Exp, scale=scale)\
                                .then_inc(v["rows_exp"], 1)
                    if part[1] == 3:
                        prep_fills(banks, q)
                banks.skip(qkv_uses(q), 4)
                if q.n == 0:
                    next_tile(banks, NCH // 2, 0, TS)
                    act.wait_ge(S[1]["x_stored"], 16 * supers[1].tiles)
                else:
                    act.wait_ge(S[0]["y_out0"], 16 * (NCH + 1))

                n0 = list(banks.n)
                loop_uses = {0: 2 * nb, 1: 2 * nb}
                with act.Fori(0, 4) as i:
                    f = Fills(banks, i, loop_uses)
                    k = nb % 2
                    for n in range(4):
                        c = 2 * i + n // 2
                        next_high(s0 + 10 + n, i, 4)
                        if n % 2 == 0:
                            chunk_exps(v, n0, c, n // 2)
                        else:
                            chunk_squares(v, n0, c)
                        for b0, bl in q.blocks:
                            no = f.take(k % 2)
                            if n < 2:
                                act.wait_ge(full[k % 2], no)
                                if n == 1:
                                    act.wait_ge(v["conv_done"], i + 1)
                                dst = zbuf[:, 2 + b0:2 + b0 + bl] if n else U[:, i, b0:b0 + bl]
                                nc.scalar.activation(dst, bank[k % 2][:, 0:bl], ACT.Copy).then_inc(free[k % 2], 1)
                            k += 1
                        if n % 2:
                            chunk_out(n0, c, ds(c * P, P))
                banks.skip(loop_uses, 4)
                banks.skip(CHUNK_USES, NCH)
                if q.sample:
                    chunk_exps(v, n0, NCH, 0, TS)
                    chunk_squares(v, n0, NCH, TS)
                    chunk_out(n0, NCH, slice(TP, TM), TS)
                    banks.skip(CHUNK_USES)
                    banks.skip({2: 2, 3: 2, 6: 1})

                was_filled(act, banks, 0, 1)
                was_read(act, banks, 0, 1)
                for m in (4, 5, 6, 7):
                    nc.scalar.activation(AH[:, m, 0:q.T], U[:, m, 0:q.T], ACT.Copy).then_inc(v["mix_hi"], 1)
                for m in range(4):
                    nc.scalar.activation(U[:, m, 0:q.T], U[:, m, 0:q.T], ACT.Sigmoid).then_inc(v["sig_o"], 1)
                for m in range(4):
                    act.wait_ge(v["merged"], m + 1)
                    nc.scalar.activation(AH[:, m, 0:q.T], U[:, m, 0:q.T], ACT.Copy).then_inc(v["mix_hi"], 1)
                for g in range(NCH // 2):
                    act.wait_ge(full[2 + g], banks.take(2 + g))
                    src = bank[2 + g][:, :].rearrange("p (t c n) -> p c t n", t=2, c=2)
                    dst = hid[:, 0, 0:2, 2 * g * P:(2 * g + 2) * P].rearrange("p c (t n) -> p c t n", t=2)
                    nc.scalar.activation(dst, src, ACT.Copy).then_inc(v["p_hi"], 1)
                if q.sample:
                    act.wait_ge(full[6], banks.take(6))
                    nc.scalar.activation(hid[:, 0, 0:2, TP:TM], bank[6][:, 0:2 * TS].rearrange("p (c n) -> p c n", c=2),
                                         ACT.Copy).then_inc(v["p_hi"], 1)

                s = s0 + 25
                with act.Fori(0, 4) as i:
                    f = Fills(banks, i, uses)
                    k = 0
                    for p in range(2):
                        next_high(s + p + 1, i, 2)
                        for b0, bl in q.blocks:
                            act.wait_ge(free[k % 2], f.take(k % 2) + 1)
                            act.wait_ge(v["res_sum"], k + 1 + 2 * nb * i)
                            nc.scalar.activation(tmp[k % 2][:, 0:bl], X[:, 2 * i + p, b0:b0 + bl], ACT.Square)\
                                .then_inc(v["res_sq"], 1)
                            k += 1
                banks.skip(uses, 4)
                s += 8
                roots(q)
                for m in range(KC * nb):
                    n, (b0, bl) = m // nb, q.blocks[m % nb]
                    if m % (4 * nb) == 0:
                        next_high(s + 1)
                        s += 1
                    act.wait_ge(full[m % 2], banks.take(m % 2))
                    nc.scalar.activation(U[:, n, b0:b0 + bl], bank[m % 2][:, 0:bl], ACT.Copy).then_inc(free[m % 2], 1)
                    high_of_normed(v, q, m, "normed2", "high2")

                def up_chunk(f, s, i, hc, count):
                    next_high(s + 1, i, 12)
                    for b, (b0, bl) in enumerate(q.blocks):
                        act.wait_ge(full[b], f.take(b))
                        act.wait_ge(v["h_lo"], count + b + 1)
                        nc.scalar.activation(sl[:, b0:b0 + bl], bank[b][:, 0:bl], ACT.Silu).then_inc(free[b], 1)
                    next_high(s + 2, i, 12)
                    for b, (b0, bl) in enumerate(q.blocks):
                        act.wait_ge(free[3 + b], f.take(3 + b) + 1)
                        nc.scalar.activation(hid[:, 0, hc, b0:b0 + bl], sl[:, b0:b0 + bl], ACT.Copy).then_inc(v["h_hi"], 1)

                ffn_uses = {b: 4 for b in range(nb)}
                ffn_uses.update({3 + b: 4 for b in range(nb)})
                ffn_uses.update({6: 4 * nb, 7: 4 * nb})
                with act.Fori(0, 4) as g:
                    f = Fills(banks, g, ffn_uses)
                    for c in range(GROUP):
                        up_chunk(f, s + 2 * c, g, c, nb * (c + GROUP * g))
                    k = 0
                    for n in range(4):
                        next_high(s + 9 + n, g, 12)
                        if n >= 2:
                            for b0, bl in q.blocks:
                                act.wait_ge(v["e_sum"], k + 1 + 2 * nb * g)
                                nc.scalar.activation(tmp[k % 2][:, 0:bl], U[:, 2 * g + n - 2, b0:b0 + bl], ACT.Square)\
                                    .then_inc(v["e_sq"], 1)
                                k += 1
                banks.skip(ffn_uses, 4)
                s += 48
                count = 16 * nb
                for size in (4, 2):
                    if size == 2:
                        roots(q)
                    for c in range(size):
                        up_chunk(banks, s, 0, c, count)
                        count += nb
                        s += 2
                    k = 0
                    for m in range(size):
                        next_high(s + 1)
                        for n in range(KC // size * nb):
                            no = banks.take(6 + k % 2)
                            if size == 2:
                                c, (b0, bl) = k // nb, q.blocks[k % nb]
                                act.wait_ge(free[6 + k % 2], no + 1)
                                nc.scalar.activation(AH[:, c, b0:b0 + bl], X[:, c, b0:b0 + bl], ACT.Copy).then_inc(v["x3_hi"], 1)
                            k += 1
                        s += 1

                def gate_block(no, i, k, b):
                    b0, bl = q.blocks[b]
                    act.wait_ge(full[k % 2], no)
                    act.wait_ge(v["x4"], k + 1 + 2 * nb * i)
                    nc.scalar.activation(sl[:, b0:b0 + bl], bank[k % 2][:, 0:bl], ACT.Sigmoid).then_inc(free[k % 2], 1)

                with act.Fori(0, 3) as i:
                    f = Fills(banks, i, uses)
                    for p in range(2):
                        next_high(s + p + 1, i, 2)
                        for b in range(nb):
                            k = p * nb + b
                            gate_block(f.take(k % 2), i, k, b)
                banks.skip(uses, 3)
                for p in range(2):
                    if p == 0 or q.n == 0:
                        next_high(s + 6 + p + 1)
                    for b in range(nb):
                        k = p * nb + b
                        gate_block(banks.take(k % 2), 3, k, b)
                        if q.n == 0 and p == 1:
                            for m in range(KC * b, KC * (b + 1 if b < nb - 1 else supers[1].nb)):
                                high_of_normed(S[1], supers[1], m, "normed", "high")
                if q.n == 0:
                    for b in range(supers[1].nb):
                        banks.take(5 + b)

            for t in range(q.tiles):
                n = P if t < NCH else TS
                for m in range(2):
                    bk = 2 + 2 * (t % 3) + m
                    act.wait_ge(full[bk], banks.take(bk))
                    if t >= 3:
                        act.wait_ge(v["y_root"], t - 2)
                    nc.scalar.activation(y_squares[0:n, t % 3, m, :], bank[bk][0:n, :], ACT.Square, scale=D ** -0.5,
                                         accum_out=y_sums[0:n, t % 3, m:m + 1]).then_inc(v["y_sq"], 1)

        @block.vector
        def _(dve):
            banks = Banks()
            for b in range(8):
                dve.sem_inc(free[b], 1)
            for q in supers:
                dve.sem_inc(S[q.n]["h_lo"], q.nb)
                dve.sem_inc(S[q.n]["x4"], q.nb)
                dve.sem_inc(S[q.n]["conv_done"], 1)
            dve.sem_inc(S[0]["y_out0"], 16)
            dve.wait_ge(consts_made, 1)
            own = Chain(dve, dve_own)

            def copy_at(out, in_):
                return nc.vector.tensor_scalar(out, in_, 1.0, None, ALU.mult)

            class Normalised:

                def __init__(self, q, x, g, root, normed, high, low):
                    self.q, self.v, self.x, self.g, self.root = q, S[q.n], x, g, root
                    self.normed, self.high, self.low = normed, high, low
                    self.m = 0

                def low_part(self, m):
                    c, (b0, bl) = m % KC, self.q.blocks[m // KC]
                    dve.wait_ge(self.v[self.high], m + 1)
                    nc.vector.tensor_tensor(AL[:, c, b0:b0 + bl], tmp[m % 3][:, 0:bl], AH[:, c, b0:b0 + bl],
                                            ALU.subtract).then_inc(self.v[self.low], 1)

                def step(self, count):
                    for m in range(self.m, self.m + count):
                        c, b, (b0, bl) = m % KC, m // KC, self.q.blocks[m // KC]
                        if c == 0:
                            self.roots = self.root(b)
                        if m >= 3:
                            dve.wait_ge(self.v[self.low], m - 2)
                        nc.vector.scalar_tensor_tensor(tmp[m % 3][:, 0:bl], self.x[:, c, b0:b0 + bl], self.g[:, c:c + 1],
                                                       self.roots, ALU.mult, ALU.mult).then_inc(self.v[self.normed], 1)
                        if m:
                            self.low_part(m - 1)
                    self.m += count
                    if self.m == KC * self.q.nb:
                        self.low_part(self.m - 1)

            def spread_normalised(q, fills):
                def root(b):
                    if b:
                        dve.wait_ge(S[q.n]["normed"], KC * b)
                        dve.sem_inc(free[4 + b], 1)
                    dve.wait_ge(full[5 + b], fills[b])
                    return bank[5 + b][:, 0:q.blocks[b][1]]

                return Normalised(q, q.home, gmix, root, "normed", "high", "low")

            def chunk_weights(v, n0, c, p, n=P):
                f = ChunkFills(n0, c)
                dve.wait_ge(free[2], f.exponent + 1)
                dve.wait_ge(full[3], f.score)
                nc.vector.scalar_tensor_tensor(Pm[0:n, :, 0:n], bank[3][0:n, 0:NH * n].rearrange("p (h t) -> p h t", h=NH),
                                               QSCALE, expE[0:n, :, 0:n], ALU.mult, ALU.mult)\
                    .then_inc(free[3], 1)
                dve.wait_ge(full[4], f.keys)
                nc.vector.tensor_tensor(kw[0:n, :, :], bank[4][0:n, 0:NH * DK].rearrange("p (h d) -> p h d", h=NH),
                                        colst[p][0:n, 4:8].unsqueeze(2).to_broadcast([n, NH, DK]), ALU.mult)\
                    .then_inc(free[4], 1)

            def chunk_heads(v, n0, c, p, n=P):
                f = ChunkFills(n0, c)
                dve.wait_ge(v["sq_done"], c + 1)
                for bk, no, h in ((4, f.out01, 0), (5, f.out23, 2)):
                    dve.wait_ge(full[bk], no)
                    den = bank[bk][0:n, 0:2 * (DV + 1)].rearrange("p (h e) -> p h e", h=2)[:, :, DV]
                    own.link(nc.vector.scalar_tensor_tensor(dm[0:n, h:h + 2], den, -1.0, colst[p][0:n, 8 + h:10 + h],
                                                            ALU.mult, ALU.max))
                    own.link(nc.vector.tensor_tensor(dm[0:n, h:h + 2], den, dm[0:n, h:h + 2], ALU.max))
                own.link(nc.vector.scalar_tensor_tensor(d2[0:n, :], dm[0:n, :], EPS, dm[0:n, :], ALU.mult, ALU.mult))
                nc.vector.tensor_tensor(tt[0:n, :], d2[0:n, :], ss4[0:n, :], ALU.add).then_inc(v["root_in"], 1)
                dve.wait_ge(v["root_done"], c + 1)
                for bk, h in ((4, 0), (5, 2)):
                    num = bank[bk][0:n, 0:2 * (DV + 1)].rearrange("p (h e) -> p h e", h=2)[:, :, 0:DV]
                    nc.vector.tensor_tensor(hn[0:n, h:h + 2, :], num, rr[0:n, h:h + 2].unsqueeze(2).to_broadcast([n, 2, DV]),
                                            ALU.mult).then_inc(free[bk], 1)

            for q in supers:
                X, U, v, s0, nb = q.X, q.U, S[q.n], q.slab0, q.nb
                T = q.T
                uses = {0: nb, 1: nb}
                if q.n == 0:
                    x_norm = spread_normalised(q, [banks.take(5 + b) for b in range(nb)])
                    for t in range(NCH):
                        banks.take(2)
                        dve.wait_ge(full[3], banks.take(3))
                        nc.vector.tensor_copy(q.home[:, 4:8, t * P:(t + 1) * P],
                                              bank[3][:, :].rearrange("p (c t) -> p c t", c=4)).then_inc(free[3], 1)
                        if t == 3:
                            was_read(dve, banks, 2, 3)
                            dve.wait_ge(gmix_in, 16)
                        if t >= 4:
                            x_norm.step(2)
                    was_read(dve, banks, 2, 3)
                    x_norm.step(KC)
                dve.wait_ge(v["normed"], KC * nb)
                dve.sem_inc(free[4 + nb], 1)

                if q.n == 0:
                    dve.wait_ge(v["x_sq"], NCH)
                    dve.wait_ge(consts_in, 16 * N_CONSTS)
                for b, (b0, bl) in enumerate(q.blocks):
                    dve.wait_ge(full[b % 2], banks.take(b % 2))
                    nc.vector.tensor_scalar(G[0:2 * NH, b0:b0 + bl], bank[b % 2][0:2 * NH, 0:bl], bias8[:, 0:1], None,
                                            ALU.add).then_inc(free[b % 2], 1)
                lf = lf_fills(banks, q)
                own.link(nc.vector.tensor_copy(pair_rows[:, :, :].rearrange("p j (hh d) -> p (j hh) d", hh=2),
                                               ident[0:NH, 0:NH].unsqueeze(2).to_broadcast([NH, NH, DK])))
                own.link(nc.vector.memset(W[0:NH, 0:T], 1.0))
                own.link(nc.vector.memset(W[0:NH, 0:TP:P], 0.0))
                if q.sample:
                    own.link(nc.vector.memset(W[0:NH, TP:TM:NT_S], 0.0))
                dve.wait_ge(v["lf_soft"], 1)
                for b, (b0, bl) in enumerate(q.blocks):
                    nc.vector.scalar_tensor_tensor(LF[0:NH, b0:b0 + bl], bank[2 + b][0:NH, 0:bl], 0.0, EM[0:NH, b0:b0 + bl],
                                                   ALU.min, ALU.subtract).then_inc(free[2 + b], 1)
                for b in range(nb):
                    dve.wait_ge(free[2 + b], lf[b] + 1)
                dve.wait_ge(v["softcap"], 1)
                own.link(nc.vector.tensor_scalar(G[0:NH, 0:T], G[0:NH, 0:T], GATE_CAP, None, ALU.mult))
                own.link(nc.vector.tensor_tensor_scan(B[0:NH, 0:T], W[0:NH, 0:T], LF[0:NH, 0:T], 0.0, ALU.mult, ALU.add))
                own.link(nc.vector.tensor_tensor_scan(M[0:NH, 0:TP], LF[0:NH, 0:TP], G[0:NH, 0:TP], carry[:, 0:1],
                                                      ALU.add, ALU.max))
                own.link(nc.vector.tensor_copy(mprev[:, 0:1], carry[:, :]))
                own.link(nc.vector.tensor_copy(mprev[:, 1:NCH], M[0:NH, P - 1:TP - P:P]))
                own.link(nc.vector.tensor_copy(carry[:, :], M[0:NH, TP - 1:TP]))
                if q.sample:
                    by_batch = "p (b t) -> p b t"
                    own.link(nc.vector.tensor_copy(sI[:, :, :], G[0:NH, TP:TM].rearrange(by_batch, t=NT_S)))
                    own.link(nc.vector.tensor_copy(sF[:, :, :], LF[0:NH, TP:TM].rearrange(by_batch, t=NT_S)))
                    own.link(nc.vector.tensor_copy(mprev[:, NCH:], ms0[:, :]))
                    own.link(nc.vector.tensor_tensor(m_out[:, :], sF[:, :, 0], ms0[:, :], ALU.add))
                    own.link(nc.vector.tensor_tensor(sI[:, :, 0], sI[:, :, 0], m_out[:, :], ALU.max))
                    own.link(nc.vector.memset(sF[:, :, 0], NEG))
                    own.link(nc.vector.tensor_tensor_scan(M[0:NH, TP:TM], sF[:, :, :].rearrange("p b t -> p (b t)"),
                                                          sI[:, :, :].rearrange("p b t -> p (b t)"), 0.0, ALU.add, ALU.max))
                    own.link(nc.vector.tensor_copy(m_out[:, :], M[0:NH, TP + NT_S - 1:TM:NT_S]))
                own.link(nc.vector.tensor_tensor(R1[0:NH, 0:T], B[0:NH, 0:T], M[0:NH, 0:T], ALU.subtract))
                own.link(nc.vector.tensor_tensor(CS[0:NH, 0:T], G[0:NH, 0:T], B[0:NH, 0:T], ALU.subtract))
                spans = [(0, TP, P, 0)] + ([(TP, TM, NT_S, NCH)] if q.sample else [])
                for a, z, n, m0 in spans:
                    k = (z - a) // n
                    by = dict(n=n)
                    r1 = R1[0:NH, a:z].rearrange("p (c n) -> p c n", **by)
                    own.link(nc.vector.tensor_tensor(W[0:NH, a:z].rearrange("p (c n) -> p c n", **by), r1,
                                                     mprev[:, m0:m0 + k].unsqueeze(2).to_broadcast([NH, k, n]), ALU.add))
                    end = R1[0:NH, a + n - 1:z:n].unsqueeze(2).to_broadcast([NH, k, n])
                    own.link(nc.vector.tensor_tensor(LF[0:NH, a:z].rearrange("p (c n) -> p c n", **by),
                                                     CS[0:NH, a:z].rearrange("p (c n) -> p c n", **by), end, ALU.add))
                dve.sem_inc(v["rows_made"], 1)
                columns, pairs, over_chunk = prep_fills(banks, q)
                dve.wait_ge(full[5], columns)
                stripe = bank[5][:, 0:3 * (NCH + 1) * NH].rearrange("p (r c h) -> p r c h", r=3, h=NH)
                if q.sample:
                    own.link(nc.vector.tensor_copy(cols[0:TS, :, NCH, :], stripe[0:TS, :, NCH, :]))
                nc.vector.tensor_copy(cols[:, :, 0:NCH, :], stripe[:, :, 0:NCH, :]).then_inc(free[5], 1)
                k = 0
                for j in range(PAIRS):
                    for b0, bl in q.blocks:
                        bk, no = pairs[k]
                        dve.wait_ge(full[bk], no)
                        nc.vector.scalar_tensor_tensor(qw[:, j, b0:b0 + bl], X[:, j, b0:b0 + bl], QSCALE,
                                                       bank[bk][:, 0:bl], ALU.mult, ALU.mult).then_inc(free[bk], 1)
                        k += 1
                dve.wait_ge(full[4], over_chunk)
                width = NCH + NB_S if q.sample else NCH
                nc.vector.tensor_copy(decay[:, :, 0:width],
                                      bank[4][:, 0:PAIRS * (NCH + NB_S)].rearrange("p (j c) -> p j c", j=PAIRS)[:, :, 0:width])\
                    .then_inc(free[4], 1)

                banks.skip(qkv_uses(q), 4)
                if q.n == 0:
                    banks.skip(TILE_USES)

                n0 = list(banks.n)
                loop_uses = {0: 2 * nb, 1: 2 * nb}

                def state_update(c, p):
                    dve.wait_ge(full[6], ChunkFills(n0, c).state)
                    for j in range(PAIRS):
                        last = nc.vector.scalar_tensor_tensor(state[:, j, :], state[:, j, :], colst[p][:, 12 + j:13 + j],
                                                              bank[6][:, j * (DV + 1):(j + 1) * (DV + 1)], ALU.mult, ALU.add)
                    last.then_inc(free[6], 1)

                with dve.Fori(0, 4) as i:
                    f = Fills(banks, i, loop_uses)
                    own.loop(i, 2 * 5 + 4 + (2 + 1 + 2 + 1 if q.sample else 0))
                    k = nb % 2
                    turns = []
                    for n in range(4 * nb):
                        turns.append((k % 2, f.take(k % 2)))
                        k += 1
                    chunk_weights(v, n0, 2 * i, 0)
                    state_update(2 * i, 0)
                    chunk_heads(v, n0, 2 * i, 0)
                    chunk_weights(v, n0, 2 * i + 1, 1)
                    for b, (b0, bl) in enumerate(q.blocks):
                        dve.wait_ge(free[turns[nb + b][0]], turns[nb + b][1] + 1)
                        bk, no = turns[2 * nb + b]
                        dve.wait_ge(full[bk], no)
                        z = zbuf[:, 2 + b0:2 + b0 + bl]
                        nc.vector.tensor_tensor(z, z, bank[bk][:, 0:bl], ALU.mult).then_inc(free[bk], 1)
                    for b in range(2):
                        bk, no = turns[2 * nb + nb - 1 - b]
                        dve.wait_ge(free[bk], no + 1)
                    own.link(copy_at(zbuf[:, 0:2], hist[:, i, :]))
                    own.link(copy_at(hist[:, i, :], zbuf[:, TP:TP + 2]))
                    if q.sample:
                        own.link(copy_at(zs[:, :, 0:2], convs[:, i, :, :]))
                        own.link(nc.vector.tensor_copy(zs[:, :, 2:], zbuf[:, 2 + TP:2 + TM].rearrange("p (b t) -> p b t", t=NT_S)))
                    own.link(nc.vector.tensor_scalar(cv[:, 0:T], zbuf[:, 2:2 + T], cw[:, 2, ds(i, 1)], None, ALU.mult))
                    own.link(nc.vector.scalar_tensor_tensor(cv[:, 0:T], zbuf[:, 1:1 + T], cw[:, 1, ds(i, 1)], cv[:, 0:T],
                                                            ALU.mult, ALU.add))
                    nc.vector.scalar_tensor_tensor(cv[:, 0:T], zbuf[:, 0:T], cw[:, 0, ds(i, 1)], cv[:, 0:T],
                                                   ALU.mult, ALU.add).then_inc(v["conv_done"], 1)
                    dve.wait_ge(v["conv_done"], i + 2)
                    if q.sample:
                        own.link(copy_at(convs[:, i, :, :], zs[:, :, NT_S:]))
                        cvs = cv[:, TP:TM].rearrange("p (b t) -> p b t", t=NT_S)
                        own.link(nc.vector.tensor_scalar(cvs, zs[:, :, 2:], cw[:, 2, ds(i, 1)], None, ALU.mult))
                        for w in (1, 0):
                            tail = nc.vector.scalar_tensor_tensor(cvs, zs[:, :, w:w + NT_S], cw[:, w, ds(i, 1)], cvs,
                                                                  ALU.mult, ALU.add)
                            own.link(tail)
                    state_update(2 * i + 1, 1)
                    chunk_heads(v, n0, 2 * i + 1, 1)
                    for b, (b0, bl) in enumerate(q.blocks):
                        bk, no = turns[3 * nb + b]
                        dve.wait_ge(full[bk], no)
                        nc.vector.tensor_tensor(U[:, i + 4, b0:b0 + bl], cv[:, b0:b0 + bl], bank[bk][:, 0:bl], ALU.mult)\
                            .then_inc(free[bk], 1)
                own.done(4)
                banks.skip(loop_uses, 4)
                banks.skip(CHUNK_USES, NCH)

                if q.sample:
                    f = ChunkFills(n0, NCH)
                    dve.wait_ge(free[5], f.out23)
                    own.link(nc.vector.memset(Pm[:, :, 0:TS], 0.0))
                    chunk_weights(v, n0, NCH, 0, TS)
                    dve.wait_ge(free[4], f.keys + 1)
                    dve.wait_ge(v["staged"], NCH + 1)
                    for h in range(NH):
                        nc.vector.tensor_tensor(kwb[:, h, :, :], kw[0:TS, h, :].unsqueeze(1).to_broadcast([TS, NB_S, DK]),
                                                batch_s[0:TS, :].unsqueeze(2).to_broadcast([TS, NB_S, DK]), ALU.mult)\
                            .then_inc(batch_keys, 1)
                    chunk_heads(v, n0, NCH, 0, TS)
                    banks.skip(CHUNK_USES)
                    banks.n[6] -= 1
                    for j in range(PAIRS):
                        own.link(nc.vector.tensor_tensor(
                            Cs[:, j, :, :], Cs[:, j, :, :],
                            decay[:, j, NCH:].unsqueeze(2).to_broadcast([P, NB_S, DV + 1]), ALU.mult))
                        for bk, b0 in ((2, 0), (3, 3), (6, 6)):
                            n = min(3, NB_S - b0)
                            dve.wait_ge(full[bk], banks.take(bk))
                            nc.vector.tensor_tensor(Cs[:, j, b0:b0 + n, :], Cs[:, j, b0:b0 + n, :],
                                                    bank[bk][:, 0:n * (DV + 1)].rearrange("p (b e) -> p b e", b=n), ALU.add)\
                                .then_inc(free[bk], 1)

                def mix_low(m, hi_count):
                    dve.wait_ge(v["mix_hi"], hi_count)
                    nc.vector.tensor_tensor(AL[:, m, 0:T], U[:, m, 0:T], AH[:, m, 0:T], ALU.subtract).then_inc(v["mix_lo"], 1)

                was_read(dve, banks, 7)
                for m in range(4):
                    mix_low(4 + m, m + 1)
                    dve.wait_ge(v["sig_o"], m + 1)
                    nc.vector.scalar_tensor_tensor(U[:, m, 0:T], X[:, 4 + m, 0:T], gmh[:, m:m + 1], U[:, m, 0:T],
                                                   ALU.mult, ALU.mult).then_inc(v["merged"], 1)
                for m in range(4):
                    mix_low(m, 5 + m)
                for g in range(NCH // 2):
                    banks.take(2 + g)
                    dve.wait_ge(v["p_hi"], g + 1)
                    toks = slice(2 * g * P, (2 * g + 2) * P)
                    for c in range(2):
                        src = bank[2 + g][:, :].rearrange("p (t c n) -> p c t n", t=2, c=2)[:, c]
                        last = nc.vector.tensor_tensor(hid[:, 1, c, toks].rearrange("p (t n) -> p t n", t=2), src,
                                                       hid[:, 0, c, toks].rearrange("p (t n) -> p t n", t=2), ALU.subtract)
                        if c == 0:
                            own.link(last)
                    last.then_inc(free[2 + g], 1)
                if q.sample:
                    banks.take(6)
                    dve.wait_ge(v["p_hi"], NCH // 2 + 1)
                    nc.vector.tensor_tensor(hid[:, 1, 0:2, TP:TM], bank[6][:, 0:2 * TS].rearrange("p (c n) -> p c n", c=2),
                                            hid[:, 0, 0:2, TP:TM], ALU.subtract).then_inc(free[6], 1)

                dve.wait_ge(v["reload"], 32)
                with dve.Fori(0, 4) as i:
                    f = Fills(banks, i, uses)
                    k = 0
                    for p in range(2):
                        for b0, bl in q.blocks:
                            dve.wait_ge(full[k % 2], f.take(k % 2))
                            x = X[:, 2 * i + p, b0:b0 + bl]
                            nc.vector.tensor_tensor(x, x, bank[k % 2][:, 0:bl], ALU.add).then_inc(free[k % 2], 1)
                            k += 1
                banks.skip(uses, 4)

                def root(b):
                    b0, bl = q.blocks[b]
                    dve.wait_ge(free[6], banks.take(6) + 1)
                    own.link(nc.vector.reciprocal(ss[:, b0:b0 + bl], ss[:, b0:b0 + bl]))
                    return ss[:, b0:b0 + bl]

                Normalised(q, X, gffn, root, "normed2", "high2", "low2").step(KC * nb)
                banks.skip(uses, 4)

                def up_chunk(f, hc, count):
                    for b, (b0, bl) in enumerate(q.blocks):
                        dve.wait_ge(free[b], f.take(b) + 1)
                        dve.wait_ge(full[3 + b], f.take(3 + b))
                        nc.vector.tensor_tensor(sl[:, b0:b0 + bl], sl[:, b0:b0 + bl], bank[3 + b][:, 0:bl], ALU.mult)\
                            .then_inc(free[3 + b], 1)
                    for b, (b0, bl) in enumerate(q.blocks):
                        dve.wait_ge(v["h_hi"], count + b + 1)
                        nc.vector.tensor_tensor(hid[:, 1, hc, b0:b0 + bl], sl[:, b0:b0 + bl], hid[:, 0, hc, b0:b0 + bl],
                                                ALU.subtract).then_inc(v["h_lo"], 1)

                def down(f, low_too):
                    for k in range(KC * nb):
                        c, (b0, bl) = k // nb, q.blocks[k % nb]
                        no = f.take(6 + k % 2)
                        dve.wait_ge(full[6 + k % 2], no)
                        x = X[:, c, b0:b0 + bl]
                        nc.vector.tensor_tensor(x, x, bank[6 + k % 2][:, 0:bl], ALU.add).then_inc(free[6 + k % 2], 1)
                        if low_too and k:
                            final_low(k - 1)
                    if low_too:
                        final_low(KC * nb - 1)

                def final_low(k):
                    c, (b0, bl) = k // nb, q.blocks[k % nb]
                    dve.wait_ge(v["x3_hi"], k + 1)
                    nc.vector.tensor_tensor(AL[:, c, b0:b0 + bl], X[:, c, b0:b0 + bl], AH[:, c, b0:b0 + bl],
                                            ALU.subtract).then_inc(v["x3_lo"], 1)

                ffn_uses = {b: 4 for b in range(nb)}
                ffn_uses.update({3 + b: 4 for b in range(nb)})
                ffn_uses.update({6: 4 * nb, 7: 4 * nb})
                with dve.Fori(0, 4) as g:
                    f = Fills(banks, g, ffn_uses)
                    for c in range(GROUP):
                        up_chunk(f, c, nb * (c + GROUP * g))
                    down(f, False)
                banks.skip(ffn_uses, 4)
                count = 16 * nb
                for size in (4, 2):
                    if size == 2:
                        for b0, bl in q.blocks:
                            dve.wait_ge(free[6], banks.take(6) + 1)
                            own.link(nc.vector.reciprocal(ss[:, b0:b0 + bl], ss[:, b0:b0 + bl]))
                    for c in range(size):
                        up_chunk(banks, c, count)
                        count += nb
                        if size == 2:
                            for e in range(4 * c, 4 * c + 4):
                                nc.vector.scalar_tensor_tensor(U[:, e, 0:T], U[:, e, 0:T], gple[:, e:e + 1], ss[:, 0:T],
                                                               ALU.mult, ALU.mult).then_inc(v["e_done"], 1)
                    down(banks, size == 2)

                dve.wait_ge(v["e_done"], KC)
                def gate_block(no, i, k, b):
                    b0, bl = q.blocks[b]
                    dve.wait_ge(free[k % 2], no + 1)
                    g_, x = sl[:, b0:b0 + bl], X[:, 2 * i + k // nb, b0:b0 + bl]
                    own.link(nc.vector.tensor_tensor(g_, g_, U[:, 2 * i + k // nb, b0:b0 + bl], ALU.mult))
                    nc.vector.tensor_tensor(x, x, g_, ALU.add).then_inc(v["x4"], 1)

                if q.n == 0:
                    x_norm = spread_normalised(supers[1], [banks.take(5 + b) for b in range(supers[1].nb)])
                with dve.Fori(0, 3) as i:
                    f = Fills(banks, i, uses)
                    own.loop(i, 2 * nb)
                    for k in range(2 * nb):
                        gate_block(f.take(k % 2), i, k, k % nb)
                own.done(3)
                banks.skip(uses, 3)
                for k in range(2 * nb):
                    gate_block(banks.take(k % 2), 3, k, k % nb)
                    if q.n == 0 and k == nb:
                        dve.wait_ge(S[1]["x_back"], 16)
                    if q.n == 0 and k >= nb:
                        x_norm.step(KC if k < 2 * nb - 1 else KC * (supers[1].nb - nb + 1))

            dve.wait_ge(v["gain_in"], 16)
            for t in range(q.tiles):
                n = P if t < NCH else TS
                if t >= 3:
                    dve.wait_ge(v[f"y_out{t % 3}"], 16 * (t // 3))
                dve.wait_ge(v["y_root"], t + 1)
                for m in range(2):
                    bk = 2 + 2 * (t % 3) + m
                    dve.wait_ge(full[bk], banks.take(bk))
                    nc.vector.scalar_tensor_tensor(y_end[t % 3][0:n, m * 512:(m + 1) * 512], bank[bk][0:n, :],
                                                   y_roots[0:n, t % 3, 0:1], gain_row[0:n, m * 512:(m + 1) * 512],
                                                   ALU.mult, ALU.mult).then_inc(free[bk], 1)

        @block.gpsimd
        def _(pool):
            banks = Banks()
            pool.sem_inc(lo_done, 2)
            for v in S:
                for name in ("res_sum", "e_sum"):
                    pool.sem_inc(v[name], 1)
            pool.sem_inc(S[1]["x_kept"], 1)
            made = Chain(pool, pool_own)
            for t, value in ((ident, 0.0), (identb, 0.0), (causal, 0.0), (causal_s, 0.0), (ones, 1.0),
                             (batch_s, 1.0), (state, 0.0), (epst, EPS), (neg_half, -0.5), (hist, 0.0), (carry, 0.0)):
                nc.gpsimd.memset(t[tuple([slice(None)] * len(t.shape))], value)
            made.link(nc.gpsimd.memset(sm[:, :, :], 0.0))

            def select(t, pattern, base, cm, op, fill):
                made.link(nc.gpsimd.affine_select(out=t, in_=t, compare_op=op, fill=fill, base=base, pattern=pattern,
                                                  channel_multiplier=cm))

            for t in (ident, identb):
                select(t[:, :], [[-1, P]], 0, 1, ALU.not_equal, 1.0)
            select(causal[:, :], [[1, P]], 0, -1, ALU.is_ge, NEG)
            select(causal_s[:, :, :], [[NT_S, NB_S], [1, NT_S]], 0, -1, ALU.is_ge, NEG)
            select(causal_s[:, :, :], [[-NT_S, NB_S], [0, NT_S]], 0, 1, ALU.is_ge, NEG)
            select(batch_s[:, :], [[-NT_S, NB_S]], 0, 1, ALU.is_ge, 0.0)
            select(batch_s[:, :], [[NT_S, NB_S]], NT_S - 1, -1, ALU.is_ge, 0.0)
            pool.sem_inc(consts_made, 1)

            def next_low(s, i=0, step=0):
                p = s % 2
                pool.wait_ge(hi_done, s + 3 + step * i)
                nc.gpsimd.tensor_tensor(wlo[p][:, :], wraw[p][:, :], whi[p][:, :], ALU.subtract).then_inc(lo_done, 1)

            def clear_sums(v, q, name):
                nc.gpsimd.memset(ss[:, 0:q.T], 0.0).then_inc(v[name], 1)

            def add_square(v, q, name, squares, k, b, turn=0):
                b0, bl = q.blocks[b]
                pool.wait_ge(v[squares], k + 1 + turn)
                pool.wait_ge(v[name], k + 2 + turn)
                nc.gpsimd.tensor_tensor(ss[:, b0:b0 + bl], ss[:, b0:b0 + bl], tmp[k % 2][:, 0:bl], ALU.add)\
                    .then_inc(v[name], 1)

            def inverse_root(out, mean, n, width=1):
                made.link(nc.gpsimd.tensor_tensor(out, mean, epst[0:n, 0:1].to_broadcast([n, width]), ALU.add))
                return nc.gpsimd.tensor_tensor(out, out, neg_half[0:n, 0:width], ALU.pow)

            def roots_of_x(sem_, a, z, n=P):
                made.link(nc.gpsimd.tensor_scalar(x_sums[0:n, a:z], x_sums[0:n, a:z], 1.0 / D, None, ALU.mult))
                inverse_root(x_roots[0:n, a:z], x_sums[0:n, a:z], n, z - a).then_inc(sem_, 1)

            next_low(0)
            for q in supers:
                X, U, v, s0, nb = q.X, q.U, S[q.n], q.slab0, q.nb
                uses = {0: nb, 1: nb}
                if q.n == 0:
                    banks.skip(TILE_USES, NCH)
                    for b in range(nb):
                        banks.take(5 + b)
                        pool.wait_ge(v["x_sq"], 4 * (b + 1))
                        roots_of_x(v["x_root"], 4 * b, 4 * b + 4)
                next_low(s0 + 1)
                for b in range(nb):
                    banks.take(b % 2)
                lf_fills(banks, q)
                slabs0 = list(banks.n)

                def qkv_part(part):
                    with turns(pool, *part) as i:
                        f = Fills(banks, i, qkv_uses(q))
                        made.loop(i - part[0], 2 if q.n == 0 else 2 * 2)
                        for p in range(2):
                            t, tile = 2 * i + p, [f.take(2), f.take(3)]
                            if q.n == 0:
                                pool.wait_ge(S[1]["x_sq"], t + 1)
                                made.link(nc.gpsimd.tensor_copy(x_sums[:, ds(t, 1)], sq_tile[:, 0:1]))
                                pool.sem_inc(S[1]["x_kept"], 1)
                            else:
                                w = S[0]
                                pool.wait_ge(w["y_sq"], 2 * t + 2)
                                made.link(nc.gpsimd.tensor_tensor(y_roots[:, 0, 0:1], y_sums[:, 0, 0:1], y_sums[:, 0, 1:2],
                                                                  ALU.add))
                                inverse_root(y_roots[:, 0, 0:1], y_roots[:, 0, 0:1], P).then_inc(w["y_root"], 1)
                            if q.n:
                                pool.wait_ge(free[2], tile[0] + 1)
                                pool.wait_ge(free[3], tile[1] + 1)
                                nc.gpsimd.tensor_tensor(y_rows[:, :], y_rows[:, :], gain_row[:, :], ALU.mult)\
                                    .then_inc(w["y_gained"], 1)
                            next_low(s0 + p + 2, i, 2)
                    made.done(part[1] - part[0])

                if q.n:
                    pool.wait_ge(S[0]["gain_in"], 16)
                qkv_part(PARTS[0])
                qkv_part(PARTS[1])
                columns, pairs, over_chunk = prep_fills(banks, q)
                pool.wait_ge(full[4], over_chunk)
                for t in (qz[:, :, :], qwz[:, :, :], rz[:, :]):
                    nc.gpsimd.memset(t, 0.0).then_inc(v["stage_clear"], 1)
                pool.wait_ge(v["stage_clear"], 3)
                was_read(pool, banks, 4, 5, 6, 7)
                n0 = list(banks.n)
                for b, k in qkv_uses(q).items():
                    n0[b] += 4 * k
                if q.n == 0:
                    for b in TILE_USES:
                        n0[b] += 1

                def stage_scores(c, tok, n=P):
                    pool.wait_ge(full[7], ChunkFills(n0, c).values - 2)
                    stage_keys(tok, n)
                    made.link(nc.gpsimd.tensor_copy(vst[:, :, 0:n], X[:, 4:8, tok]))

                def stage_keys(tok, n=P):
                    made.link(nc.gpsimd.tensor_copy(kst[:, :, 0:n], X[:, 2:4, tok]))
                    for half in range(2):
                        r = slice(half * DK, (half + 1) * DK)
                        made.link(nc.gpsimd.tensor_copy(qz[r, half:NH:2, 0:n], X[r, 0:2, tok]))
                    made.link(nc.gpsimd.tensor_copy(rz[0:NH, 0:n], R1[0:NH, tok]))

                def stage_outputs(c, p, tok, n=P):
                    pool.wait_ge(full[6], ChunkFills(n0, c).state - 1)
                    for half in range(2):
                        r = slice(half * DK, (half + 1) * DK)
                        made.link(nc.gpsimd.tensor_copy(qwz[r, half:NH:2, 0:n], qw[r, :, tok]))
                    made.link(nc.gpsimd.tensor_copy(colst[p][0:n, 0:12].rearrange("p (r h) -> p r h", r=3), cols[0:n, :, c, :]))
                    nc.gpsimd.tensor_copy(colst[p][:, 12:14], decay[:, :, c if n == P else 0]).then_inc(v["staged"], 1)

                def root(c, n=P):
                    pool.wait_ge(v["root_in"], c + 1)
                    nc.gpsimd.tensor_tensor(rr[0:n, :], tt[0:n, :], neg_half[0:n, 0:NH], ALU.pow).then_inc(v["root_done"], 1)

                def chunk(i, m, stage_next=True):
                    c = 2 * i + m
                    next_low(s0 + 10 + 2 * m, i, 4)
                    if stage_next:
                        stage_scores(c + 1, ds((c + 1) * P, P))
                        stage_outputs(c + 1, 1 - m, ds((c + 1) * P, P))
                    next_low(s0 + 11 + 2 * m, i, 4)
                    root(c)

                stage_keys(slice(0, P))
                qkv_part(PARTS[2])
                pool.wait_ge(free[nb % 2], banks.n[nb % 2] + 4 * nb + (0 if nb == 3 else 1))
                made.link(nc.gpsimd.tensor_copy(vst[:, :, :], X[:, 4:8, 0:P]))
                pool.wait_ge(full[3], n0[3] - (q.n == 0))
                made.link(nc.gpsimd.memset(V[:, :, DV:], 1.0))
                stage_outputs(0, 0, slice(0, P))
                banks.skip(qkv_uses(q), 4)
                if q.n == 0:
                    banks.skip(TILE_USES)
                with pool.Fori(0, 3) as i:
                    made.loop(i, 2 * 8)
                    chunk(i, 0)
                    chunk(i, 1)
                made.done(3)
                chunk(3, 0)
                chunk(3, 1, stage_next=False)
                banks.skip({0: 2 * nb, 1: 2 * nb}, 4)
                banks.skip(CHUNK_USES, NCH)
                if q.sample:
                    stage_scores(NCH, slice(TP, TM), TS)
                    stage_outputs(NCH, 0, slice(TP, TM), TS)
                    made.link(nc.gpsimd.memset(batch_t[:, :, :], 1.0))
                    select(batch_t[:, :, :], [[-NT_S, NB_S], [1, TS]], 0, 0, ALU.is_ge, 0.0)
                    select(batch_t[:, :, :], [[NT_S, NB_S], [-1, TS]], NT_S - 1, 0, ALU.is_ge, 0.0)
                    was_read(pool, banks, 0, 1)
                    pool.wait_ge(v["staged"], NCH + 1)
                    for h in range(NH):
                        nc.gpsimd.tensor_tensor(qb[:, h, :, :], qwz[:, h, 0:TS].unsqueeze(1).to_broadcast([P, NB_S, TS]),
                                                batch_t[:, :, :], ALU.mult).then_inc(batch_queries, 1)
                    root(NCH, TS)
                    banks.skip(CHUNK_USES)
                    banks.skip({2: 2, 3: 2, 6: 1})

                was_filled(pool, banks, 2, 3, 4, 5, 6, 7)
                was_read(pool, banks, 7)
                clear_sums(v, q, "res_sum")
                s = s0 + 25
                with pool.Fori(0, 4) as i:
                    for p in range(2):
                        next_low(s + p + 1, i, 2)
                        for b in range(nb):
                            add_square(v, q, "res_sum", "res_sq", p * nb + b, b, 2 * nb * i)
                s += 8
                for p in range(2):
                    next_low(s + 1)
                    s += 1
                pool.wait_ge(v["low2"], KC * nb)
                clear_sums(v, q, "e_sum")
                with pool.Fori(0, 4) as g:
                    for n in range(12):
                        next_low(s + n + 1, g, 12)
                        if n >= 10:
                            for b in range(nb):
                                add_square(v, q, "e_sum", "e_sq", (n - 10) * nb + b, b, 2 * nb * g)
                s += 48
                for n in range(18):
                    next_low(s + 1)
                    s += 1
                if q.n == 0:
                    pool.wait_ge(S[1]["x_sq"], NCH + 1)
                    made.link(nc.gpsimd.tensor_copy(x_sums[0:TS, NCH:NCH + 1], sq_tile[0:TS, 0:1]))
                    roots_of_x(S[1]["x_root"], 0, NCH)
                    roots_of_x(S[1]["x_root"], NCH, NCH + 1, TS)
                with pool.Fori(0, 3) as i:
                    for p in range(2):
                        next_low(s + p + 1, i, 2)
                next_low(s + 7)
                if q.n == 0:
                    next_low(s + 8)
                for g in range(4):
                    banks.take(2 + g)
                if q.sample:
                    banks.take(6)
                banks.skip({0: 12 * nb, 1: 12 * nb, 6: 2 * nb})
                for b in range(nb):
                    banks.skip({b: FF, 3 + b: FF})
                banks.skip({6: 24 * nb, 7: 24 * nb})
                if q.n == 0:
                    banks.skip({5 + b: 1 for b in range(supers[1].nb)})

            for t in range(q.tiles):
                n = P if t < NCH else TS
                pool.wait_ge(v["y_sq"], 2 * t + 2)
                if t >= 3:
                    for m in range(2):
                        pool.wait_ge(free[2 + 2 * (t % 3) + m], banks.n[2 + 2 * (t % 3) + m] + 1)
                for m in range(2):
                    banks.take(2 + 2 * (t % 3) + m)
                r = y_roots[0:n, t % 3, 0:1]
                made.link(nc.gpsimd.tensor_tensor(r, y_sums[0:n, t % 3, 0:1], y_sums[0:n, t % 3, 1:2], ALU.add))
                inverse_root(r, r, n).then_inc(v["y_root"], 1)


INS = ["x_prompt", "x_sample", "p_prompt", "p_sample", "state_C", "state_n", "state_m", "state_conv", "g_mix", "w_in",
       "b_ig", "b_fg", "g_mh", "conv_w", "w_out", "g_ffn", "w_gate", "w_up", "w_down", "w_ple", "g_ple", "w_pg", "g_final"]
OUTS = [("y_prompt", (1, 2 * TP, D)), ("y_sample", (NB_S, NT_S, D)), ("C_prompt", (1, 1, NH, DK, DV)),
        ("n_prompt", (1, 1, NH, DK)), ("m_prompt", (1, 1, NH)), ("conv_prompt", (1, 1, 2, 512)),
        ("C_sample", (1, NB_S, NH, DK, DV)), ("n_sample", (1, NB_S, NH, DK)), ("m_sample", (1, NB_S, NH)),
        ("conv_sample", (1, NB_S, 2, 512))]


def kernel(**inputs):
    import numpy as np
    import concourse.bacc as bacc
    from concourse.bass_utils import run_bass_kernel_spmd

    nc = bacc.Bacc("TRN2", target_bir_lowering=False, num_devices=1)
    arrays, args = {}, []
    for name in INS:
        a = np.ascontiguousarray(inputs[name])
        arrays[name] = a
        args.append(nc.dram_tensor(name, a.shape, F32, kind="ExternalInput").ap())
    for name, shape in OUTS:
        args.append(nc.dram_tensor(name, shape, F32, kind="ExternalOutput").ap())
    build(nc, *args)
    got = run_bass_kernel_spmd(nc, [arrays], core_ids=[0]).results[0]
    return tuple(got[name] for name, _ in OUTS)
```

```python
from contextlib import ExitStack, nullcontext

import concourse.bass as bass
from concourse import mybir

ALU = mybir.AluOpType
ACT = mybir.ActivationFunctionType
F32 = mybir.dt.float32
F32R = mybir.dt.float32r
BF16 = mybir.dt.bfloat16
ds = bass.ds

P = 128
D = 1024
KC = D // P
NH, DK, DV = 4, 64, 128
PAIRS = NH // 2
DFF = 2816
FF = DFF // P
PLE = 256
GATE_CAP = 15.0
EPS = 1e-6
NB_S, NT_S = 8, 4
TS = NB_S * NT_S
TP = 1024
TM = TP + TS
NCH = TP // P
QSCALE = DK ** -0.5
NEG = -1e30
GROUP = 4
SLAB = 1024
SLABS = 8 + 1 + 16 + 8 + 2 + (5 * 12 + 6) + 8
COL_G, COL_O = 2 * NH * DK + NH * DV, 2 * NH * DK + NH * DV + 2 * NH
COL_B = COL_O + NH * DV
COL_C = COL_B + 512
COL_H = COL_C + 512
HI = 32
N_CONSTS = 2 + 3 + 3 + 1 + 8


class Super:

    def __init__(self, n):
        self.n = n
        self.sample = n == 1
        self.T = TM if self.sample else TP
        self.nb = 3 if self.sample else 2
        size = self.T // self.nb
        self.blocks = [(b * size, size) for b in range(self.nb)]
        self.tiles = NCH + self.sample
        self.slab0 = n * SLABS


class Banks:

    def __init__(self):
        self.n = [0] * 8

    def take(self, b):
        self.n[b] += 1
        return self.n[b]

    def skip(self, uses, times=1):
        for b, m in uses.items():
            self.n[b] += m * times


class Fills:

    def __init__(self, banks, i, uses):
        self.base, self.i, self.uses, self.k = list(banks.n), i, uses, {b: 0 for b in uses}

    def take(self, b):
        self.k[b] += 1
        return self.base[b] + self.k[b] + self.i * self.uses[b]


class Chain:

    def __init__(self, eng, sem):
        self.eng, self.sem, self.n, self.i, self.per, self.start = eng, sem, 0, 0, 0, 0

    def loop(self, i, per):
        self.i, self.per, self.start = i, per, self.n

    def done(self, times):
        assert self.n - self.start == self.per, (self.n - self.start, self.per)
        self.n, self.i, self.per = self.start + self.per * times, 0, 0

    def link(self, ins):
        self.n += 1
        ins.then_inc(self.sem, 1)
        self.eng.wait_ge(self.sem, self.n + self.i * self.per)


def build(nc, x_prompt, x_sample, p_prompt, p_sample, state_C, state_n, state_m, state_conv, g_mix, w_in,
          b_ig, b_fg, g_mh, conv_w, w_out, g_ffn, w_gate, w_up, w_down, w_ple, g_ple, w_pg, g_final,
          y_prompt, y_sample, C_prompt, n_prompt, m_prompt, conv_prompt, C_sample, n_sample, m_sample,
          conv_sample):
    supers = [Super(0), Super(1)]
    stored_x = [nc.dram_tensor(f"stored_x{n}", (P, KC, TM), F32, kind="Internal").ap() for n in range(2)]

    SLOT = TM * 4
    origin = (nc.sbuf_base + 31) // 32 * 32

    def at(name, shape, dt, offset):
        return nc.alloc_sbuf_tensor_at(name, shape, dt, offset=offset)

    wide0 = at("wide0", [P, KC, TM], F32, origin)
    AH = at("AH", [P, KC, TM], F32R, origin + 8 * SLOT)
    AL = at("AL", [P, KC, TM], F32R, origin + 16 * SLOT)
    wide1 = at("wide1", [P, KC, TM], F32, origin + 24 * SLOT)
    R0 = origin + 32 * SLOT
    hid = at("hid", [P, 2, GROUP, TM], F32R, R0)
    rows = at("rows", [P, 8, TM], F32, R0)
    next_x = at("next_x", [P, KC, TM], F32, R0)
    xin = [at(f"xin{t}", [P, D], F32, R0 + t * 4096) for t in range(NCH)]
    y_end = [at(f"y_end{p}", [P, D], F32, R0 + p * 4096) for p in range(3)]
    y_squares = at("y_squares", [P, 3, 2, 512], F32, R0 + 3 * 4096)
    for q, x_, u_, home in zip(supers, (wide0, wide1), (wide1, wide0), (wide1, next_x)):
        q.X, q.U, q.home = x_, u_, home
    G, LF, B, M, R1, W, CS, EM = (rows[:, n, :] for n in range(8))
    qw = rows[:, 0:2, :]
    zbuf = at("zbuf", [P, TM + 2], F32, R0 + 2 * SLOT)
    Cs = at("Cs", [P, PAIRS, NB_S, DV + 1], F32, R0 + 2 * SLOT)
    kwb = at("kwb", [TS, NH, NB_S, DK], F32, R0)
    stage0 = R0 + 5 * SLOT
    kst = at("kst", [P, PAIRS, P], F32, stage0)
    qz = at("qz", [P, NH, P], F32, stage0 + 1024)
    qwz = at("qwz", [P, NH, P], F32, stage0 + 3072)
    vst = at("vst", [P, NH, P], F32, stage0 + 5120)
    rz = at("rz", [P, P], F32R, stage0 + 7168)
    R1_parts = at("R1_parts", [P, TM], F32R, R0 + 4 * SLOT)
    R1_high = at("R1_high", [P, TM], F32R, R0 + 2 * SLOT)
    cv = at("cv", [P, TM], F32, R0 + 7 * SLOT)
    qb = at("qb", [P, NH, NB_S, TS], F32, R0 + 4 * SLOT)
    pst = at("pst", [P, NCH, PLE], F32, R0 + 6 * SLOT)

    slab_at = R0 + 8 * SLOT
    wraw = [at(f"wraw{p}", [P, SLAB], F32, slab_at + p * 4096) for p in range(2)]
    whi = [at(f"whi{p}", [P, SLAB], F32R, slab_at + (2 + p) * 4096) for p in range(2)]
    wlo = [at(f"wlo{p}", [P, SLAB], F32R, slab_at + (4 + p) * 4096) for p in range(2)]

    cursor = [slab_at + 6 * 4096]

    def keep(name, shape, dt=F32):
        size = 1
        for n in shape[1:]:
            size *= n
        size *= 2 if dt == BF16 else 4
        t = at(name, shape, dt, cursor[0])
        cursor[0] += (size + 31) // 32 * 32
        return t

    ident = keep("ident", [P, P])
    pick = keep("pick", [P, NH], F32R)
    identb = keep("identb", [P, P], BF16)
    causal = keep("causal", [P, P], BF16)
    causal_s = keep("causal_s", [P, NB_S, NT_S], BF16)
    batch_s = keep("batch_s", [P, NB_S])
    state = keep("state", [P, PAIRS, DV + 1])
    ones = keep("ones", [P, 1])
    epst = keep("epst", [P, 1])
    neg_half = keep("neg_half", [P, NCH + 1])
    gmix, gffn, gple = (keep(n, [P, KC]) for n in ("gmix", "gffn", "gple"))
    gmh = keep("gmh", [P, NH])
    cw = keep("cw", [P, 3, 4])
    bias8 = keep("bias8", [2 * NH, 1])
    hist = keep("hist", [P, 4, 2])
    convs = keep("convs", [P, 4, NB_S, 2])
    zs = keep("zs", [P, NB_S, 2 + NT_S])
    carry = keep("carry", [NH, 1])
    mprev = keep("mprev", [NH, NCH + NB_S])
    m_out = keep("m_out", [NH, NB_S])
    ms0 = keep("ms0", [NH, NB_S])
    sI = keep("sI", [NH, NB_S, NT_S])
    sF = keep("sF", [NH, NB_S, NT_S])
    decay = keep("decay", [P, PAIRS, NCH + NB_S])
    cols = keep("cols", [P, 3, NCH + 1, NH])
    colst = [keep(f"colst{p}", [P, 14]) for p in range(2)]
    sm = keep("sm", [P, 5, NH])
    ss4, dm, d2, tt, rr = (sm[:, n, :] for n in range(5))
    sq_tile = keep("sq_tile", [P, 2])
    x_sums = keep("x_sums", [P, NCH + 1])
    x_roots = keep("x_roots", [P, NCH + 1])
    means = keep("means", [P, NCH + 1])
    mean_roots = keep("mean_roots", [P, NCH + 1])
    y_sums = keep("y_sums", [P, 3, 2])
    y_roots = keep("y_roots", [P, 3, 2])
    mix0 = cursor[0]
    expE = keep("expE", [P, NH, P])
    Pm = keep("Pm", [P, NH, P])
    cursor[0] += 128
    V = keep("V", [P, NH, DV + 1])
    kw = keep("kw", [P, NH, DK])
    hn = keep("hn", [P, NH, P])
    batch_t = keep("batch_t", [P, NB_S, TS])
    cursor[0] = mix0
    ss = keep("ss", [P, TM])
    sl = keep("sl", [P, TM])
    tmp = [keep(f"tmp{p}", [P, 512]) for p in range(3)]
    pair_rows = at("pair_rows", [NH, PAIRS, P], F32, cursor[0] - 1024)
    pst_s = at("pst_s", [P, PLE], F32, cursor[0] - 2048)
    gain_row = at("gain_row", [P, D], F32, mix0)
    xs = [at(f"xs{p}", [P, D], F32, mix0 + p * SLOT) for p in range(2)]
    squares = at("squares", [P, D], F32, mix0 + 2 * SLOT)
    y_stage = at("y_stage", [P, KC, P], F32, mix0 + SLOT)
    y_rows = at("y_rows", [P, D], F32, mix0 + 2 * SLOT)
    assert cursor[0] <= nc.sbuf_usable_end, (cursor[0], nc.sbuf_usable_end)

    def by_k(w):
        return w.rearrange("(k p) n -> p k n", p=P)

    w_in_v, w_out_v, w_gate_v, w_up_v, w_down_v, w_ple_v, w_pg_v = (
        by_k(w[0]) for w in (w_in, w_out, w_gate, w_up, w_down, w_ple, w_pg))

    with ExitStack() as ctx:
        bank = [ctx.enter_context(nc.psum_tensor(f"bank{b}", [P, 512], F32)) for b in range(8)]

        def sem(name):
            return ctx.enter_context(nc.semaphore(name))

        gmix_in = sem("gmix_in")
        consts_in = sem("consts_in")
        consts_made = sem("consts_made")
        landed = [sem("landed_even"), sem("landed_odd")]
        hi_done, lo_done = sem("hi_done"), sem("lo_done")
        slab_begun = sem("slab_begun")
        full = [sem(f"full{b}") for b in range(8)]
        free = [sem(f"free{b}") for b in range(8)]
        dve_own, pool_own = sem("dve_own"), sem("pool_own")
        names = ["x_landed0", "x_landed1", "x_sq", "x_kept", "x_root", "x_stored", "x_back", "normed", "high", "low",
                 "softcap", "lf_abs", "lf_soft", "rows_made", "rows_exp", "stage_clear", "staged", "conv_done",
                 "sq_done", "root_in", "root_done", "merged", "mix_hi", "mix_lo", "reload0", "reload1", "p_landed",
                 "p_hi", "res_sq", "res_sum", "res_mean", "res_root", "e_mean", "e_root", "normed2", "high2", "low2", "e_sq", "e_sum", "e_done",
                 "h_hi", "h_lo", "x3_hi", "x3_lo", "x4", "gain_in", "y_staged", "y_sq", "y_root", "y_gained",
                 "y_out0", "y_out1", "y_out2"]
        S = [{n: sem(f"{n}_{q}") for n in names} for q in range(2)]
        x_in = [sem(f"x_in{t}") for t in range(NCH)]
        states_in, batch_queries, batch_keys = sem("states_in"), sem("batch_queries"), sem("batch_keys")
        small_out = sem("small_out")
        ctx.enter_context(nc.allow_non_contiguous_dma(reason="gains, biases and small states"))
        block = ctx.enter_context(nc.Block())

        def was_filled(eng, banks, *bks):
            for b in bks:
                eng.wait_ge(full[b], banks.n[b])

        def was_read(eng, banks, *bks):
            for b in bks:
                eng.wait_ge(free[b], banks.n[b] + 1)

        class ChunkFills:

            def __init__(self, banks, c):
                n = banks
                self.exponent, self.score = n[2] + c + 1, n[3] + c + 1
                self.keys, self.out01 = n[4] + 2 * c + 1, n[4] + 2 * c + 2
                self.out23, self.state = n[5] + c + 1, n[6] + c + 1
                self.values_bank, self.values, self.h_t = 7, n[7] + 2 * c + 1, n[7] + 2 * c + 2
                if isinstance(c, int) and c == NCH:
                    self.values_bank, self.values, self.h_t = 6, self.state, n[7] + 2 * c + 1

        CHUNK_USES = {2: 1, 3: 1, 4: 2, 5: 1, 6: 1, 7: 2}
        SAMPLE_USES = {2: 1, 3: 1, 4: 2, 5: 1, 6: 1, 7: 1}

        TILE_USES = {2: 1, 3: 1}
        PARTS = ((0, 2), (2, 3), (3, 4))

        def turns(eng, first, last):
            return eng.Fori(first, last) if last - first > 1 else nullcontext(first)

        def qkv_uses(q):
            return {0: q.nb, 1: q.nb, 2: 2, 3: 2}

        def lf_fills(banks, q):
            return [banks.take(5 + b) for b in range(q.nb)]

        def prep_fills(banks, q):
            columns = banks.take(5)
            pairs = [(6 + k % 2, banks.take(6 + k % 2)) for k in range(PAIRS * q.nb)]
            return columns, pairs, banks.take(4)

        def norm_fills(banks, q):
            return banks.take(4), [(5 + b, banks.take(5 + b)) for b in range(q.nb)]

        def embedding_fills(banks, q):
            return banks.take(7), [(6 + b % 2, banks.take(6 + b % 2)) for b in range(q.nb)]

        E_BLOCKS = {1: (0, 1), 2: (2,)}

        def qkv_skip(banks, q):
            for b in range(q.nb):
                banks.take(b % 2)
            lf_fills(banks, q)
            prep_fills(banks, q)
            banks.skip(qkv_uses(q), 4)
            if q.n == 0:
                banks.skip(TILE_USES)

        N_SMALL = 4 + 4 + 8 + 2 * PAIRS

        def small_outputs(sp):
            def out(dst, src):
                sp.dma_start(dst, src).then_inc(small_out, 16)

            out(C_prompt[0, 0].rearrange("(j hh) d e -> (hh d) j e", hh=2), state[:, :, 0:DV])
            out(n_prompt[0, 0].rearrange("(j hh) d -> (hh d) j", hh=2), state[:, :, DV])
            out(m_prompt[0, 0].rearrange("(h a) -> h a", a=1), carry[:, :])
            out(m_sample[0].rearrange("b h -> h b"), m_out[:, :])
            for c in range(4):
                out(conv_prompt[0, 0, :, c * P:(c + 1) * P].rearrange("w p -> p w"), hist[:, c, :])
                for w in range(2):
                    out(conv_sample[0, :, w, c * P:(c + 1) * P].rearrange("b p -> p b"), convs[:, c, :, w])
            for j in range(PAIRS):
                out(C_sample[0, :, 2 * j:2 * j + 2].rearrange("b hh d e -> (hh d) b e"), Cs[:, j, :, 0:DV])
                out(n_sample[0, :, 2 * j:2 * j + 2].rearrange("b hh d -> (hh d) b"), Cs[:, j, :, DV])

        @block.sync
        def _(sp):
            banks = Banks()

            def constants():
                sp.dma_start(bias8[0:NH, :], b_ig.rearrange("a h -> h a")).then_inc(consts_in, 16)
                sp.dma_start(bias8[NH:2 * NH, :], b_fg.rearrange("a h -> h a")).then_inc(consts_in, 16)
                for t, g in ((gffn, g_ffn[0]), (gple, g_ple[0]), (gmh, g_mh[0])):
                    sp.dma_start(t[:, :], g.rearrange("(c p) -> p c", p=P)).then_inc(consts_in, 16)
                for w in range(3):
                    sp.dma_start(cw[:, w, :], conv_w[0, w].rearrange("(c p) -> p c", p=P)).then_inc(consts_in, 16)
                sp.dma_start(ms0[:, :], state_m[0].rearrange("b h -> h b")).then_inc(consts_in, 16)
                for c in range(4):
                    for w in range(2):
                        sp.dma_start(convs[:, c, :, w], state_conv[0, :, w, c * P:(c + 1) * P].rearrange("b p -> p b"))\
                            .then_inc(consts_in, 16)

            def slab(s, p, src):
                sp.wait_ge(hi_done, s + 1)
                sp.wait_ge(lo_done, s + 1)
                sp.dma_start(wraw[p][:, :].rearrange("p (k n) -> p k n", k=src.shape[1]), src).then_inc(landed[p], 16)

            def first_slabs(q):
                for s, c0 in ((q.slab0, COL_G), (q.slab0 + 1, 0)):
                    slab(s, s % 2, w_in_v[:, :, c0:c0 + P])

            for t in range(NCH):
                sp.dma_start(xin[t][:, :], x_prompt[0, t * P:(t + 1) * P, :]).then_inc(x_in[t], 16)
                if t == 1:
                    first_slabs(supers[0])
                    sp.dma_start(gmix[:, :], g_mix[0].rearrange("(c p) -> p c", p=P)).then_inc(gmix_in, 16)
            constants()
            for q in supers:
                X, v, s0 = q.X, S[q.n], q.slab0
                par = s0 % 2
                if q.n == 0:
                    banks.skip(TILE_USES, NCH)
                    was_read(sp, banks, 2, 3)
                    sp.dma_start(stored_x[0][:, :, 0:q.T], q.home[:, :, 0:q.T]).then_inc(v["x_stored"], 16)
                    for p in range(2):
                        sp.dma_start(xs[p][:, :], x_prompt[0, TP + p * P:TP + (p + 1) * P, :])\
                            .then_inc(S[1][f"x_landed{p}"], 16)
                    banks.skip({5 + b: 1 for b in range(q.nb)})
                slab(s0 + 2, par, w_in_v[:, :, P:2 * P])
                tile0 = banks.n[3]

                with sp.Fori(0, 3) as i:
                    for p in range(2):
                        if q.n == 0:
                            src = x_prompt[0, ds(i * 2 * P + (TP + (2 + p) * P), P), :]
                            sp.wait_ge(free[3], tile0 + 2 * i + p + 2)
                            sp.dma_start(xs[p][:, :], src)\
                                .then_inc(S[1][f"x_landed{p}"], 16)
                        slab(s0 + 3 + p + 2 * i, (par + 3 + p) % 2, w_in_v[:, :, ds(i * 2 * P + (2 + p) * P, P)])
                        if q.n:
                            dst = y_prompt[0, ds(i * 2 * P + p * P, P), :]
                            sp.wait_ge(S[0]["y_gained"], 2 * i + p + 1)
                            sp.dma_start(dst, y_rows[:, :]).then_inc(S[0]["y_out0"], 16)
                if q.n == 0:
                    sp.wait_ge(free[3], tile0 + NCH)
                    sp.dma_start(xs[0][0:TS, :], x_sample.rearrange("b s d -> (b s) d")).then_inc(S[1]["x_landed0"], 16)
                slab(s0 + 9, (par + 9) % 2, w_in_v[:, :, COL_O:COL_O + P])
                if q.n:
                    for t in (NCH - 2, NCH - 1):
                        sp.wait_ge(S[0]["y_gained"], t + 1)
                        sp.dma_start(y_prompt[0, t * P:(t + 1) * P, :], y_rows[:, :]).then_inc(S[0]["y_out0"], 16)
                qkv_skip(banks, q)
                for first, last in ((0, 3), (3, 4)):
                    with turns(sp, first, last) as i:
                        for n, col in enumerate((COL_C, COL_H, COL_B, COL_O + P)):
                            if first == 0 or n < 3:
                                slab(s0 + 10 + n + 4 * i, (par + 10 + n) % 2, w_in_v[:, :, ds(i * P + col, P)])
                banks.skip({0: 8 * q.nb, 1: 8 * q.nb})
                banks.skip(CHUNK_USES, NCH)
                s = s0 + 25
                for p in range(2):
                    slab(s + p, (s + p) % 2, w_out_v[:, :, p * P:(p + 1) * P])
                if q.sample:
                    sp.wait_ge(v["conv_done"], 5)
                    for j in range(PAIRS):
                        sp.dma_start(Cs[:, j, :, 0:DV],
                                     state_C[0, :, 2 * j:2 * j + 2].rearrange("b hh d e -> (hh d) b e")).then_inc(states_in, 16)
                        sp.dma_start(Cs[:, j, :, DV],
                                     state_n[0, :, 2 * j:2 * j + 2].rearrange("b hh d -> (hh d) b")).then_inc(states_in, 16)
                sp.wait_ge(v["staged"], q.tiles)
                sp.wait_ge(v["x_stored"], 16 * (1 if q.n == 0 else q.tiles))
                sp.dma_start(X[:, 0:4, 0:q.T], stored_x[q.n][:, 0:4, 0:q.T]).then_inc(v["reload0"], 16)
                was_read(sp, banks, 0, 1, 7)
                if q.sample:
                    sp.dma_start(pst_s[0:TS, :], p_sample[0].rearrange("b s n -> (b s) n")).then_inc(v["p_landed"], 16)
                    banks.skip(SAMPLE_USES)
                    was_read(sp, banks, 4, 5)
                sp.dma_start(pst[:, :, :], p_prompt[0, 0, q.n * TP:(q.n + 1) * TP, :].rearrange("(t p) n -> p t n", p=P))\
                    .then_inc(v["p_landed"], 16)
                if q.sample:
                    banks.skip({2: 2, 3: 2, 6: 2})
                sp.wait_ge(v["merged"], 4 * q.nb)
                sp.dma_start(X[:, 4:8, 0:q.T], stored_x[q.n][:, 4:8, 0:q.T]).then_inc(v["reload1"], 16)
                with sp.Fori(1, 4) as i:
                    for p in range(2):
                        slab(s + p + 2 * i, (s + p) % 2, w_out_v[:, :, ds(i * 2 * P + p * P, P)])
                if q.sample:
                    was_read(sp, banks, 2, 3, 6)
                    small_outputs(sp)
                s += 8
                for p in range(2):
                    slab(s + p, (s + p) % 2, w_ple_v[:, :, p * 512:(p + 1) * 512])
                s += 2
                with sp.Fori(0, 4) as g:
                    for c in range(GROUP):
                        for p, w in enumerate((w_gate_v, w_up_v)):
                            slab(s + 2 * c + p + 12 * g, (s + p) % 2, w[:, :, ds(g * GROUP * P + c * P, P)])
                    for n in range(4):
                        slab(s + 8 + n + 12 * g, (s + n) % 2, w_down_v[:, ds(g * GROUP, GROUP), n * 256:(n + 1) * 256])
                s += 48
                for g, size in ((4, 4), (5, 2)):
                    for c in range(size):
                        ff = g * GROUP + c
                        for w in (w_gate_v, w_up_v):
                            slab(s, s % 2, w[:, :, ff * P:(ff + 1) * P])
                            s += 1
                    nw = SLAB // size
                    for n in range(D // nw):
                        slab(s, s % 2, w_down_v[:, g * GROUP:g * GROUP + size, n * nw:(n + 1) * nw])
                        s += 1
                for p in range(2):
                    slab(s + p, (s + p) % 2, w_pg_v[:, :, p * P:(p + 1) * P])
                for g in range(4):
                    banks.take(2 + g)
                if q.sample:
                    banks.take(6)
                banks.skip({0: 4 * q.nb, 1: 4 * q.nb})
                norm_fills(banks, q)
                banks.skip({0: 4 * q.nb, 1: 4 * q.nb})
                for b in range(q.nb):
                    banks.skip({b: FF, 3 + b: FF})
                embedding_fills(banks, q)
                banks.skip({6: 6 * 4 * q.nb, 7: 6 * 4 * q.nb})
                sp.wait_ge(v["e_done"], KC * q.nb)
                sp.dma_start(gain_row[:, :], g_final.rearrange("(a d) -> a d", a=1).to_broadcast([P, D])).then_inc(v["gain_in"], 16)
                if q.n == 0:
                    was_filled(sp, banks, 6, 7)
                    sp.wait_ge(S[1]["x_stored"], 16 * supers[1].tiles)
                    sp.dma_start(next_x[:, :, :], stored_x[1][:, :, :]).then_inc(S[1]["x_back"], 16)
                with sp.Fori(1, 4) as i:
                    for p in range(2):
                        slab(s + p + 2 * i, (s + p) % 2, w_pg_v[:, :, ds(i * 2 * P + p * P, P)])
                if q.n == 0:
                    banks.skip({5 + b: 1 for b in range(supers[1].nb)})
                banks.skip({0: 4 * q.nb, 1: 4 * q.nb})
                if q.n == 0:
                    first_slabs(supers[1])
            for t in range(q.tiles):
                for bk in (2 + 2 * (t % 3), 3 + 2 * (t % 3)):
                    sp.wait_ge(free[bk], banks.take(bk) + 1)
                if t < NCH:
                    dst, n = y_prompt[0, TP + t * P:TP + (t + 1) * P, :], P
                else:
                    dst, n = y_sample.rearrange("b s d -> (b s) d"), TS
                sp.dma_start(dst, y_end[t % 3][0:n, :]).then_inc(v[f"y_out{t % 3}"], 16)
            for p in range(3):
                sp.wait_ge(v[f"y_out{p}"], 16 * 3)
            sp.wait_ge(small_out, 16 * N_SMALL)

        @block.tensor
        def _(pe):
            banks = Banks()

            pe.sem_inc(slab_begun, 1)
            pe.wait_ge(consts_made, 1)

            def product(q, no, bk, p, kc, n, b, src=(AH, AL), begins=False, ready=None):
                b0, bl = q.blocks[b]
                pe.wait_ge(free[bk], no)
                hi = whi[p][:, :].rearrange("p (k n) -> p k n", k=kc)
                lo = wlo[p][:, :].rearrange("p (k n) -> p k n", k=kc)
                o, cols_ = bank[bk][:, 0:bl], slice(n * P, (n + 1) * P)
                for k in range(kc):
                    mh, ml = src[0][:, k, b0:b0 + bl], src[1][:, k, b0:b0 + bl]
                    if ready:
                        ready(b, k)
                    first = nc.tensor.matmul(o, hi[:, k, cols_], mh, start=k == 0, stop=False)
                    if begins and k == 0:
                        first.then_inc(slab_begun, 1)
                    nc.tensor.matmul(o, hi[:, k, cols_], ml, start=False, stop=False)
                    last = nc.tensor.matmul(o, lo[:, k, cols_], mh, start=False, stop=k == kc - 1)
                last.then_inc(full[bk], 1)

            def slab_ready(s):
                pe.wait_ge(lo_done, s + 3)

            def column_sums(q, fill, bk):
                pe.wait_ge(free[bk], fill)
                for t in range(q.tiles):
                    n = P if t < NCH else TS
                    last = nc.tensor.matmul(bank[bk][0:n, t:t + 1], ss[:, t * P:t * P + n], ones[:, 0:1],
                                            start=True, stop=True)
                last.then_inc(full[bk], 1)

            def chunk_scores(v, n0, c, n=P):
                f = ChunkFills(n0, c)
                mask = causal[:, :] if n == P else causal_s[:, :, :].rearrange("p b t -> p (b t)")
                pe.wait_ge(v["staged"], c + 1)
                pe.wait_ge(free[2], f.exponent)
                for h in range(NH):
                    e = bank[2][0:n, h * n:(h + 1) * n]
                    nc.tensor.matmul(e, identb[:, 0:n], mask, start=True, stop=False)
                    last = nc.tensor.matmul(e, pick[:, h:h + 1].to_broadcast([P, n]), rz[:, 0:n], start=False, stop=True)
                last.then_inc(full[2], 1)
                pe.wait_ge(free[3], f.score)
                for h in range(NH):
                    last = nc.tensor.matmul(bank[3][0:n, h * n:(h + 1) * n], kst[:, h // 2, 0:n], qz[:, h, 0:n],
                                            start=True, stop=True)
                last.then_inc(full[3], 1)
                pe.wait_ge(free[4], f.keys)
                for j in range(PAIRS):
                    last = nc.tensor.transpose(bank[4][0:n, j * P:(j + 1) * P], kst[:, j, 0:n], ident[:, :])
                last.then_inc(full[4], 1)
                pe.wait_ge(free[f.values_bank], f.values)
                for h in range(NH):
                    last = nc.tensor.transpose(bank[f.values_bank][0:n, h * P:(h + 1) * P], vst[:, h, 0:n], ident[:, :])
                last.then_inc(full[f.values_bank], 1)

            def chunk_outputs(v, n0, c):
                f = ChunkFills(n0, c)
                pe.wait_ge(free[3], f.score + 1)
                pe.wait_ge(free[7], f.values + 1)
                pe.wait_ge(free[6], f.state)
                for bk, no, hs in ((4, f.out01, (0, 1)), (5, f.out23, (2, 3))):
                    pe.wait_ge(free[bk], no)
                    for h in hs:
                        o = bank[bk][:, (h % 2) * (DV + 1):(h % 2 + 1) * (DV + 1)]
                        nc.tensor.matmul(o, Pm[:, h, :], V[:, h, :], start=True, stop=False)
                        last = nc.tensor.matmul(o, qwz[:, h, :], state[:, h // 2, :], start=False, stop=True)
                    last.then_inc(full[bk], 1)
                for h in range(NH):
                    r, j = DK * (h % 2), h // 2
                    last = nc.tensor.matmul(bank[6][r:r + DK, j * (DV + 1):(j + 1) * (DV + 1)], kw[:, h, :], V[:, h, :],
                                            start=True, stop=True)
                last.then_inc(full[6], 1)

            def chunk_transposes(v, n0, c, n=P):
                f = ChunkFills(n0, c)
                pe.wait_ge(free[4], f.out01 + 1)
                pe.wait_ge(free[5], f.out23 + 1)
                pe.wait_ge(free[7], f.h_t)
                for h in range(NH):
                    last = nc.tensor.transpose(bank[7][:, h * n:(h + 1) * n], hn[0:n, h, :], ident[0:n, 0:n])
                last.then_inc(full[7], 1)

            def linear(q, s, uses, ready, middle=None, first_block=None):
                parts = ((0, 4),)
                if middle:
                    parts = ((0, 1), (1, 2), (2, 4)) if first_block else ((0, 2), (2, 4))
                for first, last in parts:
                    with turns(pe, first, last) as i:
                        f = Fills(banks, i, uses)
                        k = 0
                        for p in range(2):
                            slab_ready(s + p + 2 * i)
                            for b in range(q.nb):
                                product(q, f.take(k % 2), k % 2, (s + p) % 2, KC, 0, b, begins=b == 0,
                                        ready=ready if p == 0 and first == 0 else None)
                                if first_block and first == 0 and k == 0:
                                    first_block()
                                k += 1
                    if middle and last == 2:
                        middle()
                banks.skip(uses, 4)

            def to_features(f, src, n=P):
                for bk in (2, 3):
                    pe.wait_ge(free[bk], f.take(bk))
                    for c in range(4):
                        cc = (bk - 2) * 4 + c
                        last = nc.tensor.transpose(bank[bk][:, c * n:(c + 1) * n], src[0:n, cc * P:(cc + 1) * P],
                                                   ident[0:n, 0:n])
                    last.then_inc(full[bk], 1)

            def to_tokens(f, src, t, bk0, n=P):
                for m in range(2):
                    pe.wait_ge(free[bk0 + m], f.take(bk0 + m))
                    for c in range(4):
                        last = nc.tensor.transpose(bank[bk0 + m][0:n, c * P:(c + 1) * P],
                                                   src[:, m * 4 + c, t * P:t * P + n], ident[:, :])
                    last.then_inc(full[bk0 + m], 1)

            def spread_roots(q, b, bk, no, roots):
                b0, bl = q.blocks[b]
                pe.wait_ge(free[bk], no)
                for t in range(b0 // P, (b0 + bl - 1) // P + 1):
                    a, z = max(b0, t * P), min(b0 + bl, (t + 1) * P)
                    n = P if t < NCH else TS
                    last = nc.tensor.matmul(bank[bk][:, a - b0:z - b0], roots[0:n, t:t + 1].to_broadcast([n, P]),
                                            ident[0:n, a - t * P:z - t * P], start=True, stop=True)
                last.then_inc(full[bk], 1)

            for q in supers:
                X, U, v, s0, nb = q.X, q.U, S[q.n], q.slab0, q.nb
                par = s0 % 2
                uses = {0: nb, 1: nb}

                if q.n == 0:
                    for t in range(NCH):
                        pe.wait_ge(x_in[t], 16)
                        to_features(banks, xin[t])
                        if t % 4 == 3:
                            pe.wait_ge(v["x_root"], t // 4 + 1)
                            spread_roots(q, t // 4, 5 + t // 4, banks.take(5 + t // 4), x_roots)

                slab_ready(s0)
                for b in range(nb):
                    product(q, banks.take(b % 2), b % 2, par, KC, 0, b, begins=b == 0,
                            ready=lambda b, k: pe.wait_ge(v["low"], KC * b + k + 1))
                was_read(pe, banks, 0, 1)
                for b, no in enumerate(lf_fills(banks, q)):
                    b0, bl = q.blocks[b]
                    pe.wait_ge(free[5 + b], no)
                    nc.tensor.matmul(bank[5 + b][0:NH, 0:bl], ident[0:2 * NH, NH:2 * NH], G[0:2 * NH, b0:b0 + bl],
                                     start=True, stop=True).then_inc(full[5 + b], 1)

                def gate_rows():
                    columns, pairs, over_chunk = prep_fills(banks, q)
                    pe.wait_ge(v["rows_exp"], 3)
                    pe.wait_ge(free[5], columns)
                    for r, row in enumerate((CS, LF, EM)):
                        for t in range(q.tiles):
                            n = P if t < NCH else TS
                            col = (r * (NCH + 1) + t) * NH
                            last = nc.tensor.transpose(bank[5][0:n, col:col + NH], row[0:NH, t * P:t * P + n],
                                                       ident[0:NH, 0:NH])
                    last.then_inc(full[5], 1)
                    k = 0
                    for j in range(PAIRS):
                        for b0, bl in q.blocks:
                            bk, no = pairs[k]
                            pe.wait_ge(free[bk], no)
                            nc.tensor.matmul(bank[bk][:, 0:bl], pair_rows[:, j, :], W[0:NH, b0:b0 + bl], start=True,
                                             stop=True).then_inc(full[bk], 1)
                            k += 1
                    pe.wait_ge(free[4], over_chunk)
                    for j in range(PAIRS):
                        c0 = j * (NCH + NB_S)
                        last = nc.tensor.matmul(bank[4][:, c0:c0 + NCH], pair_rows[:, j, :], W[0:NH, P - 1:TP:P],
                                                start=True, stop=True)
                        if q.sample:
                            last = nc.tensor.matmul(bank[4][:, c0 + NCH:c0 + NCH + NB_S], pair_rows[:, j, :],
                                                    W[0:NH, TP + NT_S - 1:TM:NT_S], start=True, stop=True)
                    last.then_inc(full[4], 1)

                for part in PARTS:
                    with turns(pe, *part) as i:
                        f = Fills(banks, i, qkv_uses(q))
                        k = 0
                        for p in range(2):
                            if q.n == 0:
                                pe.wait_ge(S[1][f"x_landed{p}"], 16 * i + 16)
                                to_features(f, xs[p])
                            else:
                                pe.wait_ge(S[0]["y_staged"], 2 * i + p + 1)
                                to_tokens(f, y_stage, 0, 2)
                            slab_ready(s0 + 1 + p + 2 * i)
                            for b in range(nb):
                                product(q, f.take(k % 2), k % 2, (par + 1 + p) % 2, KC, 0, b, begins=b == 0)
                                k += 1
                    if part[1] == 3:
                        gate_rows()
                banks.skip(qkv_uses(q), 4)
                if q.n == 0:
                    pe.wait_ge(S[1]["x_landed0"], 16 * (NCH // 2 + 1))
                    to_features(banks, xs[0], TS)

                n0 = list(banks.n)
                loop_uses = {0: 2 * nb, 1: 2 * nb}
                def mixer_turn(i, after_block=None):
                    f = Fills(banks, i, loop_uses)
                    k = nb % 2
                    for n in range(4):
                        c = 2 * i + n // 2
                        if n % 2 == 0:
                            chunk_scores(v, n0, c)
                        else:
                            chunk_outputs(v, n0, c)
                        slab_ready(s0 + 9 + n + 4 * i)
                        for b in range(nb):
                            product(q, f.take(k % 2), k % 2, (par + 9 + n) % 2, KC, 0, b, begins=b == 0)
                            k += 1
                            if after_block:
                                after_block(n, b)
                        if n % 2:
                            chunk_transposes(v, n0, c)

                def sample_scores(n, b):
                    if (n, b) == (3, 0):
                        chunk_scores(v, n0, NCH, TS)

                def sample_states(j):
                    for g, b0 in enumerate((0, 3, 6)):
                        bk = (2, 3, 6)[g]
                        pe.wait_ge(free[bk], banks.take(bk))
                        for hh in range(2):
                            for b in range(b0, min(b0 + 3, NB_S)):
                                o = bank[bk][hh * DK:(hh + 1) * DK, (b - b0) * (DV + 1):(b - b0 + 1) * (DV + 1)]
                                last = nc.tensor.matmul(o, kwb[:, 2 * j + hh, b, :], V[0:TS, 2 * j + hh, :],
                                                        start=True, stop=True)
                        last.then_inc(full[bk], 1)

                with pe.Fori(0, 4 - q.sample) as i:
                    mixer_turn(i)
                if q.sample:
                    mixer_turn(3, sample_scores)
                banks.skip(loop_uses, 4)
                banks.skip(CHUNK_USES, NCH)
                if q.sample:
                    f = ChunkFills(n0, NCH)
                    pe.wait_ge(free[3], f.score + 1)
                    pe.wait_ge(free[f.values_bank], f.values + 1)
                    pe.wait_ge(batch_queries, 2)
                    pe.wait_ge(states_in, 16 * 2 * PAIRS)
                    for bk, no, hs in ((4, f.out01, (0, 1)), (5, f.out23, (2, 3))):
                        pe.wait_ge(free[bk], no)
                        for h in hs:
                            o = bank[bk][0:TS, (h % 2) * (DV + 1):(h % 2 + 1) * (DV + 1)]
                            nc.tensor.matmul(o, Pm[:, h, 0:TS], V[:, h, :], start=True, stop=False)
                            for b in range(NB_S):
                                last = nc.tensor.matmul(o, qb[:, h, b, :], Cs[:, h // 2, b, :], start=False,
                                                        stop=b == NB_S - 1)
                        last.then_inc(full[bk], 1)
                    pe.wait_ge(batch_keys, NH)
                    banks.skip(SAMPLE_USES)
                    sample_states(0)

                def embedding_tokens():
                    if q.sample:
                        sample_states(1)
                    pe.wait_ge(v["p_landed"], 16 * (1 + q.sample))
                    for g in range(NCH // 2):
                        bk = 2 + g
                        pe.wait_ge(free[bk], banks.take(bk))
                        for t in range(2):
                            for c in range(2):
                                o = bank[bk][:, (2 * t + c) * P:(2 * t + c + 1) * P]
                                last = nc.tensor.transpose(o, pst[:, 2 * g + t, c * P:(c + 1) * P], ident[:, :])
                        last.then_inc(full[bk], 1)
                    if q.sample:
                        pe.wait_ge(free[6], banks.take(6))
                        for c in range(2):
                            last = nc.tensor.transpose(bank[6][:, c * TS:(c + 1) * TS], pst_s[0:TS, c * P:(c + 1) * P],
                                                       ident[0:TS, 0:TS])
                        last.then_inc(full[6], 1)

                s = s0 + 25
                linear(q, s, uses, lambda b, k: pe.wait_ge(v["mix_lo"], KC * b + k + 1), middle=embedding_tokens,
                       first_block=(lambda: chunk_transposes(v, n0, NCH, TS)) if q.sample else None)
                s += 8
                was_read(pe, banks, 2, 3, 4, 5, 6)
                k = 0
                for p in range(2):
                    slab_ready(s)
                    for n in range(4):
                        for b in range(nb):
                            product(q, banks.take(k % 2), k % 2, s % 2, 2, n, b, (hid[:, 0], hid[:, 1]),
                                    begins=n == 0 and b == 0)
                            k += 1
                        if p == 0 and n == 0:
                            columns, spread = norm_fills(banks, q)
                            pe.wait_ge(v["res_sum"], KC * nb + 2)
                            column_sums(q, columns, 4)
                        if p == 0 and n == 1:
                            pe.wait_ge(v["res_root"], q.tiles - NCH + 1)
                            for b in range(nb):
                                spread_roots(q, b, *spread[b], mean_roots)
                    s += 1

                def normed_ready(b, k):
                    pe.wait_ge(v["low2"], KC * b + k + 1)

                def up_chunk(f, s, p, first):
                    for w in range(2):
                        slab_ready(s + w)
                        for b in range(nb):
                            product(q, f.take(3 * w + b), 3 * w + b, (p + w) % 2, KC, 0, b, begins=b == 0,
                                    ready=normed_ready if first and w == 0 else None)

                def down(f, s, p, size, before):
                    def hidden_ready(b, k):
                        pe.wait_ge(v["h_lo"], nb * (before + 1) + nb * k + b + 1)

                    nw = SLAB // size // P
                    k = 0
                    for m in range(KC // nw):
                        slab_ready(s + m)
                        for n in range(nw):
                            for b in range(nb):
                                product(q, f.take(6 + k % 2), 6 + k % 2, (p + m) % 2, size, n, b, (hid[:, 0], hid[:, 1]),
                                        begins=n == 0 and b == 0, ready=hidden_ready if m == 0 and n == 0 else None)
                                k += 1

                ffn_uses = {b: 4 for b in range(nb)}
                ffn_uses.update({3 + b: 4 for b in range(nb)})
                ffn_uses.update({6: 4 * nb, 7: 4 * nb})
                with pe.Fori(0, 4) as g:
                    f = Fills(banks, g, ffn_uses)
                    for c in range(GROUP):
                        up_chunk(f, s + 2 * c + 12 * g, s % 2, c == 0)
                    down(f, s + 8 + 12 * g, s % 2, GROUP, GROUP * g)
                banks.skip(ffn_uses, 4)
                s += 48
                for size, before in ((4, 16), (2, 20)):
                    for c in range(size):
                        up_chunk(banks, s, s % 2, False)
                        s += 2
                        if size == 4 and c == 0:
                            columns, spread = embedding_fills(banks, q)
                            pe.wait_ge(v["e_sum"], KC * nb + 2)
                            column_sums(q, columns, 7)
                        if size == 4 and c in E_BLOCKS:
                            pe.wait_ge(v["e_root"], q.tiles - NCH + 1)
                            for b in E_BLOCKS[c][:nb - E_BLOCKS[c][0]]:
                                spread_roots(q, b, *spread[b], mean_roots)
                    down(banks, s, s % 2, size, before)
                    s += size

                def next_roots():
                    pe.wait_ge(S[1]["x_root"], 2)
                    for b in range(supers[1].nb):
                        spread_roots(supers[1], b, 5 + b, banks.take(5 + b), x_roots)

                linear(q, s, uses, lambda b, k: pe.wait_ge(v["x3_lo"], k * nb + b + 1),
                       middle=next_roots if q.n == 0 else None)
                s += 8
                assert s == s0 + SLABS
            for t in range(q.tiles):
                n = P if t < NCH else TS
                pe.wait_ge(v["x4"], nb + (KC - 1) * nb + (t * P + n - 1) // q.blocks[0][1] + 1)
                to_tokens(banks, X, t, 2 + 2 * (t % 3), n)

        @block.scalar
        def _(act):
            banks = Banks()
            act.sem_inc(hi_done, 2)
            act.wait_ge(consts_made, 1)

            def next_high(s, i=0, step=0):
                p = s % 2
                act.wait_ge(landed[p], 16 * (s // 2 + 1) + 8 * step * i)
                act.wait_ge(slab_begun, s + 1 + step * i)
                nc.scalar.activation(whi[p][:, :], wraw[p][:, :], ACT.Copy).then_inc(hi_done, 1)

            def high_of_normed(v, q, m, normed, high):
                c, (b0, bl) = m % KC, q.blocks[m // KC]
                act.wait_ge(v[normed], m + 1)
                src = next_x[:, c, b0:b0 + bl] if normed == "normed" and q.n else tmp[m % 3][:, 0:bl]
                nc.scalar.activation(AH[:, c, b0:b0 + bl], src, ACT.Copy).then_inc(v[high], 1)

            def chunk_exps(v, n0, c, p, n=P):
                f = ChunkFills(n0, c)
                act.wait_ge(v["staged"], c + 1)
                act.wait_ge(free[5], f.out23)
                act.wait_ge(full[2], f.exponent)
                for h in range(NH):
                    last = nc.scalar.activation(expE[0:n, h, 0:n], bank[2][0:n, h * n:(h + 1) * n], ACT.Exp,
                                                bias=colst[p][0:n, h:h + 1])
                last.then_inc(free[2], 1)
                bk = f.values_bank
                act.wait_ge(full[bk], f.values)
                nc.scalar.activation(V[0:n, :, 0:DV], bank[bk][0:n, :].rearrange("p (h e) -> p h e", h=NH), ACT.Copy)\
                    .then_inc(free[bk], 1)

            def chunk_squares(v, n0, c, n=P):
                f = ChunkFills(n0, c)
                act.wait_ge(free[3], f.score + 1)
                for bk, no, hs in ((4, f.out01, (0, 1)), (5, f.out23, (2, 3))):
                    act.wait_ge(full[bk], no)
                    for h in hs:
                        o = (h % 2) * (DV + 1)
                        last = nc.scalar.activation(expE[0:n, h, :], bank[bk][0:n, o:o + DV], ACT.Square,
                                                    scale=DV ** -0.5, accum_out=ss4[0:n, h:h + 1])
                last.then_inc(v["sq_done"], 1)

            def chunk_out(n0, c, tok, n=P):
                act.wait_ge(full[7], ChunkFills(n0, c).h_t)
                for h in range(NH):
                    last = nc.scalar.activation(X[:, 4 + h, tok], bank[7][:, h * n:(h + 1) * n], ACT.Copy,
                                                scale=gmh[:, h:h + 1])
                last.then_inc(free[7], 1)

            for q in supers:
                X, U, v, s0, nb = q.X, q.U, S[q.n], q.slab0, q.nb
                uses = {0: nb, 1: nb}
                if q.n == 0:
                    for t in range(NCH):
                        act.wait_ge(x_in[t], 16)
                        nc.scalar.activation(X[:, t, 0:D], xin[t][:, :], ACT.Square, accum_out=x_sums[:, t:t + 1])\
                            .then_inc(v["x_sq"], 1)
                        act.wait_ge(full[2], banks.take(2))
                        banks.take(3)
                        nc.scalar.activation(q.home[:, 0:4, t * P:(t + 1) * P],
                                             bank[2][:, :].rearrange("p (c t) -> p c t", c=4), ACT.Copy).then_inc(free[2], 1)
                        if t == 2:
                            next_high(0)
                        if t >= 4:
                            for m in (2 * (t - 4), 2 * (t - 4) + 1):
                                high_of_normed(v, q, m, "normed", "high")
                    for b in range(nb):
                        banks.take(5 + b)
                    for m in range(KC, KC * nb):
                        high_of_normed(v, q, m, "normed", "high")
                else:
                    act.wait_ge(S[0]["x4"], supers[0].nb * (KC + 1))
                    act.wait_ge(v["low"], KC * nb)
                    nc.scalar.activation(y_stage[:, :, :], U[:, :, 0:P], ACT.Copy).then_inc(S[0]["y_staged"], 1)

                next_high(s0 + 1)
                for b in range(nb):
                    banks.take(b % 2)
                for b, no in enumerate(lf_fills(banks, q)):
                    b0, bl = q.blocks[b]
                    act.wait_ge(full[5 + b], no)
                    nc.scalar.activation(EM[0:NH, b0:b0 + bl], bank[5 + b][0:NH, 0:bl], ACT.Abs).then_inc(v["lf_abs"], 1)
                nc.scalar.activation(G[0:NH, 0:q.T], G[0:NH, 0:q.T], ACT.Tanh, scale=1.0 / GATE_CAP).then_inc(v["softcap"], 1)
                act.wait_ge(v["lf_abs"], nb)
                nc.scalar.activation(EM[0:NH, 0:q.T], EM[0:NH, 0:q.T], ACT.Exp, scale=-1.0).then_inc(v["lf_abs"], 1)
                act.wait_ge(v["lf_abs"], nb + 1)
                nc.scalar.activation(EM[0:NH, 0:q.T], EM[0:NH, 0:q.T], ACT.Ln, bias=1.0).then_inc(v["lf_soft"], 1)

                def next_tile(f, i, p, n=P):
                    t = 2 * i + p
                    w = S[1]
                    act.wait_ge(w[f"x_landed{p}"], 16 * i + 16)
                    act.wait_ge(w["x_kept"], t + 1)
                    nc.scalar.activation(squares[0:n, :], xs[p][0:n, :], ACT.Square, accum_out=sq_tile[0:n, 0:1])\
                        .then_inc(w["x_sq"], 1)
                    tok = ds(t * P, P) if n == P else slice(TP, TM)
                    last = [f.take(2), f.take(3)]
                    for m in range(2):
                        act.wait_ge(full[2 + m], last[m])
                        nc.scalar.activation(wide1[:, 4 * m:4 * m + 4, tok],
                                             bank[2 + m][:, 0:4 * n].rearrange("p (c t) -> p c t", c=4), ACT.Copy)\
                            .then_inc(free[2 + m], 1)
                    for m in range(2):
                        act.wait_ge(free[2 + m], last[m] + 1)
                    act.dma_start(stored_x[1][:, :, tok], wide1[:, :, tok]).then_inc(w["x_stored"], 16)

                def finished_tile(f, i, p, stage_next):
                    w, t = S[0], 2 * i + p
                    last = [f.take(2), f.take(3)]
                    for m in range(2):
                        act.wait_ge(full[2 + m], last[m])
                    for m in range(2):
                        nc.scalar.activation(y_stage[:, 4 * m:4 * m + 4, :], bank[2 + m][:, :].rearrange("p (c t) -> p c t", c=4),
                                             ACT.Square, scale=D ** -0.5, accum_out=y_sums[:, 0, m:m + 1])\
                            .then_inc(w["y_sq"], 1)
                    if stage_next:
                        act.wait_ge(w["y_sq"], 2 * t + 2)
                        nc.scalar.activation(y_stage[:, :, :], U[:, :, ds((t + 1) * P, P)], ACT.Copy).then_inc(w["y_staged"], 1)
                    act.wait_ge(w["y_root"], t + 1)
                    act.wait_ge(w["y_out0"], 16 * t + 16)
                    for m in range(2):
                        nc.scalar.activation(y_rows[:, m * 512:(m + 1) * 512], bank[2 + m][:, :], ACT.Copy,
                                             scale=y_roots[:, 0, 0:1]).then_inc(free[2 + m], 1)

                if q.n == 0:
                    act.wait_ge(v["x_stored"], 16)
                    act.wait_ge(v["low"], KC * nb)
                for part in PARTS:
                    with turns(act, *part) as i:
                        f = Fills(banks, i, qkv_uses(q))
                        k = 0
                        for p in range(2):
                            if q.n == 0:
                                next_tile(f, i, p)
                            else:
                                finished_tile(f, i, p, not (part[0] == 3 and p))
                            next_high(s0 + p + 2, i, 2)
                            for b0, bl in q.blocks:
                                act.wait_ge(full[k % 2], f.take(k % 2))
                                nc.scalar.activation(X[:, 2 * i + p, b0:b0 + bl], bank[k % 2][:, 0:bl], ACT.Copy)\
                                    .then_inc(free[k % 2], 1)
                                k += 1
                    if part[1] == 2:
                        act.wait_ge(v["rows_made"], 1)
                        for row, src, scale in ((EM, M, -1.0), (W, W, 1.0), (LF, LF, 1.0)):
                            nc.scalar.activation(row[0:NH, 0:q.T], src[0:NH, 0:q.T], ACT.Exp, scale=scale)\
                                .then_inc(v["rows_exp"], 1)
                    if part[1] == 3:
                        prep_fills(banks, q)
                banks.skip(qkv_uses(q), 4)
                if q.n == 0:
                    next_tile(banks, NCH // 2, 0, TS)
                    act.wait_ge(S[1]["x_stored"], 16 * supers[1].tiles)
                else:
                    act.wait_ge(S[0]["y_out0"], 16 * (NCH + 1))

                n0 = list(banks.n)
                loop_uses = {0: 2 * nb, 1: 2 * nb}
                def mixer_turn(i, sample=False):
                    f = Fills(banks, i, loop_uses)
                    k = nb % 2
                    for n in range(4):
                        c = 2 * i + n // 2
                        next_high(s0 + 10 + n, i, 4)
                        if n % 2 == 0:
                            chunk_exps(v, n0, c, n // 2)
                        else:
                            chunk_squares(v, n0, c)
                        if sample and n == 3:
                            chunk_exps(v, n0, NCH, 0, TS)
                        for b0, bl in q.blocks:
                            no = f.take(k % 2)
                            if n < 2:
                                act.wait_ge(full[k % 2], no)
                                if n == 1:
                                    act.wait_ge(v["conv_done"], i + 1)
                                    dst, func = zbuf[:, 2 + b0:2 + b0 + bl], ACT.Copy
                                else:
                                    dst, func = U[:, i, b0:b0 + bl], ACT.Sigmoid
                                nc.scalar.activation(dst, bank[k % 2][:, 0:bl], func).then_inc(free[k % 2], 1)
                            k += 1
                        if n % 2:
                            chunk_out(n0, c, ds(c * P, P) if not sample else slice(c * P, (c + 1) * P))

                with act.Fori(0, 4 - q.sample) as i:
                    mixer_turn(i)
                if q.sample:
                    mixer_turn(3, True)
                banks.skip(loop_uses, 4)
                banks.skip(CHUNK_USES, NCH)

                def mix_high(b):
                    b0, bl = q.blocks[b]
                    for m in range(KC):
                        if m < NH:
                            act.wait_ge(v["merged"], NH * b + m + 1)
                        nc.scalar.activation(AH[:, m, b0:b0 + bl], U[:, m, b0:b0 + bl], ACT.Copy).then_inc(v["mix_hi"], 1)

                was_filled(act, banks, 0, 1)
                was_read(act, banks, 0, 1)
                for b in range(nb):
                    mix_high(b)
                    if q.sample and b == 0:
                        chunk_squares(v, n0, NCH, TS)
                    if q.sample and b == 1:
                        chunk_out(n0, NCH, slice(TP, TM), TS)
                if q.sample:
                    banks.skip(SAMPLE_USES)
                    banks.skip({2: 2, 3: 2, 6: 2})

                def embedding_high():
                    for g in range(NCH // 2):
                        act.wait_ge(full[2 + g], banks.take(2 + g))
                        src = bank[2 + g][:, :].rearrange("p (t c n) -> p c t n", t=2, c=2)
                        dst = hid[:, 0, 0:2, 2 * g * P:(2 * g + 2) * P].rearrange("p c (t n) -> p c t n", t=2)
                        nc.scalar.activation(dst, src, ACT.Copy).then_inc(v["p_hi"], 1)
                    if q.sample:
                        act.wait_ge(full[6], banks.take(6))
                        nc.scalar.activation(hid[:, 0, 0:2, TP:TM], bank[6][:, 0:2 * TS].rearrange("p (c n) -> p c n", c=2),
                                             ACT.Copy).then_inc(v["p_hi"], 1)

                s = s0 + 25
                for first, last in ((0, 2), (2, 4)):
                    with act.Fori(first, last) as i:
                        f = Fills(banks, i, uses)
                        k = 0
                        for p in range(2):
                            next_high(s + p + 1, i, 2)
                            for b0, bl in q.blocks:
                                act.wait_ge(free[k % 2], f.take(k % 2) + 1)
                                act.wait_ge(v["res_sum"], k + 1 + 2 * nb * i)
                                nc.scalar.activation(tmp[k % 2][:, 0:bl], X[:, 2 * i + p, b0:b0 + bl], ACT.Square)\
                                    .then_inc(v["res_sq"], 1)
                                k += 1
                    if last == 2:
                        embedding_high()
                banks.skip(uses, 4)
                s += 8
                def embedding_out(m):
                    if m % (4 * nb) == 0:
                        next_high(s + 1 + m // (4 * nb))
                    b0, bl = q.blocks[m % nb]
                    act.wait_ge(full[m % 2], banks.take(m % 2))
                    nc.scalar.activation(U[:, m // nb, b0:b0 + bl], bank[m % 2][:, 0:bl], ACT.Copy).then_inc(free[m % 2], 1)

                for m in range(2 * nb):
                    embedding_out(m)
                for m in range(KC * nb):
                    if m + 2 * nb < KC * nb:
                        embedding_out(m + 2 * nb)
                    high_of_normed(v, q, m, "normed2", "high2")
                s += 2
                norm_fills(banks, q)

                def up_chunk(f, s, i, hc, count):
                    next_high(s + 1, i, 12)
                    for b, (b0, bl) in enumerate(q.blocks):
                        act.wait_ge(full[b], f.take(b))
                        act.wait_ge(v["h_lo"], count + b + 1)
                        nc.scalar.activation(sl[:, b0:b0 + bl], bank[b][:, 0:bl], ACT.Silu).then_inc(free[b], 1)
                    next_high(s + 2, i, 12)
                    for b, (b0, bl) in enumerate(q.blocks):
                        act.wait_ge(free[3 + b], f.take(3 + b) + 1)
                        nc.scalar.activation(hid[:, 0, hc, b0:b0 + bl], sl[:, b0:b0 + bl], ACT.Copy).then_inc(v["h_hi"], 1)

                ffn_uses = {b: 4 for b in range(nb)}
                ffn_uses.update({3 + b: 4 for b in range(nb)})
                ffn_uses.update({6: 4 * nb, 7: 4 * nb})
                if q.sample:
                    act.wait_ge(small_out, 16 * N_SMALL)
                with act.Fori(0, 4) as g:
                    f = Fills(banks, g, ffn_uses)
                    for c in range(GROUP):
                        up_chunk(f, s + 2 * c, g, c, nb * (c + GROUP * g))
                    k = 0
                    for n in range(4):
                        next_high(s + 9 + n, g, 12)
                        if n >= 2:
                            for b0, bl in q.blocks:
                                act.wait_ge(v["e_sum"], k + 1 + 2 * nb * g)
                                nc.scalar.activation(tmp[k % 2][:, 0:bl], U[:, 2 * g + n - 2, b0:b0 + bl], ACT.Square)\
                                    .then_inc(v["e_sq"], 1)
                                k += 1
                banks.skip(ffn_uses, 4)
                s += 48
                count = 16 * nb
                for size in (4, 2):
                    for c in range(size):
                        up_chunk(banks, s, 0, c, count)
                        count += nb
                        s += 2
                        if size == 4 and c == 0:
                            embedding_fills(banks, q)
                    k = 0
                    for m in range(size):
                        next_high(s + 1)
                        for n in range(KC // size * nb):
                            no = banks.take(6 + k % 2)
                            if size == 2:
                                c, (b0, bl) = k // nb, q.blocks[k % nb]
                                act.wait_ge(free[6 + k % 2], no + 1)
                                nc.scalar.activation(AH[:, c, b0:b0 + bl], X[:, c, b0:b0 + bl], ACT.Copy).then_inc(v["x3_hi"], 1)
                            k += 1
                        s += 1

                def gate_block(no, i, k, b):
                    b0, bl = q.blocks[b]
                    act.wait_ge(full[k % 2], no)
                    act.wait_ge(v["x4"], k + 1 + 2 * nb * i)
                    nc.scalar.activation(sl[:, b0:b0 + bl], bank[k % 2][:, 0:bl], ACT.Sigmoid).then_inc(free[k % 2], 1)

                with act.Fori(0, 3) as i:
                    f = Fills(banks, i, uses)
                    for p in range(2):
                        next_high(s + p + 1, i, 2)
                        for b in range(nb):
                            k = p * nb + b
                            gate_block(f.take(k % 2), i, k, b)
                banks.skip(uses, 3)
                for p in range(2):
                    if p == 0 or q.n == 0:
                        next_high(s + 6 + p + 1)
                    for b in range(nb):
                        k = p * nb + b
                        gate_block(banks.take(k % 2), 3, k, b)
                        if q.n == 0 and p == 1:
                            for m in range(KC * b, KC * (b + 1 if b < nb - 1 else supers[1].nb)):
                                high_of_normed(S[1], supers[1], m, "normed", "high")
                if q.n == 0:
                    for b in range(supers[1].nb):
                        banks.take(5 + b)

            for t in range(q.tiles):
                n = P if t < NCH else TS
                for m in range(2):
                    bk = 2 + 2 * (t % 3) + m
                    act.wait_ge(full[bk], banks.take(bk))
                    if t >= 3:
                        act.wait_ge(v["y_root"], t - 2)
                    nc.scalar.activation(y_squares[0:n, t % 3, m, :], bank[bk][0:n, :], ACT.Square, scale=D ** -0.5,
                                         accum_out=y_sums[0:n, t % 3, m:m + 1]).then_inc(v["y_sq"], 1)

        @block.vector
        def _(dve):
            banks = Banks()
            for b in range(8):
                dve.sem_inc(free[b], 1)
            for q in supers:
                dve.sem_inc(S[q.n]["h_lo"], q.nb)
                dve.sem_inc(S[q.n]["x4"], q.nb)
                dve.sem_inc(S[q.n]["conv_done"], 1)
            dve.sem_inc(S[0]["y_out0"], 16)
            dve.wait_ge(consts_made, 1)
            own = Chain(dve, dve_own)

            def copy_at(out, in_):
                return nc.vector.tensor_scalar(out, in_, 1.0, None, ALU.mult)

            class Normalised:

                def __init__(self, q, x, g, root, normed, high, low):
                    self.q, self.v, self.x, self.g, self.root = q, S[q.n], x, g, root
                    self.normed, self.high, self.low = normed, high, low
                    self.m = 0

                def low_part(self, m):
                    c, (b0, bl) = m % KC, self.q.blocks[m // KC]
                    dve.wait_ge(self.v[self.high], m + 1)
                    nc.vector.tensor_tensor(AL[:, c, b0:b0 + bl], tmp[m % 3][:, 0:bl], AH[:, c, b0:b0 + bl],
                                            ALU.subtract).then_inc(self.v[self.low], 1)

                def step(self, count):
                    for m in range(self.m, self.m + count):
                        c, b, (b0, bl) = m % KC, m // KC, self.q.blocks[m // KC]
                        if c == 0:
                            self.roots = self.root(b)
                        if m >= 3:
                            dve.wait_ge(self.v[self.low], m - 2)
                        nc.vector.scalar_tensor_tensor(tmp[m % 3][:, 0:bl], self.x[:, c, b0:b0 + bl], self.g[:, c:c + 1],
                                                       self.roots, ALU.mult, ALU.mult).then_inc(self.v[self.normed], 1)
                        if m:
                            self.low_part(m - 1)
                    self.m += count
                    if self.m == KC * self.q.nb:
                        self.low_part(self.m - 1)

            def chunk_weights(v, n0, c, p, n=P):
                f = ChunkFills(n0, c)
                dve.wait_ge(free[2], f.exponent + 1)
                dve.wait_ge(full[3], f.score)
                nc.vector.scalar_tensor_tensor(Pm[0:n, :, 0:n], bank[3][0:n, 0:NH * n].rearrange("p (h t) -> p h t", h=NH),
                                               QSCALE, expE[0:n, :, 0:n], ALU.mult, ALU.mult)\
                    .then_inc(free[3], 1)
                dve.wait_ge(full[4], f.keys)
                nc.vector.tensor_tensor(kw[0:n, :, :], bank[4][0:n, 0:NH * DK].rearrange("p (h d) -> p h d", h=NH),
                                        colst[p][0:n, 4:8].unsqueeze(2).to_broadcast([n, NH, DK]), ALU.mult)\
                    .then_inc(free[4], 1)

            def chunk_heads(v, n0, c, p, n=P):
                f = ChunkFills(n0, c)
                dve.wait_ge(v["sq_done"], c + 1)
                for bk, no, h in ((4, f.out01, 0), (5, f.out23, 2)):
                    dve.wait_ge(full[bk], no)
                    den = bank[bk][0:n, 0:2 * (DV + 1)].rearrange("p (h e) -> p h e", h=2)[:, :, DV]
                    own.link(nc.vector.scalar_tensor_tensor(dm[0:n, h:h + 2], den, -1.0, colst[p][0:n, 8 + h:10 + h],
                                                            ALU.mult, ALU.max))
                    own.link(nc.vector.tensor_tensor(dm[0:n, h:h + 2], den, dm[0:n, h:h + 2], ALU.max))
                own.link(nc.vector.scalar_tensor_tensor(d2[0:n, :], dm[0:n, :], EPS, dm[0:n, :], ALU.mult, ALU.mult))
                nc.vector.tensor_tensor(tt[0:n, :], d2[0:n, :], ss4[0:n, :], ALU.add).then_inc(v["root_in"], 1)
                dve.wait_ge(v["root_done"], c + 1)
                for bk, h in ((4, 0), (5, 2)):
                    num = bank[bk][0:n, 0:2 * (DV + 1)].rearrange("p (h e) -> p h e", h=2)[:, :, 0:DV]
                    nc.vector.tensor_tensor(hn[0:n, h:h + 2, :], num, rr[0:n, h:h + 2].unsqueeze(2).to_broadcast([n, 2, DV]),
                                            ALU.mult).then_inc(free[bk], 1)

            for q in supers:
                X, U, v, s0, nb = q.X, q.U, S[q.n], q.slab0, q.nb
                T = q.T
                uses = {0: nb, 1: nb}
                if q.n == 0:
                    fills = [banks.take(5 + b) for b in range(nb)]

                    def root(b):
                        dve.wait_ge(full[5 + b], fills[b])
                        return bank[5 + b][:, 0:q.blocks[b][1]]

                    x_norm = Normalised(q, q.home, gmix, root, "normed", "high", "low")
                    for t in range(NCH):
                        banks.take(2)
                        dve.wait_ge(full[3], banks.take(3))
                        nc.vector.tensor_copy(q.home[:, 4:8, t * P:(t + 1) * P],
                                              bank[3][:, :].rearrange("p (c t) -> p c t", c=4)).then_inc(free[3], 1)
                        if t == 3:
                            was_read(dve, banks, 2, 3)
                            dve.wait_ge(gmix_in, 16)
                        if t >= 4:
                            x_norm.step(2)
                    was_read(dve, banks, 2, 3)
                    x_norm.step(KC)
                dve.wait_ge(v["normed"], KC * nb)
                for b in range(nb):
                    dve.sem_inc(free[5 + b], 1)

                if q.n == 0:
                    dve.wait_ge(v["x_sq"], NCH)
                    dve.wait_ge(consts_in, 16 * N_CONSTS)
                for b, (b0, bl) in enumerate(q.blocks):
                    dve.wait_ge(full[b % 2], banks.take(b % 2))
                    nc.vector.tensor_scalar(G[0:2 * NH, b0:b0 + bl], bank[b % 2][0:2 * NH, 0:bl], bias8[:, 0:1], None,
                                            ALU.add).then_inc(free[b % 2], 1)
                lf = lf_fills(banks, q)
                own.link(nc.vector.tensor_copy(pair_rows[:, :, :].rearrange("p j (hh d) -> p (j hh) d", hh=2),
                                               ident[0:NH, 0:NH].unsqueeze(2).to_broadcast([NH, NH, DK])))
                own.link(nc.vector.memset(W[0:NH, 0:T], 1.0))
                own.link(nc.vector.memset(W[0:NH, 0:TP:P], 0.0))
                if q.sample:
                    own.link(nc.vector.memset(W[0:NH, TP:TM:NT_S], 0.0))
                dve.wait_ge(v["lf_soft"], 1)
                for b, (b0, bl) in enumerate(q.blocks):
                    nc.vector.scalar_tensor_tensor(LF[0:NH, b0:b0 + bl], bank[5 + b][0:NH, 0:bl], 0.0, EM[0:NH, b0:b0 + bl],
                                                   ALU.min, ALU.subtract).then_inc(free[5 + b], 1)
                for b in range(nb):
                    dve.wait_ge(free[5 + b], lf[b] + 1)
                dve.wait_ge(v["softcap"], 1)
                own.link(nc.vector.tensor_scalar(G[0:NH, 0:T], G[0:NH, 0:T], GATE_CAP, None, ALU.mult))
                own.link(nc.vector.tensor_tensor_scan(B[0:NH, 0:T], W[0:NH, 0:T], LF[0:NH, 0:T], 0.0, ALU.mult, ALU.add))
                own.link(nc.vector.tensor_tensor_scan(M[0:NH, 0:TP], LF[0:NH, 0:TP], G[0:NH, 0:TP], carry[:, 0:1],
                                                      ALU.add, ALU.max))
                own.link(nc.vector.tensor_copy(mprev[:, 0:1], carry[:, :]))
                own.link(nc.vector.tensor_copy(mprev[:, 1:NCH], M[0:NH, P - 1:TP - P:P]))
                own.link(nc.vector.tensor_copy(carry[:, :], M[0:NH, TP - 1:TP]))
                if q.sample:
                    by_batch = "p (b t) -> p b t"
                    own.link(nc.vector.tensor_copy(sI[:, :, :], G[0:NH, TP:TM].rearrange(by_batch, t=NT_S)))
                    own.link(nc.vector.tensor_copy(sF[:, :, :], LF[0:NH, TP:TM].rearrange(by_batch, t=NT_S)))
                    own.link(nc.vector.tensor_copy(mprev[:, NCH:], ms0[:, :]))
                    own.link(nc.vector.tensor_tensor(m_out[:, :], sF[:, :, 0], ms0[:, :], ALU.add))
                    own.link(nc.vector.tensor_tensor(sI[:, :, 0], sI[:, :, 0], m_out[:, :], ALU.max))
                    own.link(nc.vector.memset(sF[:, :, 0], NEG))
                    own.link(nc.vector.tensor_tensor_scan(M[0:NH, TP:TM], sF[:, :, :].rearrange("p b t -> p (b t)"),
                                                          sI[:, :, :].rearrange("p b t -> p (b t)"), 0.0, ALU.add, ALU.max))
                    own.link(nc.vector.tensor_copy(m_out[:, :], M[0:NH, TP + NT_S - 1:TM:NT_S]))
                own.link(nc.vector.tensor_tensor(R1[0:NH, 0:T], B[0:NH, 0:T], M[0:NH, 0:T], ALU.subtract))
                own.link(nc.vector.tensor_tensor(CS[0:NH, 0:T], G[0:NH, 0:T], B[0:NH, 0:T], ALU.subtract))
                spans = [(0, TP, P, 0)] + ([(TP, TM, NT_S, NCH)] if q.sample else [])
                for a, z, n, m0 in spans:
                    k = (z - a) // n
                    by = dict(n=n)
                    r1 = R1[0:NH, a:z].rearrange("p (c n) -> p c n", **by)
                    own.link(nc.vector.tensor_tensor(W[0:NH, a:z].rearrange("p (c n) -> p c n", **by), r1,
                                                     mprev[:, m0:m0 + k].unsqueeze(2).to_broadcast([NH, k, n]), ALU.add))
                    end = R1[0:NH, a + n - 1:z:n].unsqueeze(2).to_broadcast([NH, k, n])
                    own.link(nc.vector.tensor_tensor(LF[0:NH, a:z].rearrange("p (c n) -> p c n", **by),
                                                     CS[0:NH, a:z].rearrange("p (c n) -> p c n", **by), end, ALU.add))
                dve.sem_inc(v["rows_made"], 1)
                own.link(nc.vector.tensor_copy(R1_high[0:NH, 0:T], R1[0:NH, 0:T]))
                own.link(nc.vector.tensor_tensor(R1_parts[0:NH, 0:T], R1[0:NH, 0:T], R1_high[0:NH, 0:T], ALU.subtract))
                own.link(nc.vector.tensor_copy(R1_parts[HI:HI + NH, 0:T], R1_high[0:NH, 0:T]))
                columns, pairs, over_chunk = prep_fills(banks, q)
                dve.wait_ge(full[5], columns)
                stripe = bank[5][:, 0:3 * (NCH + 1) * NH].rearrange("p (r c h) -> p r c h", r=3, h=NH)
                if q.sample:
                    own.link(nc.vector.tensor_copy(cols[0:TS, :, NCH, :], stripe[0:TS, :, NCH, :]))
                nc.vector.tensor_copy(cols[:, :, 0:NCH, :], stripe[:, :, 0:NCH, :]).then_inc(free[5], 1)
                k = 0
                for j in range(PAIRS):
                    for b0, bl in q.blocks:
                        bk, no = pairs[k]
                        dve.wait_ge(full[bk], no)
                        nc.vector.scalar_tensor_tensor(qw[:, j, b0:b0 + bl], X[:, j, b0:b0 + bl], QSCALE,
                                                       bank[bk][:, 0:bl], ALU.mult, ALU.mult).then_inc(free[bk], 1)
                        k += 1
                dve.wait_ge(full[4], over_chunk)
                width = NCH + NB_S if q.sample else NCH
                nc.vector.tensor_copy(decay[:, :, 0:width],
                                      bank[4][:, 0:PAIRS * (NCH + NB_S)].rearrange("p (j c) -> p j c", j=PAIRS)[:, :, 0:width])\
                    .then_inc(free[4], 1)

                banks.skip(qkv_uses(q), 4)
                if q.n == 0:
                    banks.skip(TILE_USES)

                n0 = list(banks.n)
                loop_uses = {0: 2 * nb, 1: 2 * nb}

                def state_update(c, p):
                    dve.wait_ge(full[6], ChunkFills(n0, c).state)
                    for j in range(PAIRS):
                        last = nc.vector.scalar_tensor_tensor(state[:, j, :], state[:, j, :], colst[p][:, 12 + j:13 + j],
                                                              bank[6][:, j * (DV + 1):(j + 1) * (DV + 1)], ALU.mult, ALU.add)
                    last.then_inc(free[6], 1)

                def mixer_turn(i, sample=False):
                    f = Fills(banks, i, loop_uses)
                    k = nb % 2
                    turns = []
                    for n in range(4 * nb):
                        turns.append((k % 2, f.take(k % 2)))
                        k += 1
                    chunk_weights(v, n0, 2 * i, 0)
                    state_update(2 * i, 0)
                    chunk_heads(v, n0, 2 * i, 0)
                    chunk_weights(v, n0, 2 * i + 1, 1)
                    for b, (b0, bl) in enumerate(q.blocks):
                        dve.wait_ge(free[turns[nb + b][0]], turns[nb + b][1] + 1)
                        bk, no = turns[2 * nb + b]
                        dve.wait_ge(full[bk], no)
                        z = zbuf[:, 2 + b0:2 + b0 + bl]
                        nc.vector.tensor_tensor(z, z, bank[bk][:, 0:bl], ALU.mult).then_inc(free[bk], 1)
                    for b in range(2):
                        bk, no = turns[2 * nb + nb - 1 - b]
                        dve.wait_ge(free[bk], no + 1)
                    own.link(copy_at(zbuf[:, 0:2], hist[:, i, :]))
                    own.link(copy_at(hist[:, i, :], zbuf[:, TP:TP + 2]))
                    if q.sample:
                        own.link(copy_at(zs[:, :, 0:2], convs[:, i, :, :]))
                        own.link(nc.vector.tensor_copy(zs[:, :, 2:], zbuf[:, 2 + TP:2 + TM].rearrange("p (b t) -> p b t", t=NT_S)))
                    own.link(nc.vector.tensor_scalar(cv[:, 0:T], zbuf[:, 2:2 + T], cw[:, 2, ds(i, 1)], None, ALU.mult))
                    own.link(nc.vector.scalar_tensor_tensor(cv[:, 0:T], zbuf[:, 1:1 + T], cw[:, 1, ds(i, 1)], cv[:, 0:T],
                                                            ALU.mult, ALU.add))
                    nc.vector.scalar_tensor_tensor(cv[:, 0:T], zbuf[:, 0:T], cw[:, 0, ds(i, 1)], cv[:, 0:T],
                                                   ALU.mult, ALU.add).then_inc(v["conv_done"], 1)
                    dve.wait_ge(v["conv_done"], i + 2)

                    def gated(b):
                        b0, bl = q.blocks[b]
                        bk, no = turns[3 * nb + b]
                        dve.wait_ge(full[bk], no)
                        nc.vector.tensor_tensor(U[:, i + 4, b0:b0 + bl], cv[:, b0:b0 + bl], bank[bk][:, 0:bl], ALU.mult)\
                            .then_inc(free[bk], 1)

                    gated(0)
                    state_update(2 * i + 1, 1)
                    chunk_heads(v, n0, 2 * i + 1, 1)
                    if q.sample:
                        own.link(copy_at(convs[:, i, :, :], zs[:, :, NT_S:]))
                        cvs = cv[:, TP:TM].rearrange("p (b t) -> p b t", t=NT_S)
                        own.link(nc.vector.tensor_scalar(cvs, zs[:, :, 2:], cw[:, 2, ds(i, 1)], None, ALU.mult))
                        for w in (1, 0):
                            own.link(nc.vector.scalar_tensor_tensor(cvs, zs[:, :, w:w + NT_S], cw[:, w, ds(i, 1)], cvs,
                                                                    ALU.mult, ALU.add))
                    for b in range(1, nb):
                        gated(b)
                        if sample and b == 1:
                            sample_weights()

                def sample_weights():
                    f = ChunkFills(n0, NCH)
                    dve.wait_ge(free[5], f.out23)
                    own.link(nc.vector.memset(Pm[:, :, 0:TS], 0.0))
                    chunk_weights(v, n0, NCH, 0, TS)
                    dve.wait_ge(free[4], f.keys + 1)
                    dve.wait_ge(v["staged"], NCH + 1)
                    for h in range(NH):
                        nc.vector.tensor_tensor(kwb[:, h, :, :], kw[0:TS, h, :].unsqueeze(1).to_broadcast([TS, NB_S, DK]),
                                                batch_s[0:TS, :].unsqueeze(2).to_broadcast([TS, NB_S, DK]), ALU.mult)\
                            .then_inc(batch_keys, 1)

                loop_turns = 4 - q.sample
                with dve.Fori(0, loop_turns) as i:
                    own.loop(i, 2 * 5 + 4 + (2 + 1 + 2 + 1 if q.sample else 0))
                    mixer_turn(i)
                own.done(loop_turns)
                if q.sample:
                    mixer_turn(3, True)
                banks.skip(loop_uses, 4)
                banks.skip(CHUNK_USES, NCH)

                def states_of_sample(j):
                    own.link(nc.vector.tensor_tensor(
                        Cs[:, j, :, :], Cs[:, j, :, :],
                        decay[:, j, NCH:].unsqueeze(2).to_broadcast([P, NB_S, DV + 1]), ALU.mult))
                    for bk, b0 in ((2, 0), (3, 3), (6, 6)):
                        n = min(3, NB_S - b0)
                        dve.wait_ge(full[bk], banks.take(bk))
                        nc.vector.tensor_tensor(Cs[:, j, b0:b0 + n, :], Cs[:, j, b0:b0 + n, :],
                                                bank[bk][:, 0:n * (DV + 1)].rearrange("p (b e) -> p b e", b=n), ALU.add)\
                            .then_inc(free[bk], 1)

                def mix_low(b):
                    b0, bl = q.blocks[b]
                    for m in range(KC):
                        dve.wait_ge(v["mix_hi"], KC * b + m + 1)
                        nc.vector.tensor_tensor(AL[:, m, b0:b0 + bl], U[:, m, b0:b0 + bl], AH[:, m, b0:b0 + bl],
                                                ALU.subtract).then_inc(v["mix_lo"], 1)

                for b in range(nb):
                    mix_low(b)
                    if q.sample and b == 0:
                        chunk_heads(v, n0, NCH, 0, TS)
                        banks.skip(SAMPLE_USES)
                    if q.sample and b == 1:
                        states_of_sample(0)

                def embedding_low():
                    if q.sample:
                        states_of_sample(1)
                    for g in range(NCH // 2):
                        banks.take(2 + g)
                        dve.wait_ge(v["p_hi"], g + 1)
                        toks = slice(2 * g * P, (2 * g + 2) * P)
                        for c in range(2):
                            src = bank[2 + g][:, :].rearrange("p (t c n) -> p c t n", t=2, c=2)[:, c]
                            last = nc.vector.tensor_tensor(hid[:, 1, c, toks].rearrange("p (t n) -> p t n", t=2), src,
                                                           hid[:, 0, c, toks].rearrange("p (t n) -> p t n", t=2), ALU.subtract)
                            if c == 0:
                                own.link(last)
                        last.then_inc(free[2 + g], 1)
                    if q.sample:
                        banks.take(6)
                        dve.wait_ge(v["p_hi"], NCH // 2 + 1)
                        nc.vector.tensor_tensor(hid[:, 1, 0:2, TP:TM], bank[6][:, 0:2 * TS].rearrange("p (c n) -> p c n", c=2),
                                                hid[:, 0, 0:2, TP:TM], ALU.subtract).then_inc(free[6], 1)

                for first, last in ((0, 2), (2, 4)):
                    dve.wait_ge(v[f"reload{first // 2}"], 16)
                    with dve.Fori(first, last) as i:
                        f = Fills(banks, i, uses)
                        k = 0
                        for p in range(2):
                            for b0, bl in q.blocks:
                                dve.wait_ge(full[k % 2], f.take(k % 2))
                                x = X[:, 2 * i + p, b0:b0 + bl]
                                nc.vector.tensor_tensor(x, x, bank[k % 2][:, 0:bl], ALU.add).then_inc(free[k % 2], 1)
                                k += 1
                    if last == 2:
                        embedding_low()
                banks.skip(uses, 4)

                def mean_squares(bk, no, name):
                    dve.wait_ge(full[bk], no)
                    for a, z, n in ((0, NCH, P),) + (((NCH, NCH + 1, TS),) if q.sample else ()):
                        nc.vector.tensor_scalar(means[0:n, a:z], bank[bk][0:n, a:z], 1.0 / D, EPS, ALU.mult, ALU.add)\
                            .then_inc(v[name], 1)
                    dve.wait_ge(v[name], q.tiles - NCH + 1)
                    dve.sem_inc(free[bk], 1)

                columns, spread = norm_fills(banks, q)
                mean_squares(4, columns, "res_mean")

                def root(b):
                    dve.wait_ge(full[5 + b], spread[b][1])
                    return bank[5 + b][:, 0:q.blocks[b][1]]

                Normalised(q, X, gffn, root, "normed2", "high2", "low2").step(KC * nb)
                dve.wait_ge(v["normed2"], KC * nb)
                for b in range(nb):
                    dve.sem_inc(free[5 + b], 1)
                banks.skip(uses, 4)

                def up_chunk(f, hc, count):
                    for b, (b0, bl) in enumerate(q.blocks):
                        dve.wait_ge(free[b], f.take(b) + 1)
                        dve.wait_ge(full[3 + b], f.take(3 + b))
                        nc.vector.tensor_tensor(sl[:, b0:b0 + bl], sl[:, b0:b0 + bl], bank[3 + b][:, 0:bl], ALU.mult)\
                            .then_inc(free[3 + b], 1)
                    for b, (b0, bl) in enumerate(q.blocks):
                        dve.wait_ge(v["h_hi"], count + b + 1)
                        nc.vector.tensor_tensor(hid[:, 1, hc, b0:b0 + bl], sl[:, b0:b0 + bl], hid[:, 0, hc, b0:b0 + bl],
                                                ALU.subtract).then_inc(v["h_lo"], 1)

                def down(f, low_too):
                    for k in range(KC * nb):
                        c, (b0, bl) = k // nb, q.blocks[k % nb]
                        no = f.take(6 + k % 2)
                        dve.wait_ge(full[6 + k % 2], no)
                        x = X[:, c, b0:b0 + bl]
                        nc.vector.tensor_tensor(x, x, bank[6 + k % 2][:, 0:bl], ALU.add).then_inc(free[6 + k % 2], 1)
                        if low_too and k:
                            final_low(k - 1)
                    if low_too:
                        final_low(KC * nb - 1)

                def final_low(k):
                    c, (b0, bl) = k // nb, q.blocks[k % nb]
                    dve.wait_ge(v["x3_hi"], k + 1)
                    nc.vector.tensor_tensor(AL[:, c, b0:b0 + bl], X[:, c, b0:b0 + bl], AH[:, c, b0:b0 + bl],
                                            ALU.subtract).then_inc(v["x3_lo"], 1)

                ffn_uses = {b: 4 for b in range(nb)}
                ffn_uses.update({3 + b: 4 for b in range(nb)})
                ffn_uses.update({6: 4 * nb, 7: 4 * nb})
                with dve.Fori(0, 4) as g:
                    f = Fills(banks, g, ffn_uses)
                    for c in range(GROUP):
                        up_chunk(f, c, nb * (c + GROUP * g))
                    down(f, False)
                banks.skip(ffn_uses, 4)
                count = 16 * nb
                for size in (4, 2):
                    for c in range(size):
                        up_chunk(banks, c, count)
                        count += nb
                        if size == 4 and c == 0:
                            columns, spread = embedding_fills(banks, q)
                            mean_squares(7, columns, "e_mean")
                        if size == 4 and c in E_BLOCKS:
                            for b in E_BLOCKS[c][:nb - E_BLOCKS[c][0]]:
                                b0, bl = q.blocks[b]
                                bk, no = spread[b]
                                dve.wait_ge(full[bk], no)
                                for e in range(KC):
                                    x = U[:, e, b0:b0 + bl]
                                    nc.vector.scalar_tensor_tensor(x, x, gple[:, e:e + 1], bank[bk][:, 0:bl],
                                                                   ALU.mult, ALU.mult).then_inc(v["e_done"], 1)
                                dve.wait_ge(v["e_done"], KC * (b + 1))
                                dve.sem_inc(free[bk], 1)
                    down(banks, size == 2)

                dve.wait_ge(v["e_done"], KC * nb)
                def gate_block(no, i, k, b):
                    b0, bl = q.blocks[b]
                    dve.wait_ge(free[k % 2], no + 1)
                    g_, x = sl[:, b0:b0 + bl], X[:, 2 * i + k // nb, b0:b0 + bl]
                    own.link(nc.vector.tensor_tensor(g_, g_, U[:, 2 * i + k // nb, b0:b0 + bl], ALU.mult))
                    nc.vector.tensor_tensor(x, x, g_, ALU.add).then_inc(v["x4"], 1)

                def scale_next(b):
                    b0, bl = supers[1].blocks[b]
                    dve.wait_ge(full[5 + b], next_roots[b])
                    for c in range(KC):
                        x = next_x[:, c, b0:b0 + bl]
                        nc.vector.scalar_tensor_tensor(x, x, gmix[:, c:c + 1], bank[5 + b][:, 0:bl], ALU.mult, ALU.mult)\
                            .then_inc(S[1]["normed"], 1)

                def next_low_parts(b):
                    b0, bl = supers[1].blocks[b]
                    for c in range(KC):
                        dve.wait_ge(S[1]["high"], KC * b + c + 1)
                        nc.vector.tensor_tensor(AL[:, c, b0:b0 + bl], next_x[:, c, b0:b0 + bl], AH[:, c, b0:b0 + bl],
                                                ALU.subtract).then_inc(S[1]["low"], 1)

                if q.n == 0:
                    next_roots = [banks.take(5 + b) for b in range(supers[1].nb)]
                with dve.Fori(0, 3) as i:
                    f = Fills(banks, i, uses)
                    own.loop(i, 2 * nb)
                    for k in range(2 * nb):
                        gate_block(f.take(k % 2), i, k, k % nb)
                own.done(3)
                banks.skip(uses, 3)
                work = {0: (scale_next, (0, 1)), 1: (scale_next, (2,)), 2: (next_low_parts, (0,)), 3: (next_low_parts, (1, 2))}
                for k in range(2 * nb):
                    gate_block(banks.take(k % 2), 3, k, k % nb)
                    if q.n == 0:
                        if k == 0:
                            dve.wait_ge(S[1]["x_back"], 16)
                        for b in work[k][1]:
                            work[k][0](b)

            dve.wait_ge(v["gain_in"], 16)
            for t in range(q.tiles):
                n = P if t < NCH else TS
                if t >= 3:
                    dve.wait_ge(v[f"y_out{t % 3}"], 16 * (t // 3))
                dve.wait_ge(v["y_root"], t + 1)
                for m in range(2):
                    bk = 2 + 2 * (t % 3) + m
                    dve.wait_ge(full[bk], banks.take(bk))
                    nc.vector.scalar_tensor_tensor(y_end[t % 3][0:n, m * 512:(m + 1) * 512], bank[bk][0:n, :],
                                                   y_roots[0:n, t % 3, 0:1], gain_row[0:n, m * 512:(m + 1) * 512],
                                                   ALU.mult, ALU.mult).then_inc(free[bk], 1)

        @block.gpsimd
        def _(pool):
            banks = Banks()
            pool.sem_inc(lo_done, 2)
            for v in S:
                for name in ("res_sum", "e_sum"):
                    pool.sem_inc(v[name], 1)
            pool.sem_inc(S[1]["x_kept"], 1)
            made = Chain(pool, pool_own)
            for t, value in ((ident, 0.0), (identb, 0.0), (causal, 0.0), (causal_s, 0.0), (ones, 1.0),
                             (batch_s, 1.0), (state, 0.0), (epst, EPS), (neg_half, -0.5), (hist, 0.0), (carry, 0.0)):
                nc.gpsimd.memset(t[tuple([slice(None)] * len(t.shape))], value)
            made.link(nc.gpsimd.memset(sm[:, :, :], 0.0))

            def select(t, pattern, base, cm, op, fill):
                made.link(nc.gpsimd.affine_select(out=t, in_=t, compare_op=op, fill=fill, base=base, pattern=pattern,
                                                  channel_multiplier=cm))

            for t in (ident, identb):
                select(t[:, :], [[-1, P]], 0, 1, ALU.not_equal, 1.0)
            made.link(nc.gpsimd.tensor_tensor(pick[:, :], ident[:, 0:NH], ident[:, HI:HI + NH], ALU.add))
            select(causal[:, :], [[1, P]], 0, -1, ALU.is_ge, NEG)
            select(causal_s[:, :, :], [[NT_S, NB_S], [1, NT_S]], 0, -1, ALU.is_ge, NEG)
            select(causal_s[:, :, :], [[-NT_S, NB_S], [0, NT_S]], 0, 1, ALU.is_ge, NEG)
            select(batch_s[:, :], [[-NT_S, NB_S]], 0, 1, ALU.is_ge, 0.0)
            select(batch_s[:, :], [[NT_S, NB_S]], NT_S - 1, -1, ALU.is_ge, 0.0)
            pool.sem_inc(consts_made, 1)

            def next_low(s, i=0, step=0):
                p = s % 2
                pool.wait_ge(hi_done, s + 3 + step * i)
                nc.gpsimd.tensor_tensor(wlo[p][:, :], wraw[p][:, :], whi[p][:, :], ALU.subtract).then_inc(lo_done, 1)

            def clear_sums(v, q, name):
                nc.gpsimd.memset(ss[:, 0:q.T], 0.0).then_inc(v[name], 1)

            def add_square(v, q, name, squares, k, b, turn=0):
                b0, bl = q.blocks[b]
                pool.wait_ge(v[squares], k + 1 + turn)
                pool.wait_ge(v[name], k + 2 + turn)
                nc.gpsimd.tensor_tensor(ss[:, b0:b0 + bl], ss[:, b0:b0 + bl], tmp[k % 2][:, 0:bl], ALU.add)\
                    .then_inc(v[name], 1)

            def inverse_root(out, mean, n, width=1):
                made.link(nc.gpsimd.tensor_tensor(out, mean, epst[0:n, 0:1].to_broadcast([n, width]), ALU.add))
                return nc.gpsimd.tensor_tensor(out, out, neg_half[0:n, 0:width], ALU.pow)

            def roots_of_x(sem_, a, z, n=P):
                made.link(nc.gpsimd.tensor_scalar(x_sums[0:n, a:z], x_sums[0:n, a:z], 1.0 / D, None, ALU.mult))
                inverse_root(x_roots[0:n, a:z], x_sums[0:n, a:z], n, z - a).then_inc(sem_, 1)

            next_low(0)
            for q in supers:
                X, U, v, s0, nb = q.X, q.U, S[q.n], q.slab0, q.nb
                uses = {0: nb, 1: nb}
                if q.n == 0:
                    banks.skip(TILE_USES, NCH)
                    for b in range(nb):
                        banks.take(5 + b)
                        pool.wait_ge(v["x_sq"], 4 * (b + 1))
                        roots_of_x(v["x_root"], 4 * b, 4 * b + 4)
                next_low(s0 + 1)
                for b in range(nb):
                    banks.take(b % 2)
                lf_fills(banks, q)

                def qkv_part(part):
                    with turns(pool, *part) as i:
                        f = Fills(banks, i, qkv_uses(q))
                        made.loop(i - part[0], 2 if q.n == 0 else 2 * 2)
                        for p in range(2):
                            t, tile = 2 * i + p, [f.take(2), f.take(3)]
                            if q.n == 0:
                                pool.wait_ge(S[1]["x_sq"], t + 1)
                                made.link(nc.gpsimd.tensor_copy(x_sums[:, ds(t, 1)], sq_tile[:, 0:1]))
                                pool.sem_inc(S[1]["x_kept"], 1)
                            else:
                                w = S[0]
                                pool.wait_ge(w["y_sq"], 2 * t + 2)
                                made.link(nc.gpsimd.tensor_tensor(y_roots[:, 0, 0:1], y_sums[:, 0, 0:1], y_sums[:, 0, 1:2],
                                                                  ALU.add))
                                inverse_root(y_roots[:, 0, 0:1], y_roots[:, 0, 0:1], P).then_inc(w["y_root"], 1)
                            if q.n:
                                pool.wait_ge(free[2], tile[0] + 1)
                                pool.wait_ge(free[3], tile[1] + 1)
                                nc.gpsimd.tensor_tensor(y_rows[:, :], y_rows[:, :], gain_row[:, :], ALU.mult)\
                                    .then_inc(w["y_gained"], 1)
                            next_low(s0 + p + 2, i, 2)
                    made.done(part[1] - part[0])

                if q.n:
                    pool.wait_ge(S[0]["gain_in"], 16)
                qkv_part(PARTS[0])
                qkv_part(PARTS[1])
                columns, pairs, over_chunk = prep_fills(banks, q)
                pool.wait_ge(full[4], over_chunk)
                for t in (qz[:, :, :], qwz[:, :, :]):
                    nc.gpsimd.memset(t, 0.0).then_inc(v["stage_clear"], 1)
                nc.gpsimd.tensor_tensor(rz[:, :], ident[:, :], ident[:, :], ALU.subtract).then_inc(v["stage_clear"], 1)
                pool.wait_ge(v["stage_clear"], 3)
                was_read(pool, banks, 4, 5, 6, 7)
                n0 = list(banks.n)
                for b, k in qkv_uses(q).items():
                    n0[b] += 4 * k
                if q.n == 0:
                    for b in TILE_USES:
                        n0[b] += 1

                def stage_scores(c, tok, n=P):
                    pool.wait_ge(full[7], n0[7] + 2 * c - 1)
                    stage_keys(tok, n)
                    made.link(nc.gpsimd.tensor_copy(vst[:, :, 0:n], X[:, 4:8, tok]))

                def stage_keys(tok, n=P):
                    made.link(nc.gpsimd.tensor_copy(kst[:, :, 0:n], X[:, 2:4, tok]))
                    for half in range(2):
                        r = slice(half * DK, (half + 1) * DK)
                        made.link(nc.gpsimd.tensor_copy(qz[r, half:NH:2, 0:n], X[r, 0:2, tok]))
                    for part in (0, HI):
                        made.link(nc.gpsimd.tensor_copy(rz[part:part + NH, 0:n], R1_parts[part:part + NH, tok]))

                def stage_outputs(c, p, tok, n=P):
                    pool.wait_ge(full[6], ChunkFills(n0, c).state - 1)
                    for half in range(2):
                        r = slice(half * DK, (half + 1) * DK)
                        made.link(nc.gpsimd.tensor_copy(qwz[r, half:NH:2, 0:n], qw[r, :, tok]))
                    made.link(nc.gpsimd.tensor_copy(colst[p][0:n, 0:12].rearrange("p (r h) -> p r h", r=3), cols[0:n, :, c, :]))
                    nc.gpsimd.tensor_copy(colst[p][:, 12:14], decay[:, :, c if n == P else 0]).then_inc(v["staged"], 1)

                def root(c, n=P):
                    pool.wait_ge(v["root_in"], c + 1)
                    nc.gpsimd.tensor_tensor(rr[0:n, :], tt[0:n, :], neg_half[0:n, 0:NH], ALU.pow).then_inc(v["root_done"], 1)

                def merge(b):
                    b0, bl = q.blocks[b]
                    for h in range(NH):
                        nc.gpsimd.tensor_tensor(U[:, h, b0:b0 + bl], U[:, h, b0:b0 + bl], X[:, 4 + h, b0:b0 + bl], ALU.mult)\
                            .then_inc(v["merged"], 1)

                def chunk(i, m, following=None):
                    c = 2 * i + m
                    next_low(s0 + 10 + 2 * m, i, 4)
                    if following:
                        following()
                    else:
                        stage_scores(c + 1, ds((c + 1) * P, P))
                        stage_outputs(c + 1, 1 - m, ds((c + 1) * P, P))
                    next_low(s0 + 11 + 2 * m, i, 4)
                    root(c)

                def earlier_merges():
                    pool.wait_ge(free[7], ChunkFills(n0, 5).h_t + 1)
                    for b in range(nb - 1):
                        merge(b)

                def stage_sample():
                    made.link(nc.gpsimd.memset(batch_t[:, :, :], 1.0))
                    select(batch_t[:, :, :], [[-NT_S, NB_S], [1, TS]], 0, 0, ALU.is_ge, 0.0)
                    select(batch_t[:, :, :], [[NT_S, NB_S], [-1, TS]], NT_S - 1, 0, ALU.is_ge, 0.0)
                    stage_scores(NCH, slice(TP, TM), TS)
                    made.link(nc.gpsimd.memset(qb[:, :, :, :], 0.0))
                    stage_outputs(NCH, 0, slice(TP, TM), TS)
                    for half in range(2):
                        r = slice(half * DK, (half + 1) * DK)
                        made.link(nc.gpsimd.tensor_tensor(
                            qb[r, half:NH:2, :, :], qw[r, :, TP:TM].unsqueeze(2).to_broadcast([DK, PAIRS, NB_S, TS]),
                            batch_t[r, :, :].unsqueeze(1).to_broadcast([DK, PAIRS, NB_S, TS]), ALU.mult))
                        pool.sem_inc(batch_queries, 1)

                stage_keys(slice(0, P))
                qkv_part(PARTS[2])
                pool.wait_ge(free[nb % 2], banks.n[nb % 2] + 4 * nb + (0 if nb == 3 else 1))
                made.link(nc.gpsimd.tensor_copy(vst[:, :, :], X[:, 4:8, 0:P]))
                pool.wait_ge(full[3], n0[3] - (q.n == 0))
                made.link(nc.gpsimd.memset(V[:, :, DV:], 1.0))
                stage_outputs(0, 0, slice(0, P))
                banks.skip(qkv_uses(q), 4)
                if q.n == 0:
                    banks.skip(TILE_USES)
                with pool.Fori(0, 3) as i:
                    made.loop(i, 2 * 9)
                    chunk(i, 0)
                    chunk(i, 1)
                made.done(3)
                chunk(3, 0)
                chunk(3, 1, following=stage_sample if q.sample else earlier_merges)
                banks.skip({0: 2 * nb, 1: 2 * nb}, 4)
                banks.skip(CHUNK_USES, NCH)
                if q.sample:
                    earlier_merges()
                    root(NCH, TS)
                    banks.skip(SAMPLE_USES)
                was_read(pool, banks, 7)
                merge(nb - 1)
                if q.sample:
                    banks.skip({2: 2, 3: 2, 6: 2})

                was_filled(pool, banks, 4, 5, 7)
                clear_sums(v, q, "res_sum")

                def inverse_means(mean, root_):
                    pool.wait_ge(v[mean], q.tiles - NCH + 1)
                    for a, z, n in ((0, NCH, P),) + (((NCH, NCH + 1, TS),) if q.sample else ()):
                        nc.gpsimd.tensor_tensor(mean_roots[0:n, a:z], means[0:n, a:z], neg_half[0:n, a:z], ALU.pow)\
                            .then_inc(v[root_], 1)

                s = s0 + 25
                with pool.Fori(0, 4) as i:
                    for p in range(2):
                        next_low(s + p + 1, i, 2)
                        for b in range(nb):
                            add_square(v, q, "res_sum", "res_sq", p * nb + b, b, 2 * nb * i)
                s += 8
                inverse_means("res_mean", "res_root")
                for p in range(2):
                    next_low(s + 1)
                    s += 1
                pool.wait_ge(v["low2"], KC * nb)
                clear_sums(v, q, "e_sum")
                with pool.Fori(0, 4) as g:
                    for n in range(12):
                        next_low(s + n + 1, g, 12)
                        if n >= 10:
                            for b in range(nb):
                                add_square(v, q, "e_sum", "e_sq", (n - 10) * nb + b, b, 2 * nb * g)
                s += 48
                for n in range(18):
                    next_low(s + 1)
                    s += 1
                    if n == 2:
                        inverse_means("e_mean", "e_root")
                if q.n == 0:
                    pool.wait_ge(S[1]["x_sq"], NCH + 1)
                    made.link(nc.gpsimd.tensor_copy(x_sums[0:TS, NCH:NCH + 1], sq_tile[0:TS, 0:1]))
                    roots_of_x(S[1]["x_root"], 0, NCH)
                    roots_of_x(S[1]["x_root"], NCH, NCH + 1, TS)
                with pool.Fori(0, 3) as i:
                    for p in range(2):
                        next_low(s + p + 1, i, 2)
                next_low(s + 7)
                if q.n == 0:
                    next_low(s + 8)
                for g in range(4):
                    banks.take(2 + g)
                if q.sample:
                    banks.take(6)
                banks.skip({0: 12 * nb, 1: 12 * nb})
                norm_fills(banks, q)
                embedding_fills(banks, q)
                for b in range(nb):
                    banks.skip({b: FF, 3 + b: FF})
                banks.skip({6: 24 * nb, 7: 24 * nb})
                if q.n == 0:
                    banks.skip({5 + b: 1 for b in range(supers[1].nb)})

            for t in range(q.tiles):
                n = P if t < NCH else TS
                pool.wait_ge(v["y_sq"], 2 * t + 2)
                if t >= 3:
                    for m in range(2):
                        pool.wait_ge(free[2 + 2 * (t % 3) + m], banks.n[2 + 2 * (t % 3) + m] + 1)
                for m in range(2):
                    banks.take(2 + 2 * (t % 3) + m)
                r = y_roots[0:n, t % 3, 0:1]
                made.link(nc.gpsimd.tensor_tensor(r, y_sums[0:n, t % 3, 0:1], y_sums[0:n, t % 3, 1:2], ALU.add))
                inverse_root(r, r, n).then_inc(v["y_root"], 1)


INS = ["x_prompt", "x_sample", "p_prompt", "p_sample", "state_C", "state_n", "state_m", "state_conv", "g_mix", "w_in",
       "b_ig", "b_fg", "g_mh", "conv_w", "w_out", "g_ffn", "w_gate", "w_up", "w_down", "w_ple", "g_ple", "w_pg", "g_final"]
OUTS = [("y_prompt", (1, 2 * TP, D)), ("y_sample", (NB_S, NT_S, D)), ("C_prompt", (1, 1, NH, DK, DV)),
        ("n_prompt", (1, 1, NH, DK)), ("m_prompt", (1, 1, NH)), ("conv_prompt", (1, 1, 2, 512)),
        ("C_sample", (1, NB_S, NH, DK, DV)), ("n_sample", (1, NB_S, NH, DK)), ("m_sample", (1, NB_S, NH)),
        ("conv_sample", (1, NB_S, 2, 512))]


def kernel(**inputs):
    import numpy as np
    import concourse.bacc as bacc
    from concourse.bass_utils import run_bass_kernel_spmd

    nc = bacc.Bacc("TRN2", target_bir_lowering=False, num_devices=1)
    arrays, args = {}, []
    for name in INS:
        a = np.ascontiguousarray(inputs[name])
        arrays[name] = a
        args.append(nc.dram_tensor(name, a.shape, F32, kind="ExternalInput").ap())
    for name, shape in OUTS:
        args.append(nc.dram_tensor(name, shape, F32, kind="ExternalOutput").ap())
    build(nc, *args)
    got = run_bass_kernel_spmd(nc, [arrays], core_ids=[0]).results[0]
    return tuple(got[name] for name, _ in OUTS)
```
